# Optimizing a Trainium2 kernel written in Bass

```python
import math
import jax, jax.numpy as jnp
from jax import lax
import numpy as np
import jax
import jax.numpy as jnp

D_MODEL = 1024
BATCH = 1
SEQ = 256
DEPTH = 2

GRID_W = 64
CTX_LEN = 256
HEAD_DIM = 128
FNET_GROUPS = 4
FNET_GROUP_DIM = 64
FNET_WIDTH = FNET_GROUPS * FNET_GROUP_DIM
GQA_Q_HEADS = 6
GQA_KV_HEADS = 2
GQA_GROUP = GQA_Q_HEADS // GQA_KV_HEADS
AB_IN_WIDTH = FNET_WIDTH + (GQA_Q_HEADS + 2 * GQA_KV_HEADS) * HEAD_DIM
AB_OUT_WIDTH = FNET_WIDTH + GQA_Q_HEADS * HEAD_DIM
ROPE_THETA = 10000.0
Q_BLOCK = 128
NA_HEADS = 8
NA_WIDTH = NA_HEADS * HEAD_DIM
NA_KH = 8
NA_KW = 16
NA_ROWS_PER_BLOCK = Q_BLOCK // GRID_W
NEG_INF = -1e30
N_EXPERTS = 64
TOP_K = 8
EXPERT_DIM = 256
SHARED_DIM = 256
ROUTE_SCALE = 2.5
MOE_BLOCK = 128
DN_ALPHA = (2 * DEPTH) ** 0.25
DN_BETA = (8 * DEPTH) ** -0.25
N_EVEN = (DEPTH + 1) // 2
N_ODD = DEPTH // 2
LN_EPS = 1e-6
RMS_EPS = 1e-6


def layer_norm(x, g, b):
    xf = x.astype(jnp.float32)
    mu = xf.mean(-1, keepdims=True)
    xc = xf - mu
    var = (xc * xc).mean(-1, keepdims=True)
    return (xc * lax.rsqrt(var + LN_EPS) * g + b).astype(x.dtype)

def rms_norm(x, g):
    xf = x.astype(jnp.float32)
    return (xf * lax.rsqrt((xf * xf).mean(-1, keepdims=True) + RMS_EPS) * g).astype(x.dtype)

def axial_rope(x):
    n_tok = x.shape[1]
    t = jnp.arange(n_tok)
    half = HEAD_DIM // 2
    nf = half // 2
    inv = ROPE_THETA ** (-(2.0 / half) * jnp.arange(nf, dtype=jnp.float32))

    def rot(v, pos):
        ang = pos.astype(jnp.float32)[:, None] * inv
        cos = jnp.cos(ang)[:, None, :]
        sin = jnp.sin(ang)[:, None, :]
        v1, v2 = v[..., :nf], v[..., nf:]
        return jnp.concatenate([v1 * cos - v2 * sin, v1 * sin + v2 * cos], axis=-1)

    xf = x.astype(jnp.float32)
    out = jnp.concatenate([rot(xf[..., :half], t // GRID_W), rot(xf[..., half:], t % GRID_W)], axis=-1)
    return out.astype(x.dtype)

def gqa_attend(q, k, v):
    s = jnp.einsum("bqkgd,bnkd->bkgqn", q, k).astype(jnp.float32) * HEAD_DIM ** -0.5
    p = jax.nn.softmax(s, axis=-1).astype(v.dtype)
    return jnp.einsum("bkgqn,bnkd->bqkgd", p, v)

def fourier_mix(f, w_fnet):
    bsz, n_tok, _ = f.shape
    fg = f.reshape(bsz, n_tok, FNET_GROUPS, FNET_GROUP_DIM).astype(jnp.float32)
    fr = jnp.fft.fft2(fg, axes=(1, 3), norm="ortho").real.astype(f.dtype)
    return jnp.einsum("blgc,gcd->blgd", fr, w_fnet).reshape(bsz, n_tok, FNET_WIDTH)

def mixer_ab(h_lat, h_ctx, w_in, w_fnet, q_gain, k_gain, w_out, want_ctx):
    bsz, n_lat, _ = h_lat.shape
    n_ctx = h_ctx.shape[1]
    nq = GQA_Q_HEADS * HEAD_DIM
    nkv = GQA_KV_HEADS * HEAD_DIM
    cuts = [FNET_WIDTH, FNET_WIDTH + nq, FNET_WIDTH + nq + nkv]
    f, q, k, v = jnp.split(h_lat @ w_in, cuts, axis=-1)
    q = axial_rope(rms_norm(q.reshape(bsz, n_lat, GQA_Q_HEADS, HEAD_DIM), q_gain))
    k = axial_rope(rms_norm(k.reshape(bsz, n_lat, GQA_KV_HEADS, HEAD_DIM), k_gain))
    v = v.reshape(bsz, n_lat, GQA_KV_HEADS, HEAD_DIM)
    if want_ctx:
        fc, qc, kc, vc = jnp.split(h_ctx @ w_in, cuts, axis=-1)
    else:
        kc, vc = jnp.split(h_ctx @ w_in[:, cuts[1]:], [nkv], axis=-1)
    kc = rms_norm(kc.reshape(bsz, n_ctx, GQA_KV_HEADS, HEAD_DIM), k_gain)
    vc = vc.reshape(bsz, n_ctx, GQA_KV_HEADS, HEAD_DIM)
    k_all = jnp.concatenate([k, kc], axis=1)
    v_all = jnp.concatenate([v, vc], axis=1)
    nb = n_lat // Q_BLOCK
    qb = q.reshape(bsz, nb, Q_BLOCK, GQA_KV_HEADS, GQA_GROUP, HEAD_DIM).swapaxes(0, 1)
    o = lax.map(lambda qi: gqa_attend(qi, k_all, v_all), qb)
    o = o.swapaxes(0, 1).reshape(bsz, n_lat, nq)
    y_lat = jnp.concatenate([fourier_mix(f, w_fnet), o], axis=-1) @ w_out
    if not want_ctx:
        return y_lat, None
    qc = rms_norm(qc.reshape(bsz, n_ctx, GQA_Q_HEADS, HEAD_DIM), q_gain)
    qc = qc.reshape(bsz, n_ctx, GQA_KV_HEADS, GQA_GROUP, HEAD_DIM)
    oc = gqa_attend(qc, kc, vc).reshape(bsz, n_ctx, nq)
    y_ctx = jnp.concatenate([fourier_mix(fc, w_fnet), oc], axis=-1) @ w_out
    return y_lat, y_ctx

def mixer_na(h_lat, h_ctx, w_in, rpb, w_out, want_ctx):
    bsz, n_lat, _ = h_lat.shape
    n_ctx = h_ctx.shape[1]
    rows = n_lat // GRID_W
    kh = min(NA_KH, rows)
    kw = min(NA_KW, GRID_W)
    qr = NA_ROWS_PER_BLOCK
    nbr = min(qr + kh - 1, rows)
    nblk = rows // qr
    scale = HEAD_DIM ** -0.5
    q, k, v = jnp.split(h_lat @ w_in, 3, axis=-1)
    if want_ctx:
        qc, kc, vc = jnp.split(h_ctx @ w_in, 3, axis=-1)
    else:
        kc, vc = jnp.split(h_ctx @ w_in[:, NA_WIDTH:], 2, axis=-1)
    kc = kc.reshape(bsz, n_ctx, NA_HEADS, HEAD_DIM)
    vc = vc.reshape(bsz, n_ctx, NA_HEADS, HEAD_DIM)
    k_grid = k.reshape(bsz, rows, GRID_W, NA_HEADS, HEAD_DIM)
    v_grid = v.reshape(bsz, rows, GRID_W, NA_HEADS, HEAD_DIM)
    q_blocks = q.reshape(bsz, nblk, qr * GRID_W, NA_HEADS, HEAD_DIM).swapaxes(0, 1)
    col = jnp.arange(GRID_W)
    col_start = jnp.clip(col - kw // 2, 0, GRID_W - kw)
    in_col = (col[None, :] >= col_start[:, None]) & (col[None, :] < col_start[:, None] + kw)
    dc = jnp.clip(col[None, :] - col[:, None] + NA_KW - 1, 0, 2 * NA_KW - 2)

    def block(args):
        i, qi = args
        qrow = i * qr + jnp.arange(qr)
        rstart = jnp.clip(qrow - kh // 2, 0, rows - kh)
        bs = jnp.minimum(rstart[0], rows - nbr)
        krow = bs + jnp.arange(nbr)
        kb = lax.dynamic_slice_in_dim(k_grid, bs, nbr, axis=1).reshape(bsz, nbr * GRID_W, NA_HEADS, HEAD_DIM)
        vb = lax.dynamic_slice_in_dim(v_grid, bs, nbr, axis=1).reshape(bsz, nbr * GRID_W, NA_HEADS, HEAD_DIM)
        in_row = (krow[None, :] >= rstart[:, None]) & (krow[None, :] < rstart[:, None] + kh)
        dr = jnp.clip(krow[None, :] - qrow[:, None] + NA_KH - 1, 0, 2 * NA_KH - 2)
        mask = (in_row[:, None, :, None] & in_col[None, :, None, :]).reshape(qr * GRID_W, nbr * GRID_W)
        bias = rpb[:, dr[:, None, :, None], dc[None, :, None, :]].reshape(NA_HEADS, qr * GRID_W, nbr * GRID_W)
        s_loc = jnp.einsum("bqhd,bnhd->bhqn", qi, kb).astype(jnp.float32) * scale + bias.astype(jnp.float32)
        s_loc = jnp.where(mask, s_loc, NEG_INF)
        s_ctx = jnp.einsum("bqhd,bnhd->bhqn", qi, kc).astype(jnp.float32) * scale
        p = jax.nn.softmax(jnp.concatenate([s_loc, s_ctx], axis=-1), axis=-1).astype(vb.dtype)
        n_loc = nbr * GRID_W
        return (jnp.einsum("bhqn,bnhd->bqhd", p[..., :n_loc], vb)
                + jnp.einsum("bhqn,bnhd->bqhd", p[..., n_loc:], vc))

    o = lax.map(block, (jnp.arange(nblk), q_blocks))
    y_lat = o.swapaxes(0, 1).reshape(bsz, n_lat, NA_WIDTH) @ w_out
    if not want_ctx:
        return y_lat, None
    qc = qc.reshape(bsz, n_ctx, NA_HEADS, 1, HEAD_DIM)
    oc = gqa_attend(qc, kc, vc).reshape(bsz, n_ctx, NA_WIDTH)
    return y_lat, oc @ w_out

def moe_ffn(h, w_router, e_bias, w_gate, w_up, w_down, s_gate, s_up, s_down):
    n_tok, d = h.shape
    scores = jax.nn.sigmoid((h @ w_router).astype(jnp.float32))
    _, idx = lax.top_k(scores + e_bias.astype(jnp.float32), TOP_K)
    wts = jnp.take_along_axis(scores, idx, axis=-1)
    wts = wts / wts.sum(-1, keepdims=True) * ROUTE_SCALE
    n_pairs = n_tok * TOP_K
    flat_e = idx.reshape(-1)
    order = jnp.argsort(flat_e)
    sorted_e = flat_e[order]
    sorted_tok = (order // TOP_K).astype(jnp.int32)
    sorted_w = wts.reshape(-1)[order]
    counts = jnp.bincount(flat_e, length=N_EXPERTS)
    padded = (counts + MOE_BLOCK - 1) // MOE_BLOCK * MOE_BLOCK
    pad_end = jnp.cumsum(padded)
    pad_start = pad_end - padded
    grp_start = jnp.cumsum(counts) - counts
    dest = pad_start[sorted_e] + jnp.arange(n_pairs) - grp_start[sorted_e]
    n_blocks = (n_pairs + N_EXPERTS * (MOE_BLOCK - 1)) // MOE_BLOCK + 1
    n_slots = n_blocks * MOE_BLOCK
    slot_tok = jnp.full((n_slots,), n_tok, jnp.int32).at[dest].set(sorted_tok)
    slot_w = jnp.zeros((n_slots,), jnp.float32).at[dest].set(sorted_w)
    block_e = jnp.minimum(jnp.searchsorted(pad_end, jnp.arange(n_blocks) * MOE_BLOCK, side="right"),
                          N_EXPERTS - 1)
    h_pad = jnp.concatenate([h, jnp.zeros((1, d), h.dtype)], axis=0)

    def expert_block(args):
        tok, e = args
        xb = h_pad[tok]
        a = jax.nn.silu(xb @ w_gate[e]) * (xb @ w_up[e])
        return a @ w_down[e]

    yb = lax.map(expert_block, (slot_tok.reshape(n_blocks, MOE_BLOCK), block_e))
    y = yb.reshape(n_slots, d) * slot_w[:, None].astype(h.dtype)
    routed = jnp.zeros((n_tok + 1, d), h.dtype).at[slot_tok].add(y)[:n_tok]
    shared = (jax.nn.silu(h @ s_gate) * (h @ s_up)) @ s_down
    return routed + shared

def first_inputs(seed: int = 0) -> dict:
    key = jax.random.key(seed)
    ks = iter(jax.random.split(key, 32))
    D = D_MODEL

    def nrm(shape, scale):
        return jax.random.normal(next(ks), shape, jnp.float32) * scale

    return {
        "x": nrm((BATCH, SEQ, D), 1.0),
        "c": nrm((BATCH, D), 1.0),
        "ctx": nrm((BATCH, CTX_LEN, D), 1.0),
        "c_ctx": nrm((D,), 1.0),
        "w_mod": nrm((DEPTH, D, 6 * D), 0.5 * D ** -0.5),
        "b_mod": nrm((DEPTH, 6 * D), 0.02),
        "ln1_g": 1.0 + nrm((DEPTH, D), 0.05),
        "ln1_b": nrm((DEPTH, D), 0.02),
        "ln2_g": 1.0 + nrm((DEPTH, D), 0.05),
        "ln2_b": nrm((DEPTH, D), 0.02),
        "ab_w_in": nrm((N_EVEN, D, AB_IN_WIDTH), D ** -0.5),
        "ab_w_fnet": nrm((N_EVEN, FNET_GROUPS, FNET_GROUP_DIM, FNET_GROUP_DIM), FNET_GROUP_DIM ** -0.5),
        "ab_q_norm": 1.0 + nrm((N_EVEN, HEAD_DIM), 0.05),
        "ab_k_norm": 1.0 + nrm((N_EVEN, HEAD_DIM), 0.05),
        "ab_w_out": nrm((N_EVEN, AB_OUT_WIDTH, D), AB_OUT_WIDTH ** -0.5 * DN_BETA),
        "na_w_in": nrm((N_ODD, D, 3 * NA_WIDTH), D ** -0.5),
        "na_rpb": nrm((N_ODD, NA_HEADS, 2 * NA_KH - 1, 2 * NA_KW - 1), 0.5),
        "na_w_out": nrm((N_ODD, NA_WIDTH, D), NA_WIDTH ** -0.5 * DN_BETA),
        "moe_w_router": nrm((DEPTH, D, N_EXPERTS), D ** -0.5),
        "moe_bias": nrm((DEPTH, N_EXPERTS), 0.01),
        "moe_w_gate": nrm((DEPTH, N_EXPERTS, D, EXPERT_DIM), D ** -0.5),
        "moe_w_up": nrm((DEPTH, N_EXPERTS, D, EXPERT_DIM), D ** -0.5),
        "moe_w_down": nrm((DEPTH, N_EXPERTS, EXPERT_DIM, D), EXPERT_DIM ** -0.5 * DN_BETA),
        "sh_w_gate": nrm((DEPTH, D, SHARED_DIM), D ** -0.5),
        "sh_w_up": nrm((DEPTH, D, SHARED_DIM), D ** -0.5),
        "sh_w_down": nrm((DEPTH, SHARED_DIM, D), SHARED_DIM ** -0.5 * DN_BETA),
    }

def first_block(x, c, ctx, c_ctx, w_mod, b_mod, ln1_g, ln1_b, ln2_g, ln2_b,
              ab_w_in, ab_w_fnet, ab_q_norm, ab_k_norm, ab_w_out,
              na_w_in, na_rpb, na_w_out,
              moe_w_router, moe_bias, moe_w_gate, moe_w_up, moe_w_down,
              sh_w_gate, sh_w_up, sh_w_down):
    bsz, n_lat, d = x.shape
    n_ctx = ctx.shape[1]
    for l in range(DEPTH):
        want_ctx = l < DEPTH - 1
        j = l // 2
        mod = jax.nn.silu(c) @ w_mod[l] + b_mod[l]
        mod_c = jax.nn.silu(c_ctx) @ w_mod[l] + b_mod[l]
        sh1, sc1, g1, sh2, sc2, g2 = jnp.split(mod[:, None, :], 6, axis=-1)
        csh1, csc1, cg1, csh2, csc2, cg2 = jnp.split(mod_c, 6, axis=-1)
        h = x * (1.0 + sc1) + sh1
        hc = ctx * (1.0 + csc1) + csh1
        if l % 2 == 0:
            y, yc = mixer_ab(h, hc, ab_w_in[j], ab_w_fnet[j], ab_q_norm[j], ab_k_norm[j], ab_w_out[j], want_ctx)
        else:
            y, yc = mixer_na(h, hc, na_w_in[j], na_rpb[j], na_w_out[j], want_ctx)
        x = layer_norm(DN_ALPHA * x + g1 * y, ln1_g[l], ln1_b[l])
        h2 = (x * (1.0 + sc2) + sh2).reshape(bsz * n_lat, d)
        moe_args = (moe_w_router[l], moe_bias[l], moe_w_gate[l], moe_w_up[l], moe_w_down[l],
                    sh_w_gate[l], sh_w_up[l], sh_w_down[l])
        if want_ctx:
            ctx = layer_norm(DN_ALPHA * ctx + cg1 * yc, ln1_g[l], ln1_b[l])
            hc2 = (ctx * (1.0 + csc2) + csh2).reshape(bsz * n_ctx, d)
            ff = moe_ffn(jnp.concatenate([h2, hc2], axis=0), *moe_args)
            ff_lat = ff[:bsz * n_lat].reshape(bsz, n_lat, d)
            ff_ctx = ff[bsz * n_lat:].reshape(bsz, n_ctx, d)
            ctx = layer_norm(DN_ALPHA * ctx + cg2 * ff_ctx, ln2_g[l], ln2_b[l])
        else:
            ff_lat = moe_ffn(h2, *moe_args).reshape(bsz, n_lat, d)
        x = layer_norm(DN_ALPHA * x + g2 * ff_lat, ln2_g[l], ln2_b[l])
    return x


NORM_EPS = 1e-6
D_FF = 2816
CONV_CH = 1024
CONV_WIDTH = 31
SSM_D_INNER = 1024
SSM_HEAD_DIM = 64
SSM_HEADS = SSM_D_INNER // SSM_HEAD_DIM
SSM_GROUPS = 2
SSM_STATE = 128
SSM_CONV_WIDTH = 4
SSM_CHUNK = 128
SSM_XBC = SSM_D_INNER + 2 * SSM_GROUPS * SSM_STATE
HYB_IN_COLS = 2 * CONV_CH + SSM_D_INNER + SSM_XBC + SSM_HEADS
HYB_MIX_WIDTH = CONV_CH + SSM_D_INNER
ATTN_HEAD_DIM = 64
ATTN_HEADS = 8
DILATED_PATTERNS = ((128, 1), (512, 4), (2048, 16))
ATTN_GROUPS = len(DILATED_PATTERNS)
ATTN_BLOCK = 128
ATTN_QKV_COLS = 3 * ATTN_GROUPS * ATTN_HEADS * ATTN_HEAD_DIM
ATTN_OUT_WIDTH = ATTN_HEADS * ATTN_HEAD_DIM
N_EVEN_2 = (DEPTH + 1) // 2
N_ODD_2 = DEPTH // 2


def rms_norm_2(x, g):
    xf = x.astype(jnp.float32)
    y = xf * lax.rsqrt(jnp.mean(xf * xf, axis=-1, keepdims=True) + NORM_EPS)
    return (y * g.astype(jnp.float32)).astype(x.dtype)

def layer_norm_2(x, g, b):
    xf = x.astype(jnp.float32)
    xc = xf - jnp.mean(xf, axis=-1, keepdims=True)
    y = xc * lax.rsqrt(jnp.mean(xc * xc, axis=-1, keepdims=True) + NORM_EPS)
    return (y * g.astype(jnp.float32) + b.astype(jnp.float32)).astype(x.dtype)

def swiglu(u, w1, w2):
    gate, up = jnp.split(u @ w1, 2, axis=-1)
    return (jax.nn.silu(gate) * up) @ w2

def causal_depthwise_conv(x, w, b):
    k = w.shape[0]
    y = lax.conv_general_dilated(x, w[:, None, :].astype(x.dtype), window_strides=(1,), padding=[(k - 1, 0)], dimension_numbers=('NWC', 'WIO', 'NWC'), feature_group_count=x.shape[-1])
    return y + b.astype(x.dtype)

def conformer_conv(u, w_dw, b_dw, ln_g, ln_b):
    val, gate = jnp.split(u, 2, axis=-1)
    hid = causal_depthwise_conv(val * jax.nn.sigmoid(gate), w_dw, b_dw)
    return jax.nn.silu(layer_norm_2(hid, ln_g, ln_b))

def segsum(a):
    t = a.shape[-1]
    strict = jnp.tril(jnp.ones((t, t), dtype=bool), -1)
    incl = jnp.tril(jnp.ones((t, t), dtype=bool), 0)
    ss = jnp.cumsum(jnp.where(strict, a[..., :, None], 0.0), axis=-2)
    return jnp.where(incl, ss, -jnp.inf)

def ssd_chunked(x, a, bm, cm):
    bsz, seq, heads, hd = x.shape
    groups, nst = bm.shape[2], bm.shape[3]
    rep = heads // groups
    nc = seq // SSM_CHUNK
    x = x.reshape(bsz, nc, SSM_CHUNK, groups, rep, hd)
    a = a.reshape(bsz, nc, SSM_CHUNK, groups, rep).transpose(0, 3, 4, 1, 2)
    bm = bm.reshape(bsz, nc, SSM_CHUNK, groups, nst)
    cm = cm.reshape(bsz, nc, SSM_CHUNK, groups, nst)
    a_cum = jnp.cumsum(a, axis=-1)
    decay_in = jnp.exp(segsum(a))
    cb = jnp.einsum('bclgn,bcsgn->bgcls', cm, bm)
    y_diag = jnp.einsum('bgrcls,bcsgrp->bclgrp', cb[:, :, None] * decay_in, x)
    decay_states = jnp.exp(a_cum[..., -1:] - a_cum)
    states = jnp.einsum('bcsgn,bgrcs,bcsgrp->bcgrpn', bm, decay_states, x)
    states = jnp.concatenate([jnp.zeros_like(states[:, :1]), states], axis=1)
    chunk_tot = jnp.pad(a_cum[..., -1], ((0, 0), (0, 0), (0, 0), (1, 0)))
    decay_chunk = jnp.exp(segsum(chunk_tot))
    states = jnp.einsum('bgrzc,bcgrpn->bzgrpn', decay_chunk, states)[:, :-1]
    y_off = jnp.einsum('bclgn,bcgrpn,bgrcl->bclgrp', cm, states, jnp.exp(a_cum))
    return (y_diag + y_off).reshape(bsz, seq, heads, hd)

def mamba2_ssd(z, xbc, dt_raw, conv_w, conv_b, dt_bias, a_log, d_skip, norm_g):
    bsz, seq, _ = z.shape
    xbc = jax.nn.silu(causal_depthwise_conv(xbc, conv_w, conv_b)).astype(jnp.float32)
    xs, bm, cm = jnp.split(xbc, [SSM_D_INNER, SSM_D_INNER + SSM_GROUPS * SSM_STATE], axis=-1)
    xs = xs.reshape(bsz, seq, SSM_HEADS, SSM_HEAD_DIM)
    bm = bm.reshape(bsz, seq, SSM_GROUPS, SSM_STATE)
    cm = cm.reshape(bsz, seq, SSM_GROUPS, SSM_STATE)
    dt = jax.nn.softplus(dt_raw.astype(jnp.float32) + dt_bias.astype(jnp.float32))
    a = -jnp.exp(a_log.astype(jnp.float32))
    y = ssd_chunked(xs * dt[..., None], dt * a, bm, cm) + d_skip.astype(jnp.float32)[:, None] * xs
    y = y.reshape(bsz, seq, SSM_D_INNER) * jax.nn.silu(z.astype(jnp.float32))
    return rms_norm_2(y, norm_g).astype(z.dtype)

def conv_ssd_mixer(u, w_in, conv_dw_w, conv_dw_b, conv_ln_g, conv_ln_b, ssm_conv_w, ssm_conv_b, ssm_dt_bias, ssm_a_log, ssm_d, ssm_norm_g, w_out):
    proj = u @ w_in
    s0 = 2 * CONV_CH
    s1 = s0 + SSM_D_INNER
    s2 = s1 + SSM_XBC
    conv_in, z, xbc, dt_raw = jnp.split(proj, [s0, s1, s2], axis=-1)
    ya = conformer_conv(conv_in, conv_dw_w, conv_dw_b, conv_ln_g, conv_ln_b)
    yb = mamba2_ssd(z, xbc, dt_raw, ssm_conv_w, ssm_conv_b, ssm_dt_bias, ssm_a_log, ssm_d, ssm_norm_g)
    return jnp.concatenate([ya.astype(u.dtype), yb.astype(u.dtype)], axis=-1) @ w_out

def dilated_window_attention(q, k, v, slopes, window, dilation):
    bsz, seq, heads, dh = q.shape
    n = seq // dilation
    steps = window // dilation
    nb = -(-n // ATTN_BLOCK)
    pad = nb * ATTN_BLOCK - n

    def strided(t):
        t = t.reshape(bsz, n, dilation, heads, dh).transpose(0, 2, 1, 3, 4)
        t = t.reshape(bsz * dilation, n, heads, dh)
        t = jnp.pad(t, ((0, 0), (0, pad), (0, 0), (0, 0)))
        return t.reshape(bsz * dilation, nb, ATTN_BLOCK, heads, dh)

    def with_previous_block(t):
        prev = jnp.pad(t[:, :-1], ((0, 0), (1, 0), (0, 0), (0, 0), (0, 0)))
        return jnp.concatenate([prev, t], axis=2)

    qb = strided(q)
    kb = with_previous_block(strided(k))
    vb = with_previous_block(strided(v))
    scores = jnp.einsum('znqhd,znkhd->znhqk', qb.astype(jnp.float32), kb.astype(jnp.float32)) * (dh ** -0.5)
    qi = jnp.arange(ATTN_BLOCK)[:, None]
    kj = jnp.arange(2 * ATTN_BLOCK)[None, :] - ATTN_BLOCK
    rel = qi - kj
    blk0 = (jnp.arange(nb) * ATTN_BLOCK)[:, None, None]
    valid = (rel >= 0) & (rel <= steps) & (blk0 + kj >= 0)
    bias = -slopes[:, None, None] * (rel * dilation).astype(jnp.float32)
    scores = jnp.where(valid[None, :, None], scores + bias[None, None], -jnp.inf)
    lse = jax.nn.logsumexp(scores, axis=-1)
    probs = jnp.exp(scores - lse[..., None]).astype(v.dtype)
    out = jnp.einsum('znhqk,znkhd->znqhd', probs, vb)
    out = out.reshape(bsz, dilation, nb * ATTN_BLOCK, heads, dh)[:, :, :n]
    out = out.transpose(0, 2, 1, 3, 4).reshape(bsz, seq, heads, dh)
    lse = lse.transpose(0, 1, 3, 2).reshape(bsz, dilation, nb * ATTN_BLOCK, heads)[:, :, :n]
    lse = lse.transpose(0, 2, 1, 3).reshape(bsz, seq, heads)
    return out, lse

def dilated_attention_mixer(u, w_qkv, w_o):
    bsz, seq, _ = u.shape
    qkv = (u @ w_qkv).reshape(bsz, seq, 3, ATTN_GROUPS, ATTN_HEADS, ATTN_HEAD_DIM)
    slopes = jnp.exp2(-8.0 * jnp.arange(1, ATTN_HEADS + 1, dtype=jnp.float32) / ATTN_HEADS)
    outs = []
    lses = []
    for g, (window, dilation) in enumerate(DILATED_PATTERNS):
        o, l = dilated_window_attention(qkv[:, :, 0, g], qkv[:, :, 1, g], qkv[:, :, 2, g], slopes, window, dilation)
        outs.append(o)
        lses.append(l)
    weights = jax.nn.softmax(jnp.stack(lses, axis=0), axis=0)
    merged = jnp.einsum('gblh,gblhd->blhd', weights, jnp.stack(outs, axis=0).astype(jnp.float32))
    return merged.reshape(bsz, seq, ATTN_OUT_WIDTH).astype(u.dtype) @ w_o

def second_inputs(seed: int = 0) -> dict:
    key = jax.random.key(seed)
    ks = jax.random.split(key, 20)

    def normal(k, shape, scale):
        return jax.random.normal(k, shape, jnp.float32) * scale

    x = normal(ks[0], (BATCH, SEQ, D_MODEL), 1.0)
    norm_g = 1.0 + normal(ks[1], (DEPTH, 6, D_MODEL), 0.05)
    ffn_w1 = normal(ks[2], (DEPTH, 2, D_MODEL, 2 * D_FF), D_MODEL ** -0.5)
    ffn_w2 = normal(ks[3], (DEPTH, 2, D_FF, D_MODEL), D_FF ** -0.5)
    hyb_w_in = normal(ks[4], (N_EVEN_2, D_MODEL, HYB_IN_COLS), D_MODEL ** -0.5)
    conv_dw_w = normal(ks[5], (N_EVEN_2, CONV_WIDTH, CONV_CH), CONV_WIDTH ** -0.5)
    conv_dw_b = normal(ks[6], (N_EVEN_2, CONV_CH), 0.02)
    conv_ln_g = 1.0 + normal(ks[7], (N_EVEN_2, CONV_CH), 0.05)
    conv_ln_b = normal(ks[8], (N_EVEN_2, CONV_CH), 0.02)
    ssm_conv_w = normal(ks[9], (N_EVEN_2, SSM_CONV_WIDTH, SSM_XBC), SSM_CONV_WIDTH ** -0.5)
    ssm_conv_b = normal(ks[10], (N_EVEN_2, SSM_XBC), 0.02)
    dt0 = jnp.exp(jax.random.uniform(ks[11], (N_EVEN_2, SSM_HEADS), jnp.float32, math.log(1e-3), math.log(1e-1)))
    ssm_dt_bias = dt0 + jnp.log(-jnp.expm1(-dt0))
    ssm_a_log = jnp.log(jax.random.uniform(ks[12], (N_EVEN_2, SSM_HEADS), jnp.float32, 1.0, 16.0))
    ssm_d = 1.0 + normal(ks[13], (N_EVEN_2, SSM_HEADS), 0.1)
    ssm_norm_g = 1.0 + normal(ks[14], (N_EVEN_2, SSM_D_INNER), 0.05)
    hyb_w_out = normal(ks[15], (N_EVEN_2, HYB_MIX_WIDTH, D_MODEL), HYB_MIX_WIDTH ** -0.5)
    attn_w_qkv = normal(ks[16], (N_ODD_2, D_MODEL, ATTN_QKV_COLS), D_MODEL ** -0.5)
    attn_w_o = normal(ks[17], (N_ODD_2, ATTN_OUT_WIDTH, D_MODEL), ATTN_OUT_WIDTH ** -0.5)
    return {'x': x, 'norm_g': norm_g, 'ffn_w1': ffn_w1, 'ffn_w2': ffn_w2, 'hyb_w_in': hyb_w_in, 'conv_dw_w': conv_dw_w, 'conv_dw_b': conv_dw_b, 'conv_ln_g': conv_ln_g, 'conv_ln_b': conv_ln_b, 'ssm_conv_w': ssm_conv_w, 'ssm_conv_b': ssm_conv_b, 'ssm_dt_bias': ssm_dt_bias, 'ssm_a_log': ssm_a_log, 'ssm_d': ssm_d, 'ssm_norm_g': ssm_norm_g, 'hyb_w_out': hyb_w_out, 'attn_w_qkv': attn_w_qkv, 'attn_w_o': attn_w_o}

def second_block(x, norm_g, ffn_w1, ffn_w2, hyb_w_in, conv_dw_w, conv_dw_b, conv_ln_g, conv_ln_b, ssm_conv_w, ssm_conv_b, ssm_dt_bias, ssm_a_log, ssm_d, ssm_norm_g, hyb_w_out, attn_w_qkv, attn_w_o):
    h = x
    for i in range(DEPTH):
        g = norm_g[i]
        h = h + 0.5 * rms_norm_2(swiglu(rms_norm_2(h, g[0]), ffn_w1[i, 0], ffn_w2[i, 0]), g[1])
        u = rms_norm_2(h, g[2])
        j = i // 2
        if i % 2 == 0:
            m = conv_ssd_mixer(u, hyb_w_in[j], conv_dw_w[j], conv_dw_b[j], conv_ln_g[j], conv_ln_b[j], ssm_conv_w[j], ssm_conv_b[j], ssm_dt_bias[j], ssm_a_log[j], ssm_d[j], ssm_norm_g[j], hyb_w_out[j])
        else:
            m = dilated_attention_mixer(u, attn_w_qkv[j], attn_w_o[j])
        h = h + rms_norm_2(m, g[3])
        h = h + 0.5 * rms_norm_2(swiglu(rms_norm_2(h, g[4]), ffn_w1[i, 1], ffn_w2[i, 1]), g[5])
    return h


def setup_inputs(seed=0):
    out = dict(first_inputs(seed))
    for name, value in second_inputs(seed + 1).items():
        if name != "x":
            out[name + "_2"] = value
    return out


def reference(
    x, c, ctx, c_ctx, w_mod, b_mod, ln1_g, ln1_b, ln2_g, ln2_b, ab_w_in, ab_w_fnet, ab_q_norm,
    ab_k_norm, ab_w_out, na_w_in, na_rpb, na_w_out, moe_w_router, moe_bias, moe_w_gate,
    moe_w_up, moe_w_down, sh_w_gate, sh_w_up, sh_w_down, norm_g_2, ffn_w1_2, ffn_w2_2,
    hyb_w_in_2, conv_dw_w_2, conv_dw_b_2, conv_ln_g_2, conv_ln_b_2, ssm_conv_w_2, ssm_conv_b_2,
    ssm_dt_bias_2, ssm_a_log_2, ssm_d_2, ssm_norm_g_2, hyb_w_out_2, attn_w_qkv_2, attn_w_o_2,
):
    x = first_block(
        x, c, ctx, c_ctx, w_mod, b_mod, ln1_g, ln1_b, ln2_g, ln2_b, ab_w_in, ab_w_fnet,
        ab_q_norm, ab_k_norm, ab_w_out, na_w_in, na_rpb, na_w_out, moe_w_router, moe_bias,
        moe_w_gate, moe_w_up, moe_w_down, sh_w_gate, sh_w_up, sh_w_down,
    )
    return second_block(
        x, norm_g_2, ffn_w1_2, ffn_w2_2, hyb_w_in_2, conv_dw_w_2, conv_dw_b_2, conv_ln_g_2,
        conv_ln_b_2, ssm_conv_w_2, ssm_conv_b_2, ssm_dt_bias_2, ssm_a_log_2, ssm_d_2,
        ssm_norm_g_2, hyb_w_out_2, attn_w_qkv_2, attn_w_o_2,
    )


_drawn_inputs = setup_inputs


def setup_inputs(seed=0):
    import zlib

    import numpy as np

    out = dict(_drawn_inputs(seed))
    spreads = {}
    factors = {'ab_q_norm': 8.0,
     'ab_k_norm': 8.0,
     'na_rpb': 6.94,
     'conv_ln_b_2': 4.892,
     'ssm_conv_b_2': 3.012}
    for name, (base, spread) in spreads.items():
        noise = np.random.default_rng([zlib.crc32(name.encode()), seed]).standard_normal(out[name].shape)
        drawn = base * np.exp(spread * noise) if base else spread * noise
        out[name] = jnp.asarray(drawn.astype(out[name].dtype))
    for name, factor in factors.items():
        out[name] = (out[name] * factor).astype(out[name].dtype)
    return out
```

```python
import math
from contextlib import ExitStack

import numpy as np

import concourse.bass as bass
from concourse import mybir

F32 = mybir.dt.float32
ALU = mybir.AluOpType
ACT = mybir.ActivationFunctionType
X_AXIS = mybir.AxisListType.X

P = 128
BANK = 512
NBANKS = 8
D = 1024
KD = D // P
LAT = 256
CTX = 256
TOK = LAT + CTX
DEPTH = 2
HEAD = 128
NEG = -1e30
DN_ALPHA = (2 * DEPTH) ** 0.25
EPS = 1e-6
N_EXPERTS = 64
TOP_K = 8
ROUTE_SCALE = 2.5
GRID_W = 64
GRID_ROWS = LAT // GRID_W
NA_HEADS = 8
NA_KH = 8
NA_KW = 16
RPB_PAD = GRID_W - NA_KW
RPB_W = 2 * NA_KW - 1 + 2 * RPB_PAD
FFN_PARTS = 11
CONV_TAPS = 31
SSM_TAPS = 4
SSM_HEADS = 16
SSM_P = 64
DIL_GROUPS = 3
DIL_HEADS = 8
DIL_DH = 64



class Chain:

    def __init__(self, eng, sem):
        self.eng, self.sem, self.count = eng, sem, 0

    def then(self, ins):
        self.count += 1
        ins.then_inc(self.sem, 1)
        self.eng.wait_ge(self.sem, self.count)


class Stage:

    def __init__(self, nc, name):
        self.nc, self.name, self.stack, self.sems = nc, name, ExitStack(), []

    def __enter__(self):
        self.stack.__enter__()
        return self

    def __exit__(self, *a):
        self.stack.__exit__(*a)
        if self.sems:
            self.nc.clear_and_free_semaphores(self.sems)
            self.nc.all_engine_barrier()

    def sbuf(self, name, shape):
        return self.stack.enter_context(self.nc.sbuf_tensor(f"{self.name}_{name}", shape, F32))

    def sem(self, name):
        self.sems.append(self.nc.alloc_semaphore(f"{self.name}_{name}"))
        return self.sems[-1]

    def block(self):
        return self.stack.enter_context(self.nc.Block())


def copy_on(nc, engine, out, in_):
    if engine == "v":
        return nc.vector.tensor_copy(out, in_)
    return nc.scalar.activation(out, in_, ACT.Copy)


def affine_on(nc, engine, out, in_, scale, shift):
    if engine == "v":
        return nc.vector.tensor_scalar(out, in_, scale, shift, ALU.mult, ALU.add)
    return nc.scalar.activation(out, in_, ACT.Identity, scale=scale, bias=shift)


def rows_of(vector, n=P):
    return vector.partition_broadcast(n)



def product_stage(nc, name, psum, weights, k_tiles, n_chunks, n_tiles, operands, drain, shape):
    with Stage(nc, name) as st:
        depth = min(3, n_chunks)
        width = max(w.shape[-1] for w in weights)
        wbuf = st.sbuf("w", [P, depth, width])
        loaded = [st.sem(f"loaded{i}") for i in range(depth)]
        products, v_drained, s_drained = st.sem("products"), st.sem("v_drained"), st.sem("s_drained")
        tiles = [(c, t) for c in range(n_chunks) for t in range(n_tiles(c))]
        last_of = {c: g for g, (c, t) in enumerate(tiles)}
        block = st.block()

        @block.sync
        def _(sp):
            for c in range(n_chunks):
                if c >= depth:
                    sp.wait_ge(products, last_of[c - depth] + 1)
                sp.dma_start(wbuf[:, c % depth, 0:weights[c].shape[-1]], weights[c]).then_inc(loaded[c % depth], 16)

        @block.tensor
        def _(pe):
            for g, (c, t) in enumerate(tiles):
                if t == 0:
                    pe.wait_ge(loaded[c % depth], 16 * (c // depth + 1))
                if g >= NBANKS:
                    pe.wait_ge(s_drained if g % 2 else v_drained, (g - NBANKS) // 2 + 1)
                m, n = shape(c, t)
                w = wbuf[:, c % depth, 0:weights[c].shape[-1]].rearrange("p (k n) -> p k n", k=k_tiles)
                for k in range(k_tiles):
                    lhs, rhs = operands(c, t, k, w)
                    last = nc.tensor.matmul(psum[0:m, g % NBANKS, 0:n], lhs, rhs, start=k == 0, stop=k == k_tiles - 1)
                last.then_inc(products, 1)

        @block.vector
        def _(dve):
            for g, (c, t) in enumerate(tiles):
                if g % 2 == 0:
                    dve.wait_ge(products, g + 1)
                    m, n = shape(c, t)
                    drain("v", c, t, psum[0:m, g % NBANKS, 0:n]).then_inc(v_drained, 1)

        @block.scalar
        def _(act):
            for g, (c, t) in enumerate(tiles):
                if g % 2 == 1:
                    act.wait_ge(products, g + 1)
                    m, n = shape(c, t)
                    drain("s", c, t, psum[0:m, g % NBANKS, 0:n]).then_inc(s_drained, 1)


def rows_product(nc, name, psum, cols, weights, k_tiles, tok_tiles, drain, k0=0):
    weights = [weights[c] for c in range(weights.shape[0])]
    product_stage(
        nc, name, psum, weights, k_tiles, len(weights), lambda c: tok_tiles,
        lambda c, t, k, w: (cols[:, k0 + k, t * P:(t + 1) * P], w[:, k, :]),
        drain, lambda c, t: (P, weights[c].shape[-1] // k_tiles))


def cols_product(nc, name, psum, cols, weights, tokens, drain):
    weights = [weights[c] for c in range(weights.shape[0])]
    product_stage(
        nc, name, psum, weights, KD, len(weights), lambda c: BANK // P,
        lambda c, t, k, w: (w[:, k, t * P:(t + 1) * P], cols[:, k, 0:tokens(c)]),
        drain, lambda c, t: (P, tokens(c)))



def transpose_stage(nc, name, psum, ident, n_groups, pieces, source, drain):
    with Stage(nc, name) as st:
        transposed, v_drained, s_drained = st.sem("transposed"), st.sem("v_drained"), st.sem("s_drained")
        block = st.block()

        @block.tensor
        def _(pe):
            for j in range(n_groups):
                if j >= NBANKS:
                    pe.wait_ge(s_drained if j % 2 else v_drained, (j - NBANKS) // 2 + 1)
                for i in range(pieces):
                    src = source(j, i)
                    m, n = src.shape
                    last = nc.tensor.transpose(psum[0:n, j % NBANKS, i * m:(i + 1) * m], src, ident[0:m, 0:m])
                last.then_inc(transposed, 1)

        @block.vector
        def _(dve):
            for j in range(0, n_groups, 2):
                dve.wait_ge(transposed, j + 1)
                drain("v", j, psum[:, j % NBANKS, :]).then_inc(v_drained, 1)

        @block.scalar
        def _(act):
            for j in range(1, n_groups, 2):
                act.wait_ge(transposed, j + 1)
                drain("s", j, psum[:, j % NBANKS, :]).then_inc(s_drained, 1)



def modulation_stage(nc, psum, ident, cvec, w_mod, b_mod, mod_dram, mod_cols):
    n_chunks = 6 * D // BANK
    for layer in range(DEPTH):
        with Stage(nc, f"mod{layer}") as st:
            depth = 3
            craw, cs = st.sbuf("craw", [P, KD, 2]), st.sbuf("cs", [P, KD, 2])
            bias, rows = st.sbuf("bias", [2, 6 * D]), st.sbuf("rows", [2, 6 * D])
            wbuf = st.sbuf("w", [P, depth, KD * BANK])
            loaded = [st.sem(f"loaded{i}") for i in range(depth)]
            small, activated, products, drained = st.sem("small"), st.sem("activated"), st.sem("products"), st.sem("drained")
            turned, turned_out, stored, shifted = st.sem("turned"), st.sem("turned_out"), st.sem("stored"), st.sem("shifted")
            block = st.block()

            @block.sync
            def _(sp):
                sp.dma_start(craw[:], cvec).then_inc(small, 16)
                sp.dma_start(bias[:], rows_of(b_mod[layer], 2)).then_inc(small, 16)
                for c in range(depth):
                    sp.dma_start(wbuf[:, c, :], w_mod[layer * n_chunks + c]).then_inc(loaded[c], 16)
                with sp.Fori(1, n_chunks // depth) as i:
                    for j in range(depth):
                        sp.wait_ge(products, depth * i + (j + 1 - depth))
                        sp.dma_start(wbuf[:, j, :], w_mod[depth * i + (layer * n_chunks + j)]).then_inc(loaded[j], 16)
                sp.wait_ge(drained, n_chunks)
                sp.dma_start(mod_dram[layer], rows[:]).then_inc(stored, 16)
                sp.wait_ge(stored, 16)

            @block.scalar
            def _(act):
                act.wait_ge(small, 32)
                nc.scalar.activation(cs[:], craw[:], ACT.Silu).then_inc(activated, 1)

            @block.tensor
            def _(pe):
                pe.wait_ge(activated, 1)
                with pe.Fori(0, n_chunks // depth) as i:
                    for j in range(depth):
                        pe.wait_ge(loaded[j], 16 * i + 16)
                        w = wbuf[:, j, :].rearrange("p (k n) -> p k n", k=KD)
                        for k in range(KD):
                            last = nc.tensor.matmul(psum[0:2, j, :], cs[:, k, :], w[:, k, :], start=k == 0, stop=k == KD - 1)
                        last.then_inc(products, 1)
                    pe.wait_ge(drained, depth * i + depth)
                for m in range(6 * KD):
                    last = nc.tensor.transpose(psum[:, 4, 2 * m:2 * m + 2], rows[:, m * P:(m + 1) * P], ident[0:2, 0:2])
                last.then_inc(turned, 1)

            @block.vector
            def _(dve):
                dve.wait_ge(small, 32)
                with dve.Fori(0, n_chunks // depth) as i:
                    for j in range(depth):
                        dve.wait_ge(products, depth * i + (j + 1))
                        at = bass.ds(i * (depth * BANK) + j * BANK, BANK)
                        nc.vector.tensor_tensor(rows[:, at], psum[0:2, j, :], bias[:, at], ALU.add).then_inc(drained, 1)
                dve.wait_ge(turned, 1)
                cols = mod_cols[:, layer, :, :]
                nc.vector.tensor_copy(cols, psum[:, 4, 0:12 * KD].rearrange("p (m r) -> p m r", r=2)).then_inc(turned_out, 1)
                dve.wait_ge(turned_out, 1)
                for kind in (1, 4):
                    at = cols[:, kind * KD:(kind + 1) * KD, :]
                    nc.vector.tensor_scalar(at, at, 1.0, None, ALU.add).then_inc(shifted, 1)



def residual_norm_stage(nc, name, x, y, tok_tiles, gate_lat, gate_ctx, gain, shift):
    with Stage(nc, name) as st:
        vec = st.sbuf("vec", [P, 4, D])
        stats, agg = st.sbuf("stats", [P, tok_tiles, 2, 6]), st.sbuf("agg", [P, tok_tiles, 2])
        std, rstd = st.sbuf("std", [P, tok_tiles]), st.sbuf("rstd", [P, tok_tiles])
        loaded, gated, summed, varied = st.sem("loaded"), st.sem("gated"), st.sem("summed"), st.sem("varied")
        rooted, scaled, chain_sem, shifted = st.sem("rooted"), st.sem("scaled"), st.sem("chain"), st.sem("shifted")
        block = st.block()

        @block.sync
        def _(sp):
            for i, v in enumerate((gate_lat, gate_ctx, gain, shift)):
                sp.dma_start(vec[:, i, :], rows_of(v)).then_inc(loaded, 16)

        @block.gpsimd
        def _(pool):
            pool.wait_ge(loaded, 64)
            for t in range(tok_tiles):
                nc.gpsimd.tensor_tensor(y[:, t, :], y[:, t, :], vec[:, 0 if t < 2 else 1, :], ALU.mult).then_inc(gated, 1)
            for t in range(tok_tiles):
                pool.wait_ge(scaled, t + 1)
                nc.gpsimd.tensor_tensor(x[:, t, :], x[:, t, :], vec[:, 3, :], ALU.add).then_inc(shifted, 1)

        @block.scalar
        def _(act):
            for t in range(tok_tiles):
                act.wait_ge(varied, t + 1)
                nc.scalar.activation(std[:, t:t + 1], agg[:, t, 1:2], ACT.Sqrt).then_inc(rooted, 1)

        @block.vector
        def _(dve):
            chain = Chain(dve, chain_sem)
            for t in range(tok_tiles):
                dve.wait_ge(gated, t + 1)
                chain.then(nc.vector.scalar_tensor_tensor(x[:, t, :], x[:, t, :], DN_ALPHA, y[:, t, :], ALU.mult, ALU.add))
                nc.vector.bn_stats(stats[:, t, 0, :], x[:, t, 0:BANK])
                chain.then(nc.vector.bn_stats(stats[:, t, 1, :], x[:, t, BANK:D]))
                chain.then(nc.vector.bn_aggr(agg[:, t, :], stats[:, t, :, :]))
                nc.vector.tensor_scalar(agg[:, t, 1:2], agg[:, t, 1:2], EPS, None, ALU.add).then_inc(varied, 1)
            dve.wait_ge(loaded, 64)
            for t in range(tok_tiles):
                dve.wait_ge(rooted, t + 1)
                chain.then(nc.vector.reciprocal(rstd[:, t:t + 1], std[:, t:t + 1]))
                chain.then(nc.vector.tensor_scalar(x[:, t, :], x[:, t, :], agg[:, t, 0:1], rstd[:, t:t + 1], ALU.subtract, ALU.mult))
                nc.vector.tensor_tensor(x[:, t, :], x[:, t, :], vec[:, 2, :], ALU.mult).then_inc(scaled, 1)



def modulated_cols(nc, name, psum, ident, x, cols, mod_cols, layer, scale_kind, tok_tiles):
    shift_kind = scale_kind - 1

    def drain(engine, j, bank):
        for row in range(tok_tiles // 2):
            at = slice(row * LAT, (row + 1) * LAT)
            last = affine_on(nc, engine, cols[:, j, at], bank[:, at],
                             mod_cols[:, layer, scale_kind * KD + j, row:row + 1],
                             mod_cols[:, layer, shift_kind * KD + j, row:row + 1])
        return last

    transpose_stage(nc, name, psum, ident, KD, tok_tiles, lambda j, i: x[:, i, j * P:(j + 1) * P], drain)



def attention_stage(nc, name, psum, ident, units, score_parts, n_keys, bias, scale, values, out, dh):
    n = len(units)
    widest = max(n_keys(u) for u in units)
    with Stage(nc, name) as st:
        biased = st.sbuf("biased", [P, 2, widest])
        probs = st.sbuf("probs", [P, 2, widest])
        probs_t = st.sbuf("probs_t", [P, 2, widest])
        peak, neg_peak = st.sbuf("peak", [P, n]), st.sbuf("neg_peak", [P, n])
        total, inv_total = st.sbuf("total", [P, n]), st.sbuf("inv_total", [P, n])
        scores_ready, peak_ready, probs_ready = st.sem("scores_ready"), st.sem("peak_ready"), st.sem("probs_ready")
        turned, turned_out, outs_ready, outs_used = st.sem("turned"), st.sem("turned_out"), st.sem("outs_ready"), st.sem("outs_used")
        chain_sem = st.sem("chain")
        block = st.block()

        def scores(u):
            return psum[:, 2 * (u % 2):2 * (u % 2) + 2, :].rearrange("p b n -> p (b n)")

        turned_ps = psum[:, 4:6, :].rearrange("p b n -> p (b n)")
        has_bias = bool(bias(units[0]))
        exp_scale = 1.0 if has_bias and bias(units[0])[0][2] is None else scale

        def exp_source(u):
            return biased[:, u % 2, 0:n_keys(units[u])] if has_bias else scores(u)[:, 0:n_keys(units[u])]

        @block.tensor
        def _(pe):
            for step in range(n + 2):
                if step < n:
                    u = step
                    if u >= 2:
                        pe.wait_ge(probs_ready, u - 1)
                    for col, lhs, rhs in score_parts(units[u]):
                        last = nc.tensor.matmul(scores(u)[:, col:col + rhs.shape[-1]], lhs, rhs, start=True, stop=True)
                    last.then_inc(scores_ready, 1)
                if 0 <= step - 1 < n:
                    u = step - 1
                    pe.wait_ge(probs_ready, u + 1)
                    if u >= 1:
                        pe.wait_ge(turned_out, u)
                    for c in range(n_keys(units[u]) // P):
                        last = nc.tensor.transpose(turned_ps[:, c * P:(c + 1) * P], probs[:, u % 2, c * P:(c + 1) * P], ident[:])
                    last.then_inc(turned, 1)
                if 0 <= step - 2 < n:
                    u = step - 2
                    pe.wait_ge(turned_out, u + 1)
                    if u >= 2:
                        pe.wait_ge(outs_used, u - 1)
                    vs = values(units[u])
                    for c, v in enumerate(vs):
                        last = nc.tensor.matmul(psum[:, 6 + u % 2, 0:dh], probs_t[:, u % 2, c * P:(c + 1) * P], v,
                                                start=c == 0, stop=c == len(vs) - 1)
                    last.then_inc(outs_ready, 1)

        @block.vector
        def _(dve):
            chain = Chain(dve, chain_sem)
            for step in range(n + 2):
                if step < n:
                    u = step
                    dve.wait_ge(scores_ready, u + 1)
                    if has_bias:
                        if u >= 2:
                            dve.wait_ge(probs_ready, u - 1)
                        for at, table, factor in bias(units[u]):
                            if table is None:
                                ins = nc.vector.tensor_scalar(biased[:, u % 2, at], scores(u)[:, at], scale, None, ALU.mult)
                            elif factor is None:
                                ins = nc.vector.scalar_tensor_tensor(biased[:, u % 2, at], scores(u)[:, at], scale, table, ALU.mult, ALU.add)
                            else:
                                ins = nc.vector.scalar_tensor_tensor(biased[:, u % 2, at], table, factor, scores(u)[:, at], ALU.mult, ALU.add)
                        chain.then(ins)
                    chain.then(nc.vector.reduce_max(peak[:, u:u + 1], exp_source(u), X_AXIS))
                    nc.vector.tensor_scalar(neg_peak[:, u:u + 1], peak[:, u:u + 1], -exp_scale, None, ALU.mult).then_inc(peak_ready, 1)
                if 0 <= step - 2 < n:
                    u = step - 2
                    dve.wait_ge(outs_ready, u + 1)
                    chain.then(nc.vector.reciprocal(inv_total[:, u:u + 1], total[:, u:u + 1]))
                    nc.vector.tensor_scalar(out(units[u]), psum[:, 6 + u % 2, 0:dh], inv_total[:, u:u + 1], None, ALU.mult).then_inc(outs_used, 1)

        @block.scalar
        def _(act):
            for step in range(n + 1):
                if step < n:
                    u = step
                    act.wait_ge(peak_ready, u + 1)
                    if u >= 2:
                        act.wait_ge(turned, u - 1)
                    nc.scalar.activation(probs[:, u % 2, 0:n_keys(units[u])], exp_source(u), ACT.Exp,
                                         bias=neg_peak[:, u:u + 1], scale=exp_scale,
                                         accum_out=total[:, u:u + 1]).then_inc(probs_ready, 1)
                if step >= 1:
                    u = step - 1
                    act.wait_ge(turned, u + 1)
                    if u >= 2:
                        act.wait_ge(outs_ready, u - 1)
                    nc.scalar.activation(probs_t[:, u % 2, 0:n_keys(units[u])], turned_ps[:, 0:n_keys(units[u])],
                                         ACT.Copy).then_inc(turned_out, 1)



def resident_product_stage(nc, name, psum, tiles, drain):
    with Stage(nc, name) as st:
        products, v_drained, s_drained = st.sem("products"), st.sem("v_drained"), st.sem("s_drained")
        block = st.block()

        @block.tensor
        def _(pe):
            for g, (m, n, terms) in enumerate(tiles):
                if g >= NBANKS:
                    pe.wait_ge(s_drained if g % 2 else v_drained, (g - NBANKS) // 2 + 1)
                for k, (lhs, rhs) in enumerate(terms):
                    last = nc.tensor.matmul(psum[0:m, g % NBANKS, 0:n], lhs, rhs, start=k == 0, stop=k == len(terms) - 1)
                last.then_inc(products, 1)

        @block.vector
        def _(dve):
            for g in range(0, len(tiles), 2):
                dve.wait_ge(products, g + 1)
                drain("v", g, psum[0:tiles[g][0], g % NBANKS, 0:tiles[g][1]]).then_inc(v_drained, 1)

        @block.scalar
        def _(act):
            for g in range(1, len(tiles), 2):
                act.wait_ge(products, g + 1)
                drain("s", g, psum[0:tiles[g][0], g % NBANKS, 0:tiles[g][1]]).then_inc(s_drained, 1)



def norm_rope_stage(nc, proj, gains, rope):
    heads = 8
    with Stage(nc, "norm_rope") as st:
        gain, table = st.sbuf("gain", [P, heads, HEAD]), st.sbuf("table", [P, 2, 2, HEAD])
        square, turned = st.sbuf("square", [P, heads, HEAD]), st.sbuf("turned", [P, heads, HEAD])
        ss, std, rstd = st.sbuf("ss", [P, 4, heads]), st.sbuf("std", [P, 4, heads]), st.sbuf("rstd", [P, 4, heads])
        loaded, squared, summed, rooted, chain_sem = st.sem("loaded"), st.sem("squared"), st.sem("summed"), st.sem("rooted"), st.sem("chain")
        block = st.block()

        def qk(t):
            return proj[:, t, LAT:LAT + heads * HEAD].rearrange("p (h d) -> p h d", d=HEAD)

        @block.sync
        def _(sp):
            sp.dma_start(gain[:], rows_of(gains).rearrange("p (h d) -> p h d", d=HEAD)).then_inc(loaded, 16)
            sp.dma_start(table[:], rope).then_inc(loaded, 16)

        @block.gpsimd
        def _(pool):
            for t in range(4):
                if t >= 1:
                    pool.wait_ge(summed, t)
                nc.gpsimd.tensor_tensor(square[:], qk(t), qk(t), ALU.mult).then_inc(squared, 1)

        @block.scalar
        def _(act):
            for t in range(4):
                act.wait_ge(summed, t + 1)
                nc.scalar.activation(std[:, t, :], ss[:, t, :], ACT.Sqrt).then_inc(rooted, 1)

        @block.vector
        def _(dve):
            chain = Chain(dve, chain_sem)
            for t in range(4):
                dve.wait_ge(squared, t + 1)
                chain.then(nc.vector.reduce_sum(ss[:, t, :], square[:], X_AXIS))
                nc.vector.tensor_scalar(ss[:, t, :], ss[:, t, :], 1.0 / HEAD, EPS, ALU.mult, ALU.add).then_inc(summed, 1)
            dve.wait_ge(loaded, 32)
            for t in range(4):
                dve.wait_ge(rooted, t + 1)
                chain.then(nc.vector.reciprocal(rstd[:, t, :], std[:, t, :]))
                chain.then(nc.vector.tensor_tensor(qk(t), qk(t), rstd[:, t, :].unsqueeze(2).to_broadcast([P, heads, HEAD]), ALU.mult))
                chain.then(nc.vector.tensor_tensor(qk(t), qk(t), gain[:], ALU.mult))
                if t < 2:
                    for half in range(2):
                        for part in range(2):
                            to = slice(half * 64 + part * 32, half * 64 + part * 32 + 32)
                            of = slice(half * 64 + (1 - part) * 32, half * 64 + (1 - part) * 32 + 32)
                            sin = table[:, t, 1, to].unsqueeze(1).to_broadcast([P, heads, 32])
                            ins = nc.vector.tensor_tensor(turned[:, :, to], qk(t)[:, :, of], sin, ALU.mult)
                    chain.then(ins)
                    cos = table[:, t, 0, :].unsqueeze(1).to_broadcast([P, heads, HEAD])
                    chain.then(nc.vector.tensor_tensor(qk(t), qk(t), cos, ALU.mult))
                    chain.then(nc.vector.tensor_tensor(qk(t), qk(t), turned[:], ALU.add))



def fourier_stages(nc, psum, proj, cat, w_fnet, dft_tokens, dft_channels):
    with Stage(nc, "fourier_tables") as st:
        tok = st.sbuf("tok", [P, 2, 2, LAT])
        chan = st.sbuf("chan", [P, 2, P])
        mix = st.sbuf("mix", [P, 2, P])
        half = st.sbuf("half", [P, 2, 2, TOK])
        spectrum = st.sbuf("spectrum", [P, 2, TOK])
        loaded, cleared = st.sem("loaded"), st.sem("cleared")
        with nc.Block() as block:
            @block.gpsimd
            def _(pool):
                nc.gpsimd.memset(mix[:], 0.0).then_inc(cleared, 1)

            @block.sync
            def _(sp):
                sp.dma_start(tok[:], dft_tokens).then_inc(loaded, 16)
                sp.dma_start(chan[:], dft_channels).then_inc(loaded, 16)
                sp.wait_ge(cleared, 1)
                for g in range(4):
                    at = slice((g % 2) * 64, (g % 2) * 64 + 64)
                    sp.dma_start(mix[at, g // 2, at], w_fnet[g]).then_inc(loaded, 16)
                sp.wait_ge(loaded, 96)

        tiles = []
        for side in range(2):
            for m in range(2):
                for part in range(2):
                    tiles.append((side, m, part))
        resident_product_stage(
            nc, "fourier_tokens", psum,
            [(P, LAT, [(proj[:, 2 * side + t, m * P:(m + 1) * P], tok[:, t, part, :]) for t in range(2)])
             for side, m, part in tiles],
            lambda engine, g, bank: copy_on(nc, engine, half[:, tiles[g][2], tiles[g][1], tiles[g][0] * LAT:(tiles[g][0] + 1) * LAT], bank))
        resident_product_stage(
            nc, "fourier_channels", psum,
            [(P, TOK, [(chan[:, part, :], half[:, part, m, :]) for part in range(2)]) for m in range(2)],
            lambda engine, g, bank: copy_on(nc, engine, spectrum[:, g, :], bank))
        resident_product_stage(
            nc, "fourier_mix", psum,
            [(P, TOK, [(mix[:, m, :], spectrum[:, m, :])]) for m in range(2)],
            lambda engine, g, bank: copy_on(nc, engine, cat[:, g, :], bank))



def router_stage(nc, name, psum, cols, w_router, e_bias, routes, tok_tiles):
    with Stage(nc, name) as st:
        w, bias = st.sbuf("w", [P, KD, N_EXPERTS]), st.sbuf("bias", [P, N_EXPERTS])
        scores, ranked = st.sbuf("scores", [P, tok_tiles, N_EXPERTS]), st.sbuf("ranked", [P, tok_tiles, N_EXPERTS])
        struck, top = st.sbuf("struck", [P, tok_tiles, N_EXPERTS]), st.sbuf("top", [P, tok_tiles, 8])
        total, inv = st.sbuf("total", [P, tok_tiles]), st.sbuf("inv", [P, tok_tiles])
        loaded, products, squashed, chain_sem = st.sem("loaded"), st.sem("products"), st.sem("squashed"), st.sem("chain")
        block = st.block()

        @block.sync
        def _(sp):
            sp.dma_start(w[:], w_router.rearrange("(k p) e -> p k e", p=P)).then_inc(loaded, 16)
            sp.dma_start(bias[:], rows_of(e_bias)).then_inc(loaded, 16)

        @block.tensor
        def _(pe):
            pe.wait_ge(loaded, 32)
            for t in range(tok_tiles):
                for k in range(KD):
                    last = nc.tensor.matmul(psum[:, t, 0:N_EXPERTS], cols[:, k, t * P:(t + 1) * P], w[:, k, :], start=k == 0, stop=k == KD - 1)
                last.then_inc(products, 1)

        @block.scalar
        def _(act):
            for t in range(tok_tiles):
                act.wait_ge(products, t + 1)
                nc.scalar.activation(scores[:, t, :], psum[:, t, 0:N_EXPERTS], ACT.Sigmoid).then_inc(squashed, 1)

        @block.vector
        def _(dve):
            chain = Chain(dve, chain_sem)
            chain.then(nc.vector.memset(routes[:], 1.0))
            dve.wait_ge(loaded, 32)
            for t in range(tok_tiles):
                dve.wait_ge(squashed, t + 1)
                chain.then(nc.vector.tensor_tensor(ranked[:, t, :], scores[:, t, :], bias[:], ALU.add))
                chain.then(nc.vector.max(top[:, t, :], ranked[:, t, :]))
                chain.then(nc.vector.match_replace(struck[:, t, :], top[:, t, :], ranked[:, t, :], NEG))
                chain.then(nc.vector.tensor_tensor(struck[:, t, :], struck[:, t, :], ranked[:, t, :], ALU.not_equal))
                chain.then(nc.vector.tensor_tensor(struck[:, t, :], struck[:, t, :], scores[:, t, :], ALU.mult))
                chain.then(nc.vector.reduce_sum(total[:, t:t + 1], struck[:, t, :], X_AXIS))
                chain.then(nc.vector.reciprocal(inv[:, t:t + 1], total[:, t:t + 1]))
                chain.then(nc.vector.tensor_scalar(routes[:, t, 0:N_EXPERTS], struck[:, t, :], inv[:, t:t + 1], ROUTE_SCALE, ALU.mult, ALU.mult))



def gated_units_stage(nc, name, psum, weights, first, n, cols, tokens, routes, acc):
    width = 256
    nd = tokens // P * 2
    with Stage(nc, name) as st:
        wbuf = st.sbuf("w", [P, 2, 6 * D])
        silu = st.sbuf("silu", [P, 2, tokens])
        gated = st.sbuf("gated", [P, 2, 2, tokens])
        loaded = [st.sem(f"loaded{i}") for i in range(2)]
        ups, silus, gates, downs, added = st.sem("ups"), st.sem("silus"), st.sem("gates"), st.sem("downs"), st.sem("added")
        block = st.block()
        gate_up = [wbuf[:, s, 0:4 * D].rearrange("p (k n) -> p k n", k=KD) for s in range(2)]
        down = [wbuf[:, s, 4 * D:6 * D].rearrange("p (m n) -> p m n", m=2) for s in range(2)]

        @block.sync
        def _(sp):
            for s in range(2):
                sp.dma_start(wbuf[:, s, :], weights[first + s]).then_inc(loaded[s], 16)
            with sp.Fori(1, n // 2) as i:
                for s in range(2):
                    sp.wait_ge(downs, i * (2 * nd) + (s - 1) * nd)
                    sp.dma_start(wbuf[:, s, :], weights[2 * i + (first + s)]).then_inc(loaded[s], 16)
            sp.wait_ge(downs, (n - 2) * nd)
            sp.dma_start(wbuf[:, 0, :], weights[first + n - 1]).then_inc(loaded[0], 16)

        @block.tensor
        def _(pe):
            def ups_of(slot, loads, earlier):
                pe.wait_ge(loaded[slot], loads)
                for m in range(2):
                    for kind in range(2):
                        if earlier is not None:
                            pe.wait_ge(gates if kind else silus, earlier + (m - 1))
                        for k in range(KD):
                            last = nc.tensor.matmul(psum[:, 2 * m + kind, 0:tokens], gate_up[slot][:, k, kind * width + m * P:kind * width + (m + 1) * P],
                                                    cols[:, k, 0:tokens], start=k == 0, stop=k == KD - 1)
                        last.then_inc(ups, 1)

            def down_of(slot, gates_wanted, adds_before):
                pe.wait_ge(gates, gates_wanted)
                for d in range(nd):
                    pe.wait_ge(added, adds_before + (d + 1))
                    for m in range(2):
                        last = nc.tensor.matmul(psum[:, 4 + d % 4, :], gated[:, slot, m, (d // 2) * P:(d // 2 + 1) * P],
                                                down[slot][:, m, (d % 2) * BANK:(d % 2 + 1) * BANK], start=m == 0, stop=m == 1)
                    last.then_inc(downs, 1)

            ups_of(0, 16, None)
            with pe.Fori(0, n // 2) as i:
                ups_of(1, 16 * i + 16, 4 * i + 2)
                down_of(0, 4 * i + 2, i * (2 * nd))
                ups_of(0, 16 * i + 32, 4 * i + 4)
                down_of(1, 4 * i + 4, i * (2 * nd) + nd)
            down_of(0, 2 * n, (n - 1) * nd)

        @block.scalar
        def _(act):
            def silus_of(ups_before, gates_before):
                for m in range(2):
                    act.wait_ge(ups, ups_before + (2 * m + 1))
                    if gates_before is not None:
                        act.wait_ge(gates, gates_before + (m - 1))
                    nc.scalar.activation(silu[:, m, :], psum[:, 2 * m, 0:tokens], ACT.Silu).then_inc(silus, 1)

            silus_of(0, None)
            with act.Fori(0, n // 2) as i:
                silus_of(8 * i + 4, 4 * i + 2)
                silus_of(8 * i + 8, 4 * i + 4)

        @block.vector
        def _(dve):
            def gates_of(slot, ups_before, silus_before):
                for m in range(2):
                    dve.wait_ge(ups, ups_before + (2 * m + 2))
                    dve.wait_ge(silus, silus_before + (m + 1))
                    nc.vector.tensor_tensor(gated[:, slot, m, :], silu[:, m, :], psum[:, 2 * m + 1, 0:tokens], ALU.mult).then_inc(gates, 1)

            def adds_of(expert, downs_before):
                for d in range(nd):
                    dve.wait_ge(downs, downs_before + (d + 1))
                    dve.wait_ge(added, downs_before + (d + 1))
                    part = acc[:, d // 2, (d % 2) * BANK:(d % 2 + 1) * BANK]
                    if routes is None:
                        ins = nc.vector.tensor_tensor(part, psum[:, 4 + d % 4, :], part, ALU.add)
                    else:
                        ins = nc.vector.scalar_tensor_tensor(part, psum[:, 4 + d % 4, :], routes[:, d // 2, bass.ds(expert, 1)], part, ALU.mult, ALU.add)
                    ins.then_inc(added, 1)

            for q in range(4):
                rows = acc[:, 0:tokens // P, :].rearrange("p t n -> p (t n)")
                quarter = tokens // P * D // 4
                nc.vector.memset(rows[:, q * quarter:(q + 1) * quarter], 0.0).then_inc(added, 1)
            gates_of(0, 0, 0)
            with dve.Fori(0, n // 2) as i:
                gates_of(1, 8 * i + 4, 4 * i + 2)
                adds_of(2 * i, i * (2 * nd))
                gates_of(0, 8 * i + 8, 4 * i + 4)
                adds_of(2 * i + 1, i * (2 * nd) + nd)
            adds_of(n - 1, (n - 1) * nd)



def neighbourhood_bias_stage(nc, table, rpb_turned, column_mask):
    with Stage(nc, "na_bias") as st:
        mask = st.sbuf("mask", [P, GRID_W])
        turned = st.sbuf("turned", [P, 2, NA_HEADS, LAT])
        loaded, masked = st.sem("loaded"), st.sem("masked")
        block = st.block()

        @block.sync
        def _(sp):
            sp.dma_start(mask[:], column_mask).then_inc(loaded, 16)
            for qt in range(2):
                for r in range(2):
                    dr0 = NA_KH - 1 - (2 * qt + r)
                    for h in range(NA_HEADS):
                        start = rpb_turned[h, dr0:dr0 + GRID_ROWS, 0:GRID_W]
                        diagonal = bass.AP(start.tensor, start.offset, [[1, GRID_W], [RPB_W, GRID_ROWS], [1, GRID_W]])
                        sp.dma_start(turned[r * GRID_W:(r + 1) * GRID_W, qt, h, :].rearrange("p (a b) -> p a b", b=GRID_W), diagonal).then_inc(loaded, 16)

        @block.vector
        def _(dve):
            dve.wait_ge(loaded, 16 * (1 + 4 * NA_HEADS))
            for qt in range(2):
                out = table[:, qt, :, :].rearrange("p h (a b) -> p (h a) b", b=GRID_W)
                of = turned[:, qt, :, :].rearrange("p h (a b) -> p (h a) b", b=GRID_W)
                steps = [list(x) for x in of.ap]
                right_to_left = bass.AP(of.tensor, of.offset + GRID_W - 1, [*steps[:2], [-1, GRID_W]])
                nc.vector.tensor_tensor(out, right_to_left, mask[:].unsqueeze(1).to_broadcast([P, NA_HEADS * GRID_ROWS, GRID_W]), ALU.add).then_inc(masked, 1)



def first_block(nc, i, psum, ident, x, cols, acc, mod_cols, mod_dram):
    modulation_stage(nc, psum, ident, i["cvec"], i["w_mod"], i["b_mod"], mod_dram, mod_cols)

    def gate(layer, kind, row):
        return mod_dram[layer, row, kind * D:(kind + 1) * D]

    def to_rows(dst):
        return lambda engine, c, t, bank: copy_on(nc, engine, dst[:, t, c * BANK:(c + 1) * BANK], bank)

    def attention_outputs_to_cols(name, n_heads, tok_tiles, dst, k0):
        transpose_stage(nc, name, psum, ident, n_heads, tok_tiles, lambda j, t: acc[:, t, j * HEAD:(j + 1) * HEAD],
                        lambda engine, j, bank: copy_on(nc, engine, dst[:, k0 + j, 0:tok_tiles * P], bank[:, 0:tok_tiles * P]))

    for layer in range(DEPTH):
        tok_tiles = 4 if layer == 0 else 2
        modulated_cols(nc, f"h{layer}", psum, ident, x, cols, mod_cols, layer, 1, 4)
        if layer == 0:
            with Stage(nc, "ab") as st:
                proj = st.sbuf("proj", [P, 4, 3 * BANK])
                rows_product(nc, "ab_in", psum, cols, i["ab_w_in"], KD, 4, to_rows(proj))
                norm_rope_stage(nc, proj, i["qk_gains"], i["rope"])
                with Stage(nc, "ab_qk") as st2:
                    qk = st2.sbuf("qk", [P, 8, TOK])
                    transpose_stage(nc, "qk_t", psum, ident, 8, 4, lambda j, t: proj[:, t, LAT + j * HEAD:LAT + (j + 1) * HEAD],
                                    lambda engine, j, bank: copy_on(nc, engine, qk[:, j, :], bank))
                    units = [(h, t) for t in range(4) for h in range(6)]
                    first_key = lambda u: 0 if u[1] < 2 else LAT
                    attention_stage(
                        nc, "ab_att", psum, ident, units,
                        lambda u: [(0, qk[:, u[0], u[1] * P:(u[1] + 1) * P], qk[:, 6 + u[0] // 3, first_key(u):TOK])],
                        lambda u: TOK - first_key(u), lambda u: [], HEAD ** -0.5,
                        lambda u: [proj[:, t, 10 * HEAD + (u[0] // 3) * HEAD:10 * HEAD + (u[0] // 3 + 1) * HEAD] for t in range(first_key(u) // P, 4)],
                        lambda u: acc[:, u[1], u[0] * HEAD:(u[0] + 1) * HEAD], HEAD)
                fourier_stages(nc, psum, proj, cols, i["ab_w_fnet"], i["dft_tokens"], i["dft_channels"])
                attention_outputs_to_cols("ab_o", 6, 4, cols, 2)
            rows_product(nc, "ab_out", psum, cols, i["ab_w_out"], KD, 4, to_rows(acc))
        else:
            with Stage(nc, "na") as st:
                q, k, v = st.sbuf("q", [P, 8, LAT]), st.sbuf("k", [P, 8, TOK]), st.sbuf("v", [P, 4, D])
                cols_product(nc, "na_qk", psum, cols, i["na_w_in"][0:4], lambda c: LAT if c < 2 else TOK,
                             lambda engine, c, t, bank: copy_on(nc, engine, (q if c < 2 else k)[:, (c % 2) * 4 + t, :], bank))
                rows_product(nc, "na_v", psum, cols, i["na_w_in"][4:6], KD, 4, to_rows(v))
                with Stage(nc, "na2") as st2:
                    table = st2.sbuf("table", [P, 2, NA_HEADS, LAT])
                    neighbourhood_bias_stage(nc, table, i["rpb_turned"], i["column_mask"])
                    units = [(h, t) for t in range(2) for h in range(NA_HEADS)]
                    attention_stage(
                        nc, "na_att", psum, ident, units,
                        lambda u: [(0, q[:, u[0], u[1] * P:(u[1] + 1) * P], k[:, u[0], :])],
                        lambda u: TOK,
                        lambda u: [(slice(0, LAT), table[:, u[1], u[0], :], None), (slice(LAT, TOK), None, None)], HEAD ** -0.5,
                        lambda u: [v[:, t, u[0] * HEAD:(u[0] + 1) * HEAD] for t in range(4)],
                        lambda u: acc[:, u[1], u[0] * HEAD:(u[0] + 1) * HEAD], HEAD)
                attention_outputs_to_cols("na_o", 8, 2, cols, 0)
            rows_product(nc, "na_out", psum, cols, i["na_w_out"], KD, 2, to_rows(acc))
        residual_norm_stage(nc, f"ln1_{layer}", x, acc, tok_tiles, gate(layer, 2, 0), gate(layer, 2, 1), i["ln1_g"][layer], i["ln1_b"][layer])
        modulated_cols(nc, f"h2_{layer}", psum, ident, x, cols, mod_cols, layer, 4, tok_tiles)
        with Stage(nc, f"moe{layer}") as st:
            routes = st.sbuf("routes", [P, tok_tiles, N_EXPERTS + 1])
            router_stage(nc, f"router{layer}", psum, cols, i["w_router"][layer], i["moe_bias"][layer], routes, tok_tiles)
            gated_units_stage(nc, f"experts{layer}", psum, i["experts"], layer * (N_EXPERTS + 1), N_EXPERTS + 1, cols, tok_tiles * P, routes, acc)
        residual_norm_stage(nc, f"ln2_{layer}", x, acc, tok_tiles, gate(layer, 5, 0), gate(layer, 5, 1), i["ln2_g"][layer], i["ln2_b"][layer])



def rms_stage(nc, name, source, out, width, tok_tiles, gate=None):
    with Stage(nc, name) as st:
        square, ss = st.sbuf("square", [P, width]), st.sbuf("ss", [P, tok_tiles])
        std, rstd = st.sbuf("std", [P, tok_tiles]), st.sbuf("rstd", [P, tok_tiles])
        activated, gated, squared, varied, rooted, chain_sem = (
            st.sem("activated"), st.sem("gated"), st.sem("squared"), st.sem("varied"), st.sem("rooted"), st.sem("chain"))
        block = st.block()

        @block.scalar
        def _(act):
            if gate is not None:
                for t in range(tok_tiles):
                    nc.scalar.activation(gate[:, t, :], gate[:, t, :], ACT.Silu).then_inc(activated, 1)
            for t in range(tok_tiles):
                if gate is not None:
                    act.wait_ge(gated, t + 1)
                if t >= 1:
                    act.wait_ge(squared, t)
                nc.scalar.activation(square[:], source[:, t, 0:width], ACT.Square, accum_out=ss[:, t:t + 1]).then_inc(squared, 1)
            for t in range(tok_tiles):
                act.wait_ge(varied, t + 1)
                nc.scalar.activation(std[:, t:t + 1], ss[:, t:t + 1], ACT.Sqrt).then_inc(rooted, 1)

        @block.vector
        def _(dve):
            chain = Chain(dve, chain_sem)
            if gate is not None:
                for t in range(tok_tiles):
                    dve.wait_ge(activated, t + 1)
                    nc.vector.tensor_tensor(source[:, t, :], source[:, t, :], gate[:, t, :], ALU.mult).then_inc(gated, 1)
            for t in range(tok_tiles):
                dve.wait_ge(squared, t + 1)
                nc.vector.tensor_scalar(ss[:, t:t + 1], ss[:, t:t + 1], 1.0 / width, EPS, ALU.mult, ALU.add).then_inc(varied, 1)
            for t in range(tok_tiles):
                dve.wait_ge(rooted, t + 1)
                chain.then(nc.vector.reciprocal(rstd[:, t:t + 1], std[:, t:t + 1]))
                chain.then(nc.vector.tensor_scalar(out[:, t, 0:width], source[:, t, 0:width], rstd[:, t:t + 1], None, ALU.mult))


def scaled_cols(nc, name, psum, ident, rows, cols, k0, gain_cols):
    def drain(engine, j, bank):
        if engine == "v":
            return nc.vector.tensor_scalar(cols[:, k0 + j, 0:LAT], bank[:, 0:LAT], gain_cols[:, j:j + 1], None, ALU.mult)
        return nc.scalar.activation(cols[:, k0 + j, 0:LAT], bank[:, 0:LAT], ACT.Copy, scale=gain_cols[:, j:j + 1])
    transpose_stage(nc, name, psum, ident, KD, 2, lambda j, i: rows[:, i, j * P:(j + 1) * P], drain)


def add_scaled_stage(nc, name, x, y, gain, factor):
    with Stage(nc, name) as st:
        vec = st.sbuf("vec", [P, D])
        loaded, chain_sem = st.sem("loaded"), st.sem("chain")
        block = st.block()

        @block.sync
        def _(sp):
            sp.dma_start(vec[:], rows_of(gain)).then_inc(loaded, 16)

        @block.vector
        def _(dve):
            chain = Chain(dve, chain_sem)
            dve.wait_ge(loaded, 16)
            for t in range(2):
                chain.then(nc.vector.scalar_tensor_tensor(y[:, t, :], y[:, t, :], factor, vec[:], ALU.mult, ALU.mult))
                chain.then(nc.vector.tensor_tensor(x[:, t, :], x[:, t, :], y[:, t, :], ALU.add))



def causal_conv_stage(nc, name, padded, out, taps, bias, n_tiles, n_taps, activation=None):
    with Stage(nc, name) as st:
        w, b = st.sbuf("w", [P, n_tiles, n_taps]), st.sbuf("b", [P, n_tiles])
        loaded, tapped, activated = st.sem("loaded"), st.sem("tapped"), st.sem("activated")
        block = st.block()

        @block.sync
        def _(sp):
            sp.dma_start(w[:], taps).then_inc(loaded, 16)
            sp.dma_start(b[:], bias).then_inc(loaded, 16)

        @block.vector
        def _(dve):
            dve.wait_ge(loaded, 32)
            for j in range(n_taps):
                for m in range(n_tiles):
                    source = padded[:, m, j:j + LAT]
                    if j == 0:
                        ins = nc.vector.tensor_scalar(out[:, m, :], source, w[:, m, 0:1], b[:, m:m + 1], ALU.mult, ALU.add)
                    else:
                        dve.wait_ge(tapped, (j - 1) * n_tiles + m + 1)
                        ins = nc.vector.scalar_tensor_tensor(out[:, m, :], source, w[:, m, j:j + 1], out[:, m, :], ALU.mult, ALU.add)
                    ins.then_inc(tapped, 1)

        if activation is not None:
            @block.scalar
            def _(act):
                for m in range(n_tiles):
                    act.wait_ge(tapped, (n_taps - 1) * n_tiles + m + 1)
                    nc.scalar.activation(out[:, m, :], out[:, m, :], activation).then_inc(activated, 1)


def glu_stage(nc, val_gate, hidden, pad):
    with Stage(nc, "glu") as st:
        squashed, made = st.sem("squashed"), st.sem("made")
        block = st.block()

        @block.scalar
        def _(act):
            for half in range(2):
                at = val_gate[:, KD + 4 * half:KD + 4 * half + 4, :]
                nc.scalar.activation(at, at, ACT.Sigmoid).then_inc(squashed, 1)

        @block.gpsimd
        def _(pool):
            nc.gpsimd.memset(hidden[:, :, 0:pad], 0.0).then_inc(made, 1)

        @block.vector
        def _(dve):
            for half in range(2):
                dve.wait_ge(squashed, half + 1)
                ks = slice(4 * half, 4 * half + 4)
                nc.vector.tensor_tensor(hidden[:, ks, pad:pad + LAT], val_gate[:, ks, :],
                                        val_gate[:, KD + 4 * half:KD + 4 * half + 4, :], ALU.mult).then_inc(made, 1)


def conformer_norm_stage(nc, psum, hid, cat, averager, gain_cols, shift_cols):
    with Stage(nc, "conformer") as st:
        avg, gain, shift = st.sbuf("avg", [P, P]), st.sbuf("gain", [P, KD]), st.sbuf("shift", [P, KD])
        square, rstd = st.sbuf("square", [P, KD, LAT]), st.sbuf("rstd", [P, LAT])
        loaded, means, centred, squared, variances = st.sem("loaded"), st.sem("means"), st.sem("centred"), st.sem("squared"), st.sem("variances")
        shifted, rooted, scaled, activated, chain_sem = st.sem("shifted"), st.sem("rooted"), st.sem("scaled"), st.sem("activated"), st.sem("chain")
        block = st.block()

        @block.sync
        def _(sp):
            sp.dma_start(avg[:], averager).then_inc(loaded, 16)
            sp.dma_start(gain[:], gain_cols).then_inc(loaded, 16)
            sp.dma_start(shift[:], shift_cols).then_inc(loaded, 16)

        @block.tensor
        def _(pe):
            pe.wait_ge(loaded, 48)
            for m in range(KD):
                last = nc.tensor.matmul(psum[:, 0, 0:LAT], avg[:], hid[:, m, :], start=m == 0, stop=m == KD - 1)
            last.then_inc(means, 1)
            for m in range(KD):
                pe.wait_ge(squared, m + 1)
                last = nc.tensor.matmul(psum[:, 1, 0:LAT], avg[:], square[:, m, :], start=m == 0, stop=m == KD - 1)
            last.then_inc(variances, 1)

        @block.vector
        def _(dve):
            chain = Chain(dve, chain_sem)
            dve.wait_ge(means, 1)
            for m in range(KD):
                nc.vector.tensor_tensor(hid[:, m, :], hid[:, m, :], psum[:, 0, 0:LAT], ALU.subtract).then_inc(centred, 1)
            dve.wait_ge(variances, 1)
            nc.vector.tensor_scalar(rstd[:], psum[:, 1, 0:LAT], EPS, None, ALU.add).then_inc(shifted, 1)
            dve.wait_ge(rooted, 1)
            chain.then(nc.vector.reciprocal(rstd[:], rstd[:]))
            for m in range(KD):
                dve.wait_ge(squared, m + 1)
                nc.vector.tensor_tensor(hid[:, m, :], hid[:, m, :], rstd[:], ALU.mult).then_inc(scaled, 1)

        @block.scalar
        def _(act):
            act.wait_ge(loaded, 48)
            for m in range(KD):
                act.wait_ge(centred, m + 1)
                nc.scalar.activation(square[:, m, :], hid[:, m, :], ACT.Square).then_inc(squared, 1)
            act.wait_ge(shifted, 1)
            nc.scalar.activation(rstd[:], rstd[:], ACT.Sqrt).then_inc(rooted, 1)
            for m in range(KD):
                act.wait_ge(scaled, m + 1)
                nc.scalar.activation(cat[:, m, :], hid[:, m, :], ACT.Silu, scale=gain[:, m:m + 1], bias=shift[:, m:m + 1]).then_inc(activated, 1)



def time_step_stage(nc, dt_raw, dt_bias, a_log, dt, da):
    with Stage(nc, "time_step") as st:
        shape = [P, 2, SSM_HEADS]
        bias, rate = st.sbuf("bias", [P, SSM_HEADS]), st.sbuf("rate", [P, SSM_HEADS])
        size, tail = st.sbuf("size", shape), st.sbuf("tail", shape)
        loaded, biased, tailed, rated, chain_sem, act_chain = (
            st.sem("loaded"), st.sem("biased"), st.sem("tailed"), st.sem("rated"), st.sem("chain"), st.sem("act_chain"))
        block = st.block()

        @block.sync
        def _(sp):
            sp.dma_start(bias[:], rows_of(dt_bias)).then_inc(loaded, 16)
            sp.dma_start(rate[:], rows_of(a_log)).then_inc(loaded, 16)

        @block.scalar
        def _(act):
            chain = Chain(act, act_chain)
            act.wait_ge(loaded, 32)
            nc.scalar.activation(rate[:], rate[:], ACT.Exp).then_inc(rated, 1)
            act.wait_ge(biased, 1)
            chain.then(nc.scalar.activation(size[:], dt_raw[:], ACT.Abs))
            chain.then(nc.scalar.activation(size[:], size[:], ACT.Exp, scale=-1.0))
            nc.scalar.activation(tail[:], size[:], ACT.Ln, bias=1.0).then_inc(tailed, 1)

        @block.vector
        def _(dve):
            chain = Chain(dve, chain_sem)
            dve.wait_ge(loaded, 32)
            nc.vector.tensor_tensor(dt_raw[:], dt_raw[:], bias[:].unsqueeze(1).to_broadcast(shape), ALU.add).then_inc(biased, 1)
            dve.wait_ge(tailed, 1)
            dve.wait_ge(rated, 1)
            chain.then(nc.vector.scalar_tensor_tensor(dt[:], dt_raw[:], 0.0, tail[:], ALU.max, ALU.add))
            chain.then(nc.vector.scalar_tensor_tensor(da[:], dt[:], -1.0, rate[:].unsqueeze(1).to_broadcast(shape), ALU.mult, ALU.mult))


def state_space_stages(nc, psum, ident, xbc, dt, da, triangles, d_skip, y):
    heads, dim = SSM_HEADS, SSM_P
    per = heads // 2
    with Stage(nc, "ssd") as st:
        tri = st.sbuf("tri", [P, 2, P])
        skip = st.sbuf("skip", [P, heads])
        spread = st.sbuf("spread", [P, 2, heads, P])
        x_rows, x_dt = st.sbuf("x_rows", [P, 2, D]), st.sbuf("x_dt", [P, 2, D])
        x_state = st.sbuf("x_state", [P, D])
        b_rows = st.sbuf("b_rows", [P, 2, P])
        cum, tail_decay, cum_exp = st.sbuf("cum", [P, 2, heads]), st.sbuf("tail_decay", [P, heads]), st.sbuf("cum_exp", [P, heads])
        pair = st.sbuf("pair", [P, 2, 2, P])
        decay = st.sbuf("decay", [P, 2, heads, P])
        state = st.sbuf("state", [P, 2, BANK])
        loaded, chain_sem = st.sem("loaded"), st.sem("chain")
        rows_turned, rows_out = st.sem("rows_turned"), st.sem("rows_out")
        sums_ready, sums_out, spread_made = st.sem("sums_ready"), st.sem("sums_out"), st.sem("spread_made")
        pairs_ready, pairs_out = st.sem("pairs_ready"), st.sem("pairs_out")
        with nc.Block() as block:
            @block.sync
            def _(sp):
                sp.dma_start(tri[:], triangles).then_inc(loaded, 16)
                sp.dma_start(skip[:], rows_of(d_skip)).then_inc(loaded, 16)

            @block.tensor
            def _(pe):
                for c in range(2):
                    for k in range(KD):
                        last = nc.tensor.transpose(psum[:, 2 * c + k // 4, (k % 4) * P:(k % 4 + 1) * P], xbc[:, k, c * P:(c + 1) * P], ident[:])
                    last.then_inc(rows_turned, 1)
                for g in range(2):
                    last = nc.tensor.transpose(psum[:, 4, g * P:(g + 1) * P], xbc[:, KD + g, 0:P], ident[:])
                last.then_inc(rows_turned, 1)
                pe.wait_ge(loaded, 32)
                for c in range(2):
                    nc.tensor.matmul(psum[:, 5, c * heads:(c + 1) * heads], tri[:, 0, :], da[:, c, :], start=True, stop=True)
                nc.tensor.matmul(psum[:, 5, 2 * heads:3 * heads], tri[:, 1, :], da[:, 0, :], start=True, stop=True).then_inc(sums_ready, 1)
                for c in range(2):
                    for g in range(2):
                        last = nc.tensor.matmul(psum[:, 6, (2 * c + g) * P:(2 * c + g + 1) * P], xbc[:, KD + g, c * P:(c + 1) * P],
                                                xbc[:, KD + 2 + g, c * P:(c + 1) * P], start=True, stop=True)
                last.then_inc(pairs_ready, 1)

            @block.scalar
            def _(act):
                act.wait_ge(rows_turned, 1)
                nc.scalar.activation(x_rows[:, 0, :], psum[:, 0:2, :].rearrange("p b n -> p (b n)"), ACT.Copy).then_inc(rows_out, 1)
                act.wait_ge(rows_turned, 2)
                nc.scalar.activation(x_rows[:, 1, :], psum[:, 2:4, :].rearrange("p b n -> p (b n)"), ACT.Copy).then_inc(rows_out, 1)
                act.wait_ge(rows_turned, 3)
                nc.scalar.activation(b_rows[:], psum[:, 4, 0:2 * P].rearrange("p (g n) -> p g n", g=2), ACT.Copy).then_inc(rows_out, 1)
                act.wait_ge(sums_out, 1)
                nc.scalar.activation(tail_decay[:], psum[:, 5, 2 * heads:3 * heads], ACT.Exp).then_inc(sums_out, 1)
                nc.scalar.activation(cum_exp[:], psum[:, 5, heads:2 * heads], ACT.Exp).then_inc(sums_out, 1)

            @block.gpsimd
            def _(pool):
                for c in range(2):
                    nc.gpsimd.tensor_copy(spread[:, c, :, :], da[:, c, :].unsqueeze(2).to_broadcast([P, heads, P])).then_inc(spread_made, 1)

            @block.vector
            def _(dve):
                chain = Chain(dve, chain_sem)
                dve.wait_ge(sums_ready, 1)
                nc.vector.tensor_copy(cum[:], psum[:, 5, 0:2 * heads].rearrange("p (c h) -> p c h", c=2)).then_inc(sums_out, 1)
                dve.wait_ge(pairs_ready, 1)
                dve.wait_ge(loaded, 32)
                nc.vector.tensor_tensor(pair[:].rearrange("p c g l -> p (c g) l"), psum[:, 6, :].rearrange("p (a l) -> p a l", l=P),
                                        tri[:, 0, :].unsqueeze(1).to_broadcast([P, 4, P]), ALU.mult).then_inc(pairs_out, 1)
                for c in range(2):
                    dve.wait_ge(rows_out, c + 1)
                    chain.then(nc.vector.tensor_tensor(x_dt[:, c, :].rearrange("p (h d) -> p h d", d=dim), x_rows[:, c, :].rearrange("p (h d) -> p h d", d=dim),
                                                       dt[:, c, :].unsqueeze(2).to_broadcast([P, heads, dim]), ALU.mult))
                dve.wait_ge(sums_out, 3)
                chain.then(nc.vector.tensor_tensor(x_state[:].rearrange("p (h d) -> p h d", d=dim), x_dt[:, 0, :].rearrange("p (h d) -> p h d", d=dim),
                                                   tail_decay[:].unsqueeze(2).to_broadcast([P, heads, dim]), ALU.mult))

        decays, narrowed, exped, weighed = st.sem("decays"), st.sem("narrowed"), st.sem("exped"), st.sem("weighed")
        with nc.Block() as block:
            @block.tensor
            def _(pe):
                for b in range(8):
                    for j in range(4):
                        h = 4 * (b % 4) + j
                        last = nc.tensor.matmul(psum[:, b, j * P:(j + 1) * P], spread[:, b // 4, h, :], tri[:, 0, :], start=True, stop=True)
                    last.then_inc(decays, 1)

            @block.vector
            def _(dve):
                for step in range(9):
                    if step < 8:
                        b = step
                        dve.wait_ge(decays, b + 1)
                        for j in range(4):
                            h = 4 * (b % 4) + j
                            last = nc.vector.tensor_scalar(decay[:, b // 4, h, :], psum[:, b, j * P:(j + 1) * P], cum[:, b // 4, h:h + 1], 0.0, ALU.subtract, ALU.min)
                        last.then_inc(narrowed, 1)
                    if step >= 1:
                        b = step - 1
                        dve.wait_ge(exped, b + 1)
                        at = decay[:, b // 4, 4 * (b % 4):4 * (b % 4) + 4, :]
                        nc.vector.tensor_tensor(at, at, pair[:, b // 4, (b % 4) // 2, :].unsqueeze(1).to_broadcast([P, 4, P]), ALU.mult).then_inc(weighed, 1)

            @block.scalar
            def _(act):
                for b in range(8):
                    act.wait_ge(narrowed, b + 1)
                    at = decay[:, b // 4, 4 * (b % 4):4 * (b % 4) + 4, :]
                    nc.scalar.activation(at, at, ACT.Exp).then_inc(exped, 1)

        states, states_out, inner, outer, chain2 = st.sem("states"), st.sem("states_out"), st.sem("inner"), st.sem("outer"), st.sem("chain2")
        with nc.Block() as block:
            @block.tensor
            def _(pe):
                for g in range(2):
                    last = nc.tensor.matmul(psum[:, 4 + g, :], b_rows[:, g, :], x_state[:, g * BANK:(g + 1) * BANK], start=True, stop=True)
                last.then_inc(states, 1)
                for c in range(2):
                    for h in range(heads):
                        last = nc.tensor.matmul(psum[:, 2 * c + h // per, (h % per) * dim:(h % per + 1) * dim], decay[:, c, h, :],
                                                x_dt[:, c, h * dim:(h + 1) * dim], start=True, stop=True)
                    last.then_inc(inner, 1)
                pe.wait_ge(states_out, 1)
                for g in range(2):
                    last = nc.tensor.matmul(psum[:, 6 + g, :], xbc[:, KD + 2 + g, P:2 * P], state[:, g, :], start=True, stop=True)
                last.then_inc(outer, 1)

            @block.scalar
            def _(act):
                act.wait_ge(states, 1)
                nc.scalar.activation(state[:], psum[:, 4:6, :], ACT.Copy).then_inc(states_out, 1)

            @block.vector
            def _(dve):
                chain = Chain(dve, chain2)
                for c in range(2):
                    chain.then(nc.vector.tensor_tensor(y[:, c, :].rearrange("p (h d) -> p h d", d=dim), x_rows[:, c, :].rearrange("p (h d) -> p h d", d=dim),
                                                       skip[:].unsqueeze(2).to_broadcast([P, heads, dim]), ALU.mult))
                    dve.wait_ge(inner, c + 1)
                    chain.then(nc.vector.tensor_tensor(y[:, c, :], y[:, c, :], psum[:, 2 * c:2 * c + 2, :].rearrange("p b n -> p (b n)"), ALU.add))
                dve.wait_ge(outer, 1)
                chain.then(nc.vector.tensor_tensor(x_state[:].rearrange("p (h d) -> p h d", d=dim), psum[:, 6:8, :].rearrange("p b (h d) -> p (b h) d", d=dim),
                                                   cum_exp[:].unsqueeze(2).to_broadcast([P, heads, dim]), ALU.mult))
                chain.then(nc.vector.tensor_tensor(y[:, 1, :], y[:, 1, :], x_state[:], ALU.add))



def second_block(nc, i, psum, ident, x, cols, acc):
    def ffn(layer, which):
        g = 4 * which
        name = f"ffn{layer}{which}"
        rms_stage(nc, name + "_pre", x, acc, D, 2)
        scaled_cols(nc, name + "_cols", psum, ident, acc, cols, 0, gains[:, layer, g, :])
        gated_units_stage(nc, name, psum, i["ffn"], (2 * layer + which) * FFN_PARTS, FFN_PARTS, cols, LAT, None, acc)
        rms_stage(nc, name + "_post", acc, acc, D, 2)
        add_scaled_stage(nc, name + "_add", x, acc, i["norm_g"][layer, g + 1], 0.5)

    def to_cols(dst, k0, per_chunk=4):
        return lambda engine, c, t, bank: copy_on(nc, engine, dst[:, k0 + c * per_chunk + t, :], bank)

    def to_rows(dst):
        return lambda engine, c, t, bank: copy_on(nc, engine, dst[:, t, c * BANK:(c + 1) * BANK], bank)

    with Stage(nc, "second") as top:
        gains, ssm_gain = top.sbuf("gains", [P, DEPTH, 6, KD]), top.sbuf("ssm_gain", [P, KD])
        loaded = top.sem("loaded")
        with nc.Block() as block:
            @block.sync
            def _(sp):
                sp.dma_start(gains[:], i["norm_g_cols"]).then_inc(loaded, 16)
                sp.dma_start(ssm_gain[:], i["ssm_norm_g_cols"]).then_inc(loaded, 16)
                sp.wait_ge(loaded, 32)
        for layer in range(DEPTH):
            ffn(layer, 0)
            rms_stage(nc, f"mix{layer}_pre", x, acc, D, 2)
            scaled_cols(nc, f"mix{layer}_cols", psum, ident, acc, cols, 0, gains[:, layer, 2, :])
            if layer == 0:
                with Stage(nc, "hyb") as st:
                    cat, z = st.sbuf("cat", [P, 2 * KD, LAT]), st.sbuf("z", [P, 2, D])
                    hid = st.sbuf("hid", [P, KD, CONV_TAPS - 1 + LAT])
                    xbc = st.sbuf("xbc", [P, 12, SSM_TAPS - 1 + LAT])
                    dt_raw, dt, da = (st.sbuf(n, [P, 2, SSM_HEADS]) for n in ("dt_raw", "dt", "da"))
                    with Stage(nc, "hyb_glu") as st2:
                        val_gate = st2.sbuf("val_gate", [P, 2 * KD, LAT])
                        cols_product(nc, "hyb_vg", psum, cols, i["hyb_w_in"][0:4], lambda c: LAT, to_cols(val_gate, 0))
                        glu_stage(nc, val_gate, hid, CONV_TAPS - 1)
                    rows_product(nc, "hyb_z", psum, cols, i["hyb_w_in"][4:6], KD, 2, to_rows(z))
                    cleared = st.sem("cleared")
                    with nc.Block() as block:
                        @block.gpsimd
                        def _(pool):
                            nc.gpsimd.memset(xbc[:, :, 0:SSM_TAPS - 1], 0.0).then_inc(cleared, 1)
                    cols_product(nc, "hyb_xbc", psum, cols, i["hyb_w_in"][6:9], lambda c: LAT,
                                 lambda engine, c, t, bank: copy_on(nc, engine, xbc[:, 4 * c + t, SSM_TAPS - 1:], bank))
                    rows_product(nc, "hyb_dt", psum, cols, i["hyb_w_dt"], KD, 2,
                                 lambda engine, c, t, bank: copy_on(nc, engine, dt_raw[:, t, :], bank))
                    with Stage(nc, "hyb_conv") as st2:
                        conv = st2.sbuf("conv", [P, KD, LAT])
                        causal_conv_stage(nc, "conv31", hid, conv, i["conv_taps"], i["conv_b_cols"], KD, CONV_TAPS)
                        conformer_norm_stage(nc, psum, conv, cat, i["averager"], i["conv_ln_g_cols"], i["conv_ln_b_cols"])
                    with Stage(nc, "hyb_ssm") as st2:
                        mixed = st2.sbuf("mixed", [P, 12, LAT])
                        causal_conv_stage(nc, "conv4", xbc, mixed, i["ssm_taps"], i["ssm_b_cols"], 12, SSM_TAPS, ACT.Silu)
                        time_step_stage(nc, dt_raw, i["ssm_dt_bias"], i["ssm_a_log"], dt, da)
                        state_space_stages(nc, psum, ident, mixed, dt, da, i["triangles"], i["ssm_d"], acc)
                        rms_stage(nc, "ssm_norm", acc, acc, D, 2, gate=z)
                        scaled_cols(nc, "ssm_cols", psum, ident, acc, cat, KD, ssm_gain)
                    rows_product(nc, "hyb_out", psum, cat, i["hyb_w_out"], 2 * KD, 2, to_rows(acc))
            else:
                with Stage(nc, "dil") as st:
                    q, k = st.sbuf("q", [P, 12, LAT]), st.sbuf("k", [P, 12, LAT])
                    v = st.sbuf("v", [P, 2, 3 * BANK])
                    cols_product(nc, "dil_q", psum, cols, i["attn_w_qkv"][0:3], lambda c: LAT, to_cols(q, 0))
                    cols_product(nc, "dil_k", psum, cols, i["attn_w_qkv"][3:6], lambda c: LAT, to_cols(k, 0))
                    rows_product(nc, "dil_v", psum, cols, i["attn_w_qkv"][6:9], KD, 2, to_rows(v))
                    with Stage(nc, "dil2") as st2:
                        table = st2.sbuf("table", [P, 2, DIL_GROUPS, LAT])
                        there = st2.sem("there")
                        with nc.Block() as block:
                            @block.sync
                            def _(sp):
                                sp.dma_start(table[:], i["distances"]).then_inc(there, 16)
                                sp.wait_ge(there, 16)
                        scale = DIL_DH ** -0.5
                        units = [(h, t) for t in range(2) for h in range(DIL_HEADS)]
                        n_keys = lambda t: P * (t + 1)

                        def head_of(tensor, h, g):
                            return tensor[(h % 2) * DIL_DH:(h % 2 + 1) * DIL_DH, 4 * g + h // 2, :]

                        attention_stage(
                            nc, "dil_att", psum, ident, units,
                            lambda u: [(g * n_keys(u[1]), head_of(q, u[0], g)[:, u[1] * P:(u[1] + 1) * P], head_of(k, u[0], g)[:, 0:n_keys(u[1])]) for g in range(DIL_GROUPS)],
                            lambda u: DIL_GROUPS * n_keys(u[1]),
                            lambda u: [(slice(g * n_keys(u[1]), (g + 1) * n_keys(u[1])), table[:, u[1], g, 0:n_keys(u[1])],
                                        -(2.0 ** -(u[0] + 1)) / scale) for g in range(DIL_GROUPS)],
                            scale,
                            lambda u: [v[:, t, g * BANK + u[0] * DIL_DH:g * BANK + (u[0] + 1) * DIL_DH] for g in range(DIL_GROUPS) for t in range(u[1] + 1)],
                            lambda u: acc[:, u[1], u[0] * DIL_DH:(u[0] + 1) * DIL_DH], DIL_DH)
                    transpose_stage(nc, "dil_o", psum, ident, 4, 2, lambda j, t: acc[:, t, j * P:(j + 1) * P],
                                    lambda engine, j, bank: copy_on(nc, engine, cols[:, j, 0:LAT], bank[:, 0:LAT]))
                rows_product(nc, "dil_out", psum, cols, i["attn_w_o"], 4, 2, to_rows(acc))
            rms_stage(nc, f"mix{layer}_post", acc, acc, D, 2)
            add_scaled_stage(nc, f"mix{layer}_add", x, acc, i["norm_g"][layer, 3], 1.0)
            ffn(layer, 1)



def program(nc, i, out):
    with Stage(nc, "all") as st:
        psum = st.stack.enter_context(nc.psum_tensor("psum", [P, NBANKS, BANK], F32))
        mod_dram = nc.dram_tensor("mod_dram", [DEPTH, 2, 6 * D], F32, kind="Internal").ap()
        x, cols, acc = st.sbuf("x", [P, 4, D]), st.sbuf("cols", [P, KD, TOK]), st.sbuf("acc", [P, 4, D])
        ident, mod_cols = st.sbuf("ident", [P, P]), st.sbuf("mod_cols", [P, DEPTH, 6 * KD, 2])
        loaded, stored = st.sem("loaded"), st.sem("stored")
        with nc.Block() as block:
            @block.sync
            def _(sp):
                sp.dma_start(x[:, 0:2, :], i["x"].rearrange("(t p) d -> p t d", p=P)).then_inc(loaded, 16)
                sp.dma_start(x[:, 2:4, :], i["ctx"].rearrange("(t p) d -> p t d", p=P)).then_inc(loaded, 16)
                sp.dma_start(ident[:], i["ident"]).then_inc(loaded, 16)
                sp.wait_ge(loaded, 48)
        first_block(nc, i, psum, ident, x, cols, acc, mod_cols, mod_dram)
        second_block(nc, i, psum, ident, x, cols, acc)
        with nc.Block() as block:
            @block.sync
            def _(sp):
                sp.dma_start(out.rearrange("(t p) d -> p t d", p=P), x[:, 0:2, :]).then_inc(stored, 16)
                sp.wait_ge(stored, 16)



def chunks(w, width=BANK, k_tiles=None):
    k, n = w.shape
    return np.ascontiguousarray(w.reshape(k // P, P, n // width, width).transpose(2, 1, 0, 3)).reshape(n // width, P, -1)


def gated_parts(gate, up, down):
    lead = gate.shape[:-2]
    n = gate.shape[-1] // 256
    g = gate.reshape(*lead, KD, P, n, 256)
    u = up.reshape(*lead, KD, P, n, 256)
    d = down.reshape(*lead, n, 2, P, D)
    g, u, d = np.moveaxis(g, -2, -4), np.moveaxis(u, -2, -4), np.swapaxes(d, -3, -2)
    g, u = np.swapaxes(g, -3, -2), np.swapaxes(u, -3, -2)
    out = np.empty((*lead, n, P, 6 * D), np.float32)
    gu = out[..., 0:4 * D].reshape(*lead, n, P, KD, 2, 256)
    out[..., 0:4 * D].reshape(*lead, n, P, KD, 2, 256)
    for kind, w in enumerate((g, u)):
        for k in range(KD):
            out[..., k * 512 + kind * 256:k * 512 + kind * 256 + 256] = w[..., k, :]
    for m in range(2):
        out[..., 4 * D + m * D:4 * D + (m + 1) * D] = d[..., m, :]
    return out.reshape(-1, P, 6 * D)


def shape_tables():
    t = {"ident": np.eye(P)}
    half, nf = HEAD // 2, HEAD // 4
    inv = (10000.0 ** (-(2.0 / half) * np.arange(nf, dtype=np.float32))).astype(np.float32)
    tok = np.arange(LAT)
    rope = np.zeros((LAT, 2, HEAD))
    for h, pos in enumerate((tok // GRID_W, tok % GRID_W)):
        ang = (pos.astype(np.float32)[:, None] * inv).astype(np.float64)
        rope[:, 0, h * half:(h + 1) * half] = np.concatenate([np.cos(ang)] * 2, -1)
        rope[:, 1, h * half:(h + 1) * half] = np.concatenate([-np.sin(ang), np.sin(ang)], -1)
    t["rope"] = rope.reshape(2, P, 2, HEAD).transpose(1, 0, 2, 3)
    n, c = np.arange(LAT), np.arange(64)
    tok_angle = 2 * np.pi * (np.outer(n, n) % LAT) / LAT
    chan_angle = 2 * np.pi * (np.outer(c, c) % 64) / 64
    t["dft_tokens"] = np.stack([np.cos(tok_angle), np.sin(tok_angle)], 1).reshape(2, P, 2, LAT).transpose(1, 0, 2, 3) / 16
    chan = np.zeros((P, 2, P))
    for g in range(2):
        chan[g * 64:(g + 1) * 64, 0, g * 64:(g + 1) * 64] = np.cos(chan_angle) / 8
        chan[g * 64:(g + 1) * 64, 1, g * 64:(g + 1) * 64] = -np.sin(chan_angle) / 8
    t["dft_channels"] = chan
    col = np.arange(GRID_W)
    start = np.clip(col - NA_KW // 2, 0, GRID_W - NA_KW)
    inside = (col[None, :] >= start[:, None]) & (col[None, :] < start[:, None] + NA_KW)
    t["column_mask"] = np.tile(np.where(inside, 0.0, NEG), (2, 1))
    return {name: np.ascontiguousarray(a, dtype=np.float32) for name, a in t.items()}


def first_block_arrays(v):
    a = {}
    a["x"], a["ctx"] = v["x"][0], v["ctx"][0]
    a["cvec"] = np.stack([v["c"][0], v["c_ctx"]], -1).reshape(KD, P, 2).transpose(1, 0, 2)
    a["w_mod"] = np.concatenate([chunks(v["w_mod"][l]) for l in range(DEPTH)])
    for n in ("b_mod", "ln1_g", "ln1_b", "ln2_g", "ln2_b", "moe_bias"):
        a[n] = v[n]
    a["w_router"] = v["moe_w_router"]
    a["ab_w_in"], a["ab_w_out"] = chunks(v["ab_w_in"][0]), chunks(v["ab_w_out"][0])
    a["na_w_in"], a["na_w_out"] = chunks(v["na_w_in"][0]), chunks(v["na_w_out"][0])
    a["ab_w_fnet"] = v["ab_w_fnet"][0]
    a["qk_gains"] = np.concatenate([np.tile(v["ab_q_norm"][0], 6), np.tile(v["ab_k_norm"][0], 2)])
    a["rpb_turned"] = np.pad(v["na_rpb"][0], ((0, 0), (0, 0), (RPB_PAD, RPB_PAD)))[:, :, ::-1]
    parts = []
    for l in range(DEPTH):
        parts.append(gated_parts(v["moe_w_gate"][l], v["moe_w_up"][l], v["moe_w_down"][l]))
        parts.append(gated_parts(v["sh_w_gate"][l], v["sh_w_up"][l], v["sh_w_down"][l]))
    a["experts"] = np.concatenate(parts)
    return a


def second_tables():
    t = {"averager": np.full((P, P), 1.0 / D)}
    k = np.arange(P)
    t["triangles"] = np.stack([k[:, None] <= k[None, :], k[:, None] > k[None, :]], 1)
    q, key = np.arange(LAT)[:, None], np.arange(LAT)[None, :]
    tables = []
    for window, dilation in ((128, 1), (512, 4), (2048, 16)):
        near = (q >= key) & (q - key <= window) & ((q - key) % dilation == 0)
        tables.append(np.where(near, q - key, -NEG))
    t["distances"] = np.stack(tables, 1).reshape(2, P, DIL_GROUPS, LAT).transpose(1, 0, 2, 3)
    return {name: np.ascontiguousarray(a, dtype=np.float32) for name, a in t.items()}


def columns(v):
    return np.moveaxis(v.reshape(*v.shape[:-1], -1, P), -1, 0)


def second_block_arrays(v):
    a = {}
    a["norm_g"], a["norm_g_cols"] = v["norm_g_2"], columns(v["norm_g_2"])
    parts = []
    for l in range(DEPTH):
        for f in range(2):
            w1 = v["ffn_w1_2"][l, f]
            half = w1.shape[-1] // 2
            parts.append(gated_parts(w1[:, :half], w1[:, half:], v["ffn_w2_2"][l, f]))
    a["ffn"] = np.concatenate(parts)
    w = v["hyb_w_in_2"][0]
    n = w.shape[-1] - SSM_HEADS
    a["hyb_w_in"], a["hyb_w_dt"] = chunks(w[:, :n]), chunks(w[:, n:], SSM_HEADS)
    a["hyb_w_out"] = chunks(v["hyb_w_out_2"][0])
    a["attn_w_qkv"], a["attn_w_o"] = chunks(v["attn_w_qkv_2"][0]), chunks(v["attn_w_o_2"][0])
    a["conv_taps"] = columns(v["conv_dw_w_2"][0]).transpose(0, 2, 1)
    a["conv_b_cols"] = columns(v["conv_dw_b_2"][0])
    a["conv_ln_g_cols"], a["conv_ln_b_cols"] = columns(v["conv_ln_g_2"][0]), columns(v["conv_ln_b_2"][0])
    a["ssm_taps"] = columns(v["ssm_conv_w_2"][0]).transpose(0, 2, 1)
    a["ssm_b_cols"] = columns(v["ssm_conv_b_2"][0])
    a["ssm_norm_g_cols"] = columns(v["ssm_norm_g_2"][0])
    a["ssm_dt_bias"], a["ssm_a_log"], a["ssm_d"] = v["ssm_dt_bias_2"][0], v["ssm_a_log_2"][0], v["ssm_d_2"][0]
    return a


def kernel(**inputs):
    import concourse.bacc as bacc
    from concourse.bass_utils import run_bass_kernel_spmd

    values = {name: np.asarray(a) for name, a in inputs.items()}
    arrays = {**shape_tables(), **second_tables(), **first_block_arrays(values), **second_block_arrays(values)}
    nc = bacc.Bacc("TRN2", target_bir_lowering=False, num_devices=1)
    aps = {}
    feeds = {}
    for name, a in arrays.items():
        feeds[f"in_{name}"] = np.ascontiguousarray(a)
        aps[name] = nc.dram_tensor(f"in_{name}", a.shape, mybir.dt.from_np(a.dtype), kind="ExternalInput").ap()
    out = nc.dram_tensor("out_rows", [LAT, D], F32, kind="ExternalOutput").ap()
    program(nc, aps, out)
    result = run_bass_kernel_spmd(nc, [feeds], core_ids=[0])
    return result.results[0]["out_rows"].reshape(1, LAT, D)
```

```python
import math
from contextlib import ExitStack

import numpy as np

import concourse.bass as bass
from concourse import mybir

F32 = mybir.dt.float32
F32R = mybir.dt.float32r
ALU = mybir.AluOpType
ACT = mybir.ActivationFunctionType
X_AXIS = mybir.AxisListType.X

P = 128
BANK = 512
NBANKS = 8
D = 1024
KD = D // P
LAT = 256
CTX = 256
TOK = LAT + CTX
DEPTH = 2
HEAD = 128
NEG = -1e30
DN_ALPHA = (2 * DEPTH) ** 0.25
EPS = 1e-6
N_EXPERTS = 64
TOP_K = 8
ROUTE_SCALE = 2.5
GRID_W = 64
GRID_ROWS = LAT // GRID_W
NA_HEADS = 8
NA_KH = 8
NA_KW = 16
RPB_PAD = GRID_W - NA_KW
RPB_W = 2 * NA_KW - 1 + 2 * RPB_PAD
FFN_PARTS = 11
CONV_TAPS = 31
SSM_TAPS = 4
SSM_HEADS = 16
SSM_P = 64
DIL_GROUPS = 3
DIL_HEADS = 8
DIL_DH = 64



class Chain:

    def __init__(self, eng, sem):
        self.eng, self.sem, self.count = eng, sem, 0

    def then(self, ins):
        self.count += 1
        ins.then_inc(self.sem, 1)
        self.eng.wait_ge(self.sem, self.count)


class Stage:

    def __init__(self, nc, name):
        self.nc, self.name, self.stack, self.sems = nc, name, ExitStack(), []

    def __enter__(self):
        self.stack.__enter__()
        return self

    def __exit__(self, *a):
        self.stack.__exit__(*a)
        if self.sems:
            self.nc.clear_and_free_semaphores(self.sems)
            self.nc.all_engine_barrier()

    def sbuf(self, name, shape, dtype=F32):
        return self.stack.enter_context(self.nc.sbuf_tensor(f"{self.name}_{name}", shape, dtype))

    def sem(self, name):
        self.sems.append(self.nc.alloc_semaphore(f"{self.name}_{name}"))
        return self.sems[-1]

    def block(self):
        return self.stack.enter_context(self.nc.Block())


def copy_on(nc, engine, out, in_):
    if engine == "v":
        return nc.vector.tensor_copy(out, in_)
    return nc.scalar.activation(out, in_, ACT.Copy)


def affine_on(nc, engine, out, in_, scale, shift):
    if engine == "v":
        return nc.vector.tensor_scalar(out, in_, scale, shift, ALU.mult, ALU.add)
    return nc.scalar.activation(out, in_, ACT.Identity, scale=scale, bias=shift)


def rows_of(vector, n=P):
    return vector.partition_broadcast(n)



def product_stage(nc, name, psum, weights, k_tiles, n_chunks, n_tiles, operands, drain, shape):
    with Stage(nc, name) as st:
        depth = min(3, n_chunks)
        width = max(w.shape[-1] for w in weights)
        wbuf = st.sbuf("w", [P, depth, width])
        loaded = [st.sem(f"loaded{i}") for i in range(depth)]
        products, v_drained, s_drained = st.sem("products"), st.sem("v_drained"), st.sem("s_drained")
        tiles = [(c, t) for c in range(n_chunks) for t in range(n_tiles(c))]
        last_of = {c: g for g, (c, t) in enumerate(tiles)}
        block = st.block()

        @block.sync
        def _(sp):
            for c in range(n_chunks):
                if c >= depth:
                    sp.wait_ge(products, last_of[c - depth] + 1)
                sp.dma_start(wbuf[:, c % depth, 0:weights[c].shape[-1]], weights[c]).then_inc(loaded[c % depth], 16)

        @block.tensor
        def _(pe):
            for g, (c, t) in enumerate(tiles):
                if t == 0:
                    pe.wait_ge(loaded[c % depth], 16 * (c // depth + 1))
                if g >= NBANKS:
                    pe.wait_ge(s_drained if g % 2 else v_drained, (g - NBANKS) // 2 + 1)
                m, n = shape(c, t)
                w = wbuf[:, c % depth, 0:weights[c].shape[-1]].rearrange("p (k n) -> p k n", k=k_tiles)
                for k in range(k_tiles):
                    lhs, rhs = operands(c, t, k, w)
                    last = nc.tensor.matmul(psum[0:m, g % NBANKS, 0:n], lhs, rhs, start=k == 0, stop=k == k_tiles - 1)
                last.then_inc(products, 1)

        @block.vector
        def _(dve):
            for g, (c, t) in enumerate(tiles):
                if g % 2 == 0:
                    dve.wait_ge(products, g + 1)
                    m, n = shape(c, t)
                    drain("v", c, t, psum[0:m, g % NBANKS, 0:n]).then_inc(v_drained, 1)

        @block.scalar
        def _(act):
            for g, (c, t) in enumerate(tiles):
                if g % 2 == 1:
                    act.wait_ge(products, g + 1)
                    m, n = shape(c, t)
                    drain("s", c, t, psum[0:m, g % NBANKS, 0:n]).then_inc(s_drained, 1)


def rows_product(nc, name, psum, cols, weights, k_tiles, tok_tiles, drain, k0=0):
    weights = [weights[c] for c in range(weights.shape[0])]
    product_stage(
        nc, name, psum, weights, k_tiles, len(weights), lambda c: tok_tiles,
        lambda c, t, k, w: (cols[:, k0 + k, t * P:(t + 1) * P], w[:, k, :]),
        drain, lambda c, t: (P, weights[c].shape[-1] // k_tiles))


def cols_product(nc, name, psum, cols, weights, tokens, drain):
    weights = [weights[c] for c in range(weights.shape[0])]
    product_stage(
        nc, name, psum, weights, KD, len(weights), lambda c: BANK // P,
        lambda c, t, k, w: (w[:, k, t * P:(t + 1) * P], cols[:, k, 0:tokens(c)]),
        drain, lambda c, t: (P, tokens(c)))



def transpose_stage(nc, name, psum, ident, n_groups, pieces, source, drain):
    with Stage(nc, name) as st:
        transposed, v_drained, s_drained = st.sem("transposed"), st.sem("v_drained"), st.sem("s_drained")
        block = st.block()

        @block.tensor
        def _(pe):
            for j in range(n_groups):
                if j >= NBANKS:
                    pe.wait_ge(s_drained if j % 2 else v_drained, (j - NBANKS) // 2 + 1)
                for i in range(pieces):
                    src = source(j, i)
                    m, n = src.shape
                    last = nc.tensor.transpose(psum[0:n, j % NBANKS, i * m:(i + 1) * m], src, ident[0:m, 0:m])
                last.then_inc(transposed, 1)

        @block.vector
        def _(dve):
            for j in range(0, n_groups, 2):
                dve.wait_ge(transposed, j + 1)
                drain("v", j, psum[:, j % NBANKS, :]).then_inc(v_drained, 1)

        @block.scalar
        def _(act):
            for j in range(1, n_groups, 2):
                act.wait_ge(transposed, j + 1)
                drain("s", j, psum[:, j % NBANKS, :]).then_inc(s_drained, 1)



def modulation_stage(nc, psum, ident, cvec, w_mod, b_mod, mod_dram, mod_cols):
    n_chunks = 6 * D // BANK
    for layer in range(DEPTH):
        with Stage(nc, f"mod{layer}") as st:
            depth = 3
            craw, cs = st.sbuf("craw", [P, KD, 2]), st.sbuf("cs", [P, KD, 2])
            bias, rows = st.sbuf("bias", [2, 6 * D]), st.sbuf("rows", [2, 6 * D])
            wbuf = st.sbuf("w", [P, depth, KD * BANK])
            loaded = [st.sem(f"loaded{i}") for i in range(depth)]
            small, activated, products, drained = st.sem("small"), st.sem("activated"), st.sem("products"), st.sem("drained")
            turned, turned_out, stored, shifted = st.sem("turned"), st.sem("turned_out"), st.sem("stored"), st.sem("shifted")
            block = st.block()

            @block.sync
            def _(sp):
                sp.dma_start(craw[:], cvec).then_inc(small, 16)
                sp.dma_start(bias[:], rows_of(b_mod[layer], 2)).then_inc(small, 16)
                for c in range(depth):
                    sp.dma_start(wbuf[:, c, :], w_mod[layer * n_chunks + c]).then_inc(loaded[c], 16)
                with sp.Fori(1, n_chunks // depth) as i:
                    for j in range(depth):
                        sp.wait_ge(products, depth * i + (j + 1 - depth))
                        sp.dma_start(wbuf[:, j, :], w_mod[depth * i + (layer * n_chunks + j)]).then_inc(loaded[j], 16)
                sp.wait_ge(drained, n_chunks)
                sp.dma_start(mod_dram[layer], rows[:]).then_inc(stored, 16)
                sp.wait_ge(stored, 16)

            @block.scalar
            def _(act):
                act.wait_ge(small, 32)
                nc.scalar.activation(cs[:], craw[:], ACT.Silu).then_inc(activated, 1)

            @block.tensor
            def _(pe):
                pe.wait_ge(activated, 1)
                with pe.Fori(0, n_chunks // depth) as i:
                    for j in range(depth):
                        pe.wait_ge(loaded[j], 16 * i + 16)
                        w = wbuf[:, j, :].rearrange("p (k n) -> p k n", k=KD)
                        for k in range(KD):
                            last = nc.tensor.matmul(psum[0:2, j, :], cs[:, k, :], w[:, k, :], start=k == 0, stop=k == KD - 1)
                        last.then_inc(products, 1)
                    pe.wait_ge(drained, depth * i + depth)
                for m in range(6 * KD):
                    last = nc.tensor.transpose(psum[:, 4, 2 * m:2 * m + 2], rows[:, m * P:(m + 1) * P], ident[0:2, 0:2])
                last.then_inc(turned, 1)

            @block.vector
            def _(dve):
                dve.wait_ge(small, 32)
                with dve.Fori(0, n_chunks // depth) as i:
                    for j in range(depth):
                        dve.wait_ge(products, depth * i + (j + 1))
                        at = bass.ds(i * (depth * BANK) + j * BANK, BANK)
                        nc.vector.tensor_tensor(rows[:, at], psum[0:2, j, :], bias[:, at], ALU.add).then_inc(drained, 1)
                dve.wait_ge(turned, 1)
                cols = mod_cols[:, layer, :, :]
                nc.vector.tensor_copy(cols, psum[:, 4, 0:12 * KD].rearrange("p (m r) -> p m r", r=2)).then_inc(turned_out, 1)
                dve.wait_ge(turned_out, 1)
                for kind in (1, 4):
                    at = cols[:, kind * KD:(kind + 1) * KD, :]
                    nc.vector.tensor_scalar(at, at, 1.0, None, ALU.add).then_inc(shifted, 1)



def residual_norm_stage(nc, name, x, y, tok_tiles, gate_lat, gate_ctx, gain, shift):
    with Stage(nc, name) as st:
        vec = st.sbuf("vec", [P, 4, D])
        stats, agg = st.sbuf("stats", [P, tok_tiles, 2, 6]), st.sbuf("agg", [P, tok_tiles, 2])
        std, rstd = st.sbuf("std", [P, tok_tiles]), st.sbuf("rstd", [P, tok_tiles])
        loaded, gated, summed, varied = st.sem("loaded"), st.sem("gated"), st.sem("summed"), st.sem("varied")
        rooted, scaled, chain_sem, shifted = st.sem("rooted"), st.sem("scaled"), st.sem("chain"), st.sem("shifted")
        block = st.block()

        @block.sync
        def _(sp):
            for i, v in enumerate((gate_lat, gate_ctx, gain, shift)):
                sp.dma_start(vec[:, i, :], rows_of(v)).then_inc(loaded, 16)

        @block.gpsimd
        def _(pool):
            pool.wait_ge(loaded, 64)
            for t in range(tok_tiles):
                nc.gpsimd.tensor_tensor(y[:, t, :], y[:, t, :], vec[:, 0 if t < 2 else 1, :], ALU.mult).then_inc(gated, 1)
            for t in range(tok_tiles):
                pool.wait_ge(scaled, t + 1)
                nc.gpsimd.tensor_tensor(x[:, t, :], x[:, t, :], vec[:, 3, :], ALU.add).then_inc(shifted, 1)

        @block.scalar
        def _(act):
            for t in range(tok_tiles):
                act.wait_ge(varied, t + 1)
                nc.scalar.activation(std[:, t:t + 1], agg[:, t, 1:2], ACT.Sqrt).then_inc(rooted, 1)

        @block.vector
        def _(dve):
            chain = Chain(dve, chain_sem)
            for t in range(tok_tiles):
                dve.wait_ge(gated, t + 1)
                chain.then(nc.vector.scalar_tensor_tensor(x[:, t, :], x[:, t, :], DN_ALPHA, y[:, t, :], ALU.mult, ALU.add))
                nc.vector.bn_stats(stats[:, t, 0, :], x[:, t, 0:BANK])
                chain.then(nc.vector.bn_stats(stats[:, t, 1, :], x[:, t, BANK:D]))
                chain.then(nc.vector.bn_aggr(agg[:, t, :], stats[:, t, :, :]))
                nc.vector.tensor_scalar(agg[:, t, 1:2], agg[:, t, 1:2], EPS, None, ALU.add).then_inc(varied, 1)
            dve.wait_ge(loaded, 64)
            for t in range(tok_tiles):
                dve.wait_ge(rooted, t + 1)
                chain.then(nc.vector.reciprocal(rstd[:, t:t + 1], std[:, t:t + 1]))
                chain.then(nc.vector.tensor_scalar(x[:, t, :], x[:, t, :], agg[:, t, 0:1], rstd[:, t:t + 1], ALU.subtract, ALU.mult))
                nc.vector.tensor_tensor(x[:, t, :], x[:, t, :], vec[:, 2, :], ALU.mult).then_inc(scaled, 1)



def modulated_cols(nc, name, psum, ident, x, cols, mod_cols, layer, scale_kind, tok_tiles):
    shift_kind = scale_kind - 1

    def drain(engine, j, bank):
        for row in range(tok_tiles // 2):
            at = slice(row * LAT, (row + 1) * LAT)
            last = affine_on(nc, engine, cols[:, j, at], bank[:, at],
                             mod_cols[:, layer, scale_kind * KD + j, row:row + 1],
                             mod_cols[:, layer, shift_kind * KD + j, row:row + 1])
        return last

    transpose_stage(nc, name, psum, ident, KD, tok_tiles, lambda j, i: x[:, i, j * P:(j + 1) * P], drain)



def attention_stage(nc, name, psum, ident, units, score_parts, n_keys, bias, scale, values, out, dh, idle_fill=None):
    n = len(units)
    widest = max(n_keys(u) for u in units)
    with Stage(nc, name) as st:
        biased = st.sbuf("biased", [P, 2, widest])
        probs = st.sbuf("probs", [P, 2, widest])
        probs_t = st.sbuf("probs_t", [P, 2, widest])
        peak, neg_peak = st.sbuf("peak", [P, n]), st.sbuf("neg_peak", [P, n])
        total, inv_total = st.sbuf("total", [P, n]), st.sbuf("inv_total", [P, n])
        scores_ready, peak_ready, probs_ready = st.sem("scores_ready"), st.sem("peak_ready"), st.sem("probs_ready")
        turned, turned_out, outs_ready, outs_used = st.sem("turned"), st.sem("turned_out"), st.sem("outs_ready"), st.sem("outs_used")
        chain_sem = st.sem("chain")
        block = st.block()

        if idle_fill is not None:
            zeros, filled, cleared = st.sbuf("zeros", [P, D]), st.sem("filled"), st.sem("cleared")

            @block.gpsimd
            def _(pool):
                nc.gpsimd.memset(zeros[:], 0.0).then_inc(cleared, 1)

            @block.sync
            def _(sp):
                sp.wait_ge(cleared, 1)
                fills = idle_fill.shape[0] // P
                for b in range(fills):
                    sp.dma_start(idle_fill[b * P:(b + 1) * P, :], zeros[:]).then_inc(filled, 16)
                sp.wait_ge(filled, 16 * fills)

        def scores(u):
            return psum[:, 2 * (u % 2):2 * (u % 2) + 2, :].rearrange("p b n -> p (b n)")

        turned_ps = psum[:, 4:6, :].rearrange("p b n -> p (b n)")
        has_bias = bool(bias(units[0]))
        exp_scale = 1.0 if has_bias and bias(units[0])[0][2] is None else scale

        def exp_source(u):
            return biased[:, u % 2, 0:n_keys(units[u])] if has_bias else scores(u)[:, 0:n_keys(units[u])]

        @block.tensor
        def _(pe):
            for step in range(n + 2):
                if step < n:
                    u = step
                    if u >= 2:
                        pe.wait_ge(probs_ready, u - 1)
                    for col, lhs, rhs in score_parts(units[u]):
                        last = nc.tensor.matmul(scores(u)[:, col:col + rhs.shape[-1]], lhs, rhs, start=True, stop=True)
                    last.then_inc(scores_ready, 1)
                if 0 <= step - 1 < n:
                    u = step - 1
                    pe.wait_ge(probs_ready, u + 1)
                    if u >= 1:
                        pe.wait_ge(turned_out, u)
                    for c in range(n_keys(units[u]) // P):
                        last = nc.tensor.transpose(turned_ps[:, c * P:(c + 1) * P], probs[:, u % 2, c * P:(c + 1) * P], ident[:])
                    last.then_inc(turned, 1)
                if 0 <= step - 2 < n:
                    u = step - 2
                    pe.wait_ge(turned_out, u + 1)
                    if u >= 2:
                        pe.wait_ge(outs_used, u - 1)
                    vs = values(units[u])
                    for c, v in enumerate(vs):
                        last = nc.tensor.matmul(psum[:, 6 + u % 2, 0:dh], probs_t[:, u % 2, c * P:(c + 1) * P], v,
                                                start=c == 0, stop=c == len(vs) - 1)
                    last.then_inc(outs_ready, 1)

        @block.vector
        def _(dve):
            chain = Chain(dve, chain_sem)
            for step in range(n + 2):
                if step < n:
                    u = step
                    dve.wait_ge(scores_ready, u + 1)
                    if has_bias:
                        if u >= 2:
                            dve.wait_ge(probs_ready, u - 1)
                        for at, table, factor in bias(units[u]):
                            if table is None:
                                ins = nc.vector.tensor_scalar(biased[:, u % 2, at], scores(u)[:, at], scale, None, ALU.mult)
                            elif factor is None:
                                ins = nc.vector.scalar_tensor_tensor(biased[:, u % 2, at], scores(u)[:, at], scale, table, ALU.mult, ALU.add)
                            else:
                                ins = nc.vector.scalar_tensor_tensor(biased[:, u % 2, at], table, factor, scores(u)[:, at], ALU.mult, ALU.add)
                        chain.then(ins)
                    chain.then(nc.vector.reduce_max(peak[:, u:u + 1], exp_source(u), X_AXIS))
                    nc.vector.tensor_scalar(neg_peak[:, u:u + 1], peak[:, u:u + 1], -exp_scale, None, ALU.mult).then_inc(peak_ready, 1)
                if 0 <= step - 2 < n:
                    u = step - 2
                    dve.wait_ge(outs_ready, u + 1)
                    chain.then(nc.vector.reciprocal(inv_total[:, u:u + 1], total[:, u:u + 1]))
                    nc.vector.tensor_scalar(out(units[u]), psum[:, 6 + u % 2, 0:dh], inv_total[:, u:u + 1], None, ALU.mult).then_inc(outs_used, 1)

        @block.scalar
        def _(act):
            for step in range(n + 1):
                if step < n:
                    u = step
                    act.wait_ge(peak_ready, u + 1)
                    if u >= 2:
                        act.wait_ge(turned, u - 1)
                    nc.scalar.activation(probs[:, u % 2, 0:n_keys(units[u])], exp_source(u), ACT.Exp,
                                         bias=neg_peak[:, u:u + 1], scale=exp_scale,
                                         accum_out=total[:, u:u + 1]).then_inc(probs_ready, 1)
                if step >= 1:
                    u = step - 1
                    act.wait_ge(turned, u + 1)
                    if u >= 2:
                        act.wait_ge(outs_ready, u - 1)
                    nc.scalar.activation(probs_t[:, u % 2, 0:n_keys(units[u])], turned_ps[:, 0:n_keys(units[u])],
                                         ACT.Copy).then_inc(turned_out, 1)



def resident_product_stage(nc, name, psum, tiles, drain):
    with Stage(nc, name) as st:
        products, v_drained, s_drained = st.sem("products"), st.sem("v_drained"), st.sem("s_drained")
        block = st.block()

        @block.tensor
        def _(pe):
            for g, (m, n, terms) in enumerate(tiles):
                if g >= NBANKS:
                    pe.wait_ge(s_drained if g % 2 else v_drained, (g - NBANKS) // 2 + 1)
                for k, (lhs, rhs) in enumerate(terms):
                    last = nc.tensor.matmul(psum[0:m, g % NBANKS, 0:n], lhs, rhs, start=k == 0, stop=k == len(terms) - 1)
                last.then_inc(products, 1)

        @block.vector
        def _(dve):
            for g in range(0, len(tiles), 2):
                dve.wait_ge(products, g + 1)
                drain("v", g, psum[0:tiles[g][0], g % NBANKS, 0:tiles[g][1]]).then_inc(v_drained, 1)

        @block.scalar
        def _(act):
            for g in range(1, len(tiles), 2):
                act.wait_ge(products, g + 1)
                drain("s", g, psum[0:tiles[g][0], g % NBANKS, 0:tiles[g][1]]).then_inc(s_drained, 1)



def norm_rope_stage(nc, proj, gains, rope):
    heads = 8
    with Stage(nc, "norm_rope") as st:
        gain, table = st.sbuf("gain", [P, heads, HEAD]), st.sbuf("table", [P, 2, 2, HEAD])
        square, turned = st.sbuf("square", [P, heads, HEAD]), st.sbuf("turned", [P, heads, HEAD])
        ss, std, rstd = st.sbuf("ss", [P, 4, heads]), st.sbuf("std", [P, 4, heads]), st.sbuf("rstd", [P, 4, heads])
        loaded, squared, summed, rooted, chain_sem = st.sem("loaded"), st.sem("squared"), st.sem("summed"), st.sem("rooted"), st.sem("chain")
        block = st.block()

        def qk(t):
            return proj[:, t, LAT:LAT + heads * HEAD].rearrange("p (h d) -> p h d", d=HEAD)

        @block.sync
        def _(sp):
            sp.dma_start(gain[:], rows_of(gains).rearrange("p (h d) -> p h d", d=HEAD)).then_inc(loaded, 16)
            sp.dma_start(table[:], rope).then_inc(loaded, 16)

        @block.gpsimd
        def _(pool):
            for t in range(4):
                if t >= 1:
                    pool.wait_ge(summed, t)
                nc.gpsimd.tensor_tensor(square[:], qk(t), qk(t), ALU.mult).then_inc(squared, 1)

        @block.scalar
        def _(act):
            for t in range(4):
                act.wait_ge(summed, t + 1)
                nc.scalar.activation(std[:, t, :], ss[:, t, :], ACT.Sqrt).then_inc(rooted, 1)

        @block.vector
        def _(dve):
            chain = Chain(dve, chain_sem)
            for t in range(4):
                dve.wait_ge(squared, t + 1)
                chain.then(nc.vector.reduce_sum(ss[:, t, :], square[:], X_AXIS))
                nc.vector.tensor_scalar(ss[:, t, :], ss[:, t, :], 1.0 / HEAD, EPS, ALU.mult, ALU.add).then_inc(summed, 1)
            dve.wait_ge(loaded, 32)
            for t in range(4):
                dve.wait_ge(rooted, t + 1)
                chain.then(nc.vector.reciprocal(rstd[:, t, :], std[:, t, :]))
                chain.then(nc.vector.tensor_tensor(qk(t), qk(t), rstd[:, t, :].unsqueeze(2).to_broadcast([P, heads, HEAD]), ALU.mult))
                chain.then(nc.vector.tensor_tensor(qk(t), qk(t), gain[:], ALU.mult))
                if t < 2:
                    for half in range(2):
                        for part in range(2):
                            to = slice(half * 64 + part * 32, half * 64 + part * 32 + 32)
                            of = slice(half * 64 + (1 - part) * 32, half * 64 + (1 - part) * 32 + 32)
                            sin = table[:, t, 1, to].unsqueeze(1).to_broadcast([P, heads, 32])
                            ins = nc.vector.tensor_tensor(turned[:, :, to], qk(t)[:, :, of], sin, ALU.mult)
                    chain.then(ins)
                    cos = table[:, t, 0, :].unsqueeze(1).to_broadcast([P, heads, HEAD])
                    chain.then(nc.vector.tensor_tensor(qk(t), qk(t), cos, ALU.mult))
                    chain.then(nc.vector.tensor_tensor(qk(t), qk(t), turned[:], ALU.add))



def fourier_stages(nc, psum, proj, cat, w_fnet, dft_tokens, dft_channels):
    with Stage(nc, "fourier_tables") as st:
        tok = st.sbuf("tok", [P, 2, 2, LAT])
        chan = st.sbuf("chan", [P, 2, P])
        mix = st.sbuf("mix", [P, 2, P])
        half = st.sbuf("half", [P, 2, 2, TOK])
        spectrum = st.sbuf("spectrum", [P, 2, TOK])
        loaded, cleared = st.sem("loaded"), st.sem("cleared")
        with nc.Block() as block:
            @block.gpsimd
            def _(pool):
                nc.gpsimd.memset(mix[:], 0.0).then_inc(cleared, 1)

            @block.sync
            def _(sp):
                sp.dma_start(tok[:], dft_tokens).then_inc(loaded, 16)
                sp.dma_start(chan[:], dft_channels).then_inc(loaded, 16)
                sp.wait_ge(cleared, 1)
                for g in range(4):
                    at = slice((g % 2) * 64, (g % 2) * 64 + 64)
                    sp.dma_start(mix[at, g // 2, at], w_fnet[g]).then_inc(loaded, 16)
                sp.wait_ge(loaded, 96)

        tiles = []
        for side in range(2):
            for m in range(2):
                for part in range(2):
                    tiles.append((side, m, part))
        resident_product_stage(
            nc, "fourier_tokens", psum,
            [(P, LAT, [(proj[:, 2 * side + t, m * P:(m + 1) * P], tok[:, t, part, :]) for t in range(2)])
             for side, m, part in tiles],
            lambda engine, g, bank: copy_on(nc, engine, half[:, tiles[g][2], tiles[g][1], tiles[g][0] * LAT:(tiles[g][0] + 1) * LAT], bank))
        resident_product_stage(
            nc, "fourier_channels", psum,
            [(P, TOK, [(chan[:, part, :], half[:, part, m, :]) for part in range(2)]) for m in range(2)],
            lambda engine, g, bank: copy_on(nc, engine, spectrum[:, g, :], bank))
        resident_product_stage(
            nc, "fourier_mix", psum,
            [(P, TOK, [(mix[:, m, :], spectrum[:, m, :])]) for m in range(2)],
            lambda engine, g, bank: copy_on(nc, engine, cat[:, g, :], bank))



class Routing:

    def __init__(self, st, tok_tiles):
        self.tok_tiles = tok_tiles
        self.spare = tok_tiles * P * TOP_K // P - 1
        shape = [P, tok_tiles, N_EXPERTS]
        self.weight, self.slot, self.spare_slot = st.sbuf("weight", shape), st.sbuf("slot", shape), st.sbuf("spare_slot", shape)
        self.result_rows = st.sbuf("result_rows", [P, tok_tiles, 8], mybir.dt.uint32)
        self.spare_expert = st.sbuf("spare_expert", [P, self.spare], mybir.dt.uint32)
        self.n_spare = st.sbuf("n_spare", [P, 1], mybir.dt.uint32)


def router_stage(nc, name, psum, cols, w_router, e_bias, tables, routing):
    tok_tiles, spare = routing.tok_tiles, routing.spare
    with Stage(nc, name) as st:
        shape = [P, tok_tiles, N_EXPERTS]
        w, bias = st.sbuf("w", [P, KD, N_EXPERTS]), st.sbuf("bias", [P, N_EXPERTS])
        before, every = st.sbuf("before", [P, P]), st.sbuf("every", [P, P])
        first_row, count_to = st.sbuf("first_row", [P, N_EXPERTS]), st.sbuf("count_to", [P, 32])
        scores, ranked, chosen = st.sbuf("scores", shape), st.sbuf("ranked", shape), st.sbuf("chosen", shape)
        top, total, inv = st.sbuf("top", [P, tok_tiles, 8]), st.sbuf("total", [P, tok_tiles]), st.sbuf("inv", [P, tok_tiles])
        rank, part, rest, row, later = (st.sbuf(n, shape) for n in ("rank", "part", "rest", "row", "later"))
        count, more, upto, base = (st.sbuf(n, [P, N_EXPERTS]) for n in ("count", "more", "upto", "base"))
        passed, owner = st.sbuf("passed", [P, spare, N_EXPERTS]), st.sbuf("owner", [P, spare])
        loaded, products, squashed, chosen_ready, ranks_ready, chain_sem = (
            st.sem(n) for n in ("loaded", "products", "squashed", "chosen_ready", "ranks_ready", "chain"))
        block = st.block()

        @block.sync
        def _(sp):
            sp.dma_start(w[:], w_router.rearrange("(k p) e -> p k e", p=P)).then_inc(loaded, 16)
            sp.dma_start(bias[:], rows_of(e_bias)).then_inc(loaded, 16)
            sp.dma_start(before[:], tables["before"]).then_inc(loaded, 16)
            sp.dma_start(every[:], tables["every"]).then_inc(loaded, 16)
            sp.dma_start(first_row[:], rows_of(tables["first_row"])).then_inc(loaded, 16)
            sp.dma_start(count_to[:], rows_of(tables["count_to"])).then_inc(loaded, 16)

        @block.tensor
        def _(pe):
            pe.wait_ge(loaded, 96)
            for t in range(tok_tiles):
                for k in range(KD):
                    last = nc.tensor.matmul(psum[:, t, 0:N_EXPERTS], cols[:, k, t * P:(t + 1) * P], w[:, k, :], start=k == 0, stop=k == KD - 1)
                last.then_inc(products, 1)
            pe.wait_ge(chosen_ready, 1)
            for t in range(tok_tiles):
                for t0 in range(t + 1):
                    nc.tensor.matmul(psum[:, 4, t * N_EXPERTS:(t + 1) * N_EXPERTS], before[:] if t0 == t else every[:], chosen[:, t0, :],
                                     start=t0 == 0, stop=t0 == t)
            for t in range(tok_tiles):
                last = nc.tensor.matmul(psum[:, 5, 0:N_EXPERTS], every[:], chosen[:, t, :], start=t == 0, stop=t == tok_tiles - 1)
            last.then_inc(ranks_ready, 1)

        @block.scalar
        def _(act):
            for t in range(tok_tiles):
                act.wait_ge(products, t + 1)
                nc.scalar.activation(scores[:, t, :], psum[:, t, 0:N_EXPERTS], ACT.Sigmoid).then_inc(squashed, 1)

        @block.vector
        def _(dve):
            v, chain = nc.vector, Chain(dve, chain_sem)
            then = chain.then

            def over_tokens(a):
                return a[:].unsqueeze(1).to_broadcast(shape)

            dve.wait_ge(loaded, 96)
            for t in range(tok_tiles):
                dve.wait_ge(squashed, t + 1)
                then(v.tensor_tensor(ranked[:, t, :], scores[:, t, :], bias[:], ALU.add))
                then(v.max(top[:, t, :], ranked[:, t, :]))
                then(v.match_replace(chosen[:, t, :], top[:, t, :], ranked[:, t, :], NEG))
            chosen_ins = v.tensor_tensor(chosen[:], chosen[:], ranked[:], ALU.not_equal)
            chosen_ins.then_inc(chosen_ready, 1)
            dve.wait_ge(chosen_ready, 1)
            then(v.tensor_tensor(scores[:], chosen[:], scores[:], ALU.mult))
            then(v.reduce_sum(total[:], scores[:], X_AXIS))
            then(v.reciprocal(inv[:], total[:]))
            then(v.tensor_scalar(inv[:], inv[:], ROUTE_SCALE, None, ALU.mult))
            then(v.tensor_tensor(routing.weight[:], scores[:], inv[:].unsqueeze(2).to_broadcast(shape), ALU.mult))
            dve.wait_ge(ranks_ready, 1)
            v.tensor_copy(rank[:].rearrange("p t e -> p (t e)"), psum[:, 4, 0:tok_tiles * N_EXPERTS])
            then(v.tensor_copy(count[:], psum[:, 5, 0:N_EXPERTS]))
            then(v.tensor_scalar(more[:], count[:], float(P), None, ALU.is_gt))
            then(v.tensor_scalar(part[:], rank[:], float(P), None, ALU.is_ge))
            for j in range(2, tok_tiles):
                v.scalar_tensor_tensor(more[:], count[:], float(j * P), more[:], ALU.is_gt, ALU.add)
                then(v.scalar_tensor_tensor(part[:], rank[:], float(j * P), part[:], ALU.is_ge, ALU.add))
            then(v.tensor_tensor_scan(upto[:], every[:, 0:N_EXPERTS], more[:], 0.0, ALU.mult, ALU.add))
            then(v.tensor_tensor(base[:], upto[:], more[:], ALU.subtract))
            then(v.scalar_tensor_tensor(rest[:], part[:], -float(P), rank[:], ALU.mult, ALU.add))
            then(v.tensor_tensor(later[:], part[:], over_tokens(base), ALU.add))
            then(v.tensor_scalar(later[:], later[:], float(P), -float(P), ALU.mult, ALU.add))
            then(v.tensor_tensor(later[:], later[:], rest[:], ALU.add))
            then(v.tensor_scalar(part[:], part[:], 1.0, None, ALU.min))
            then(v.tensor_tensor(row[:], rest[:], over_tokens(first_row), ALU.add))
            then(v.scalar_tensor_tensor(rank[:], later[:], float(P * N_EXPERTS), row[:], ALU.add, ALU.subtract))
            then(v.tensor_tensor(rank[:], rank[:], part[:], ALU.mult))
            then(v.tensor_tensor(row[:], row[:], rank[:], ALU.add))
            then(v.scalar_tensor_tensor(row[:], row[:], 1.0, chosen[:], ALU.add, ALU.mult))
            for t in range(tok_tiles):
                then(v.max(top[:, t, :], row[:, t, :]))
            then(v.tensor_scalar(routing.result_rows[:], top[:], -1.0, None, ALU.add))
            then(v.tensor_tensor(part[:], part[:], chosen[:], ALU.mult))
            then(v.scalar_tensor_tensor(later[:], later[:], 1.0, part[:], ALU.add, ALU.mult))
            then(v.tensor_scalar(routing.spare_slot[:], later[:], -1.0, None, ALU.add))
            then(v.tensor_tensor(chosen[:], chosen[:], part[:], ALU.subtract))
            then(v.scalar_tensor_tensor(rest[:], rest[:], 1.0, chosen[:], ALU.add, ALU.mult))
            then(v.tensor_scalar(routing.slot[:], rest[:], -1.0, None, ALU.add))
            then(v.tensor_tensor(passed[:], count_to[:, 0:spare].unsqueeze(2).to_broadcast([P, spare, N_EXPERTS]),
                                 upto[:].unsqueeze(1).to_broadcast([P, spare, N_EXPERTS]), ALU.is_ge))
            then(v.reduce_sum(owner[:], passed[:], X_AXIS))
            then(v.tensor_scalar(routing.spare_expert[:], owner[:], float(N_EXPERTS - 1), None, ALU.min))
            then(v.tensor_copy(routing.n_spare[:], upto[:, N_EXPERTS - 1:N_EXPERTS]))


def token_rows_stage(nc, name, x, h, scale_shift, h_dram, tok_tiles):
    with Stage(nc, name) as st:
        vec = st.sbuf("vec", [P, 4, D])
        loaded, scaled, shifted, stored = st.sem("loaded"), st.sem("scaled"), st.sem("shifted"), st.sem("stored")
        block = st.block()

        @block.sync
        def _(sp):
            for i, v in enumerate(scale_shift):
                sp.dma_start(vec[:, i, :], rows_of(v)).then_inc(loaded, 16)
            for t in range(tok_tiles):
                sp.wait_ge(shifted, t + 1)
                sp.dma_start(h_dram[t * P:(t + 1) * P, :], h[:, t, :]).then_inc(stored, 16)
            sp.wait_ge(stored, 16 * tok_tiles)

        @block.vector
        def _(dve):
            dve.wait_ge(loaded, 16 * len(scale_shift))
            for t in range(tok_tiles):
                nc.vector.scalar_tensor_tensor(h[:, t, :], vec[:, 2 * (t // 2), :], 1.0, x[:, t, :], ALU.add, ALU.mult).then_inc(scaled, 1)

        @block.gpsimd
        def _(pool):
            for t in range(tok_tiles):
                pool.wait_ge(scaled, t + 1)
                nc.gpsimd.tensor_tensor(h[:, t, :], h[:, t, :], vec[:, 2 * (t // 2) + 1, :], ALU.add).then_inc(shifted, 1)


def experts_stage(nc, name, psum, ident, weights, first, h_dram, tables, routing, results):
    tok_tiles = routing.tok_tiles
    ring = 4
    n = N_EXPERTS
    with Stage(nc, name) as st:
        wbuf = st.sbuf("w", [P, ring, 6 * D])
        slots, tokens = st.sbuf("slots", [P, P]), st.sbuf("tokens", [P, tok_tiles])
        match = st.sbuf("match", [P, 2, tok_tiles, P])
        pairs = st.sbuf("pairs", [P, 2, tok_tiles, 2])
        who = st.sbuf("who", [P, ring, 1], mybir.dt.uint32)
        share = st.sbuf("share", [P, N_EXPERTS])
        x_rows = st.sbuf("x_rows", [P, ring, D])
        x_cols = st.sbuf("x_cols", [P, 2, KD, P])
        silu, gated = st.sbuf("silu", [P, 256]), st.sbuf("gated", [P, 256])
        gated_t = st.sbuf("gated_t", [P, 2, P])
        y = st.sbuf("y", [P, ring, D])
        mark, marked = st.sbuf("mark", [P, 2]), st.sem("marked")
        up_loaded = [st.sem(f"up_loaded{i}") for i in range(ring)]
        down_loaded = [st.sem(f"down_loaded{i}") for i in range(ring)]
        small, matched, found, found_out = (st.sem(k) for k in ("small", "matched", "found", "found_out"))
        gathers = [st.sem(f"gathered{i}") for i in range(ring)]
        turned, turned_out, ups, silus, gates = (st.sem(k) for k in ("turned", "turned_out", "ups", "silus", "gates"))
        gates_turned, gates_out, downs, y_low, y_high = (st.sem(k) for k in ("gates_turned", "gates_out", "downs", "y_low", "y_high"))
        stored = [st.sem(f"stored{i}") for i in range(ring)]
        block = st.block()
        FIND, TURN, GATE_T, UP, DOWN = 0, 1, 3, 4, 6
        ahead = 5
        gate_up = [wbuf[:, s, 0:4 * D].rearrange("p (k n) -> p k n", k=KD) for s in range(ring)]
        down = [wbuf[:, s, 4 * D:6 * D].rearrange("p (m n) -> p m n", m=2) for s in range(ring)]

        def wait(eng, sem, value):
            if not isinstance(value, int) or value > 0:
                eng.wait_ge(sem, value)

        def steps(eng, step):
            for e in range(ring):
                step(e, e, e)
            with eng.Fori(1, n // ring - 2) as i:
                for j in range(ring):
                    step(ring * i + j, j, None)
            for e in range(n - 2 * ring, n):
                step(e, e % ring, e)

        @block.sync
        def _(sp):
            sp.dma_start(slots[:], rows_of(tables["slots"])).then_inc(small, 16)
            sp.dma_start(tokens[:], tables["token_ids"][:, 0:tok_tiles]).then_inc(small, 16)

            def step(e, j, known):
                wait(sp, ups, e - ring + 1)
                sp.dma_start(wbuf[:, j, 0:4 * D], weights[e + first][:, 0:4 * D]).then_inc(up_loaded[j], 16)
                wait(sp, downs, e - ring + 1)
                sp.dma_start(wbuf[:, j, 4 * D:6 * D], weights[e + first][:, 4 * D:6 * D]).then_inc(down_loaded[j], 16)
            steps(sp, step)

        @block.tensor
        def _(pe):
            def find(e, j):
                pe.wait_ge(matched, e + 1)
                wait(pe, found_out, e)
                for t in range(tok_tiles):
                    last = nc.tensor.matmul(psum[:, FIND, 0:2], match[:, j % 2, t, :], pairs[:, j % 2, t, :], start=t == 0, stop=t == tok_tiles - 1)
                last.then_inc(found, 1)

            def turn(e, j, rounds):
                pe.wait_ge(gathers[j], rounds * 16)
                wait(pe, turned_out, 2 * e)
                for k in range(KD):
                    last = nc.tensor.transpose(psum[:, TURN + k // 4, (k % 4) * P:(k % 4 + 1) * P], x_rows[:, j, k * P:(k + 1) * P], ident[:])
                last.then_inc(turned, 1)

            def up(e, j, rounds):
                pe.wait_ge(up_loaded[j], rounds * 16)
                pe.wait_ge(turned_out, 2 * e + 2)
                wait(pe, gates, e - 1)
                for k in range(KD):
                    last = nc.tensor.matmul(psum[:, UP + j % 2, :], x_cols[:, j % 2, k, :], gate_up[j][:, k, :], start=k == 0, stop=k == KD - 1)
                last.then_inc(ups, 1)

            def turn_gates(e, j):
                pe.wait_ge(gates, e + 1)
                wait(pe, gates_out, e)
                for m in range(2):
                    last = nc.tensor.transpose(psum[:, GATE_T, m * P:(m + 1) * P], gated[:, m * P:(m + 1) * P], ident[:])
                last.then_inc(gates_turned, 1)

            def down_product(e, j, rounds):
                pe.wait_ge(down_loaded[j], rounds * 16)
                pe.wait_ge(gates_out, e + 1)
                for half in range(2):
                    wait(pe, y_high if half else y_low, e)
                    for m in range(2):
                        last = nc.tensor.matmul(psum[:, DOWN + half, :], gated_t[:, m, :], down[j][:, m, half * BANK:(half + 1) * BANK], start=m == 0, stop=m == 1)
                last.then_inc(downs, 1)

            pe.wait_ge(small, 32)
            for e in range(ahead):
                find(e, e % ring)
            turn(0, 0, 1)
            turn(1, 1, 1)
            up(0, 0, 1)

            def step(e, j, known, i=None):
                rounds = (lambda a: (known + a) // ring + 1) if known is not None else (lambda a: i + (1 + (j + a) // ring))
                if known is None or known + ahead < n:
                    find(e + ahead, (j + ahead) % ring)
                if known is None or known + 2 < n:
                    turn(e + 2, (j + 2) % ring, rounds(2))
                turn_gates(e, j)
                if known is None or known + 1 < n:
                    up(e + 1, (j + 1) % ring, rounds(1))
                down_product(e, j, rounds(0))

            for e in range(ring):
                step(e, e, e)
            with pe.Fori(1, n // ring - 2) as i:
                for j in range(ring):
                    step(ring * i + j, j, None, i)
            for e in range(n - 2 * ring, n):
                step(e, e % ring, e)

        @block.gpsimd
        def _(pool):
            nc.gpsimd.memset(mark[:], 0.0).then_inc(marked, 1)

            def step(e, j, known):
                pool.wait_ge(found_out, e + 1)
                wait(pool, turned, e - ring + 1)
                pool.wait_ge(marked, e + 1)
                nc.gpsimd.tensor_tensor(mark[0:1, 1:2], mark[0:1, 0:1], mark[0:1, 0:1], ALU.add).then_inc(marked, 1)
                nc.gpsimd.indirect_dma_start(out=x_rows[:, j, :], out_offset=None, in_=h_dram,
                                             in_offset=bass.IndirectOffsetOnAxis(ap=who[:, j, :], axis=0)).then_inc(gathers[j], 16)
            steps(pool, step)

        @block.scalar
        def _(act):
            def copy_turned(e, j):
                act.wait_ge(turned, e + 1)
                wait(act, ups, e - 1)
                for half in range(2):
                    nc.scalar.activation(x_cols[:, j % 2, 4 * half:4 * half + 4, :], psum[:, TURN + half, :].rearrange("p (k n) -> p k n", n=P),
                                         ACT.Copy).then_inc(turned_out, 1)

            def silu_of(e, j):
                act.wait_ge(ups, e + 1)
                wait(act, gates, e)
                nc.scalar.activation(silu[:], psum[:, UP + j % 2, 0:256], ACT.Silu).then_inc(silus, 1)

            def weigh_low(e, j, rounds):
                act.wait_ge(downs, e + 1)
                wait(act, stored[j], rounds * 16)
                nc.scalar.activation(y[:, j, 0:BANK], psum[:, DOWN, :], ACT.Copy, scale=share[:, bass.ds(e, 1)]).then_inc(y_low, 1)
                act.wait_ge(y_low, e + 1)
                act.wait_ge(y_high, e + 1)
                act.dma_start(results[bass.ds(e * P, P), :], y[:, j, :]).then_inc(stored[j], 16)

            copy_turned(0, 0)
            copy_turned(1, 1)
            silu_of(0, 0)

            def step(e, j, known, i=None):
                rounds = known // ring if known is not None else i
                if known is None or known + 2 < n:
                    copy_turned(e + 2, (j + 2) % ring)
                if known is None or known + 1 < n:
                    silu_of(e + 1, (j + 1) % ring)
                weigh_low(e, j, rounds)

            for e in range(ring):
                step(e, e, e)
            with act.Fori(1, n // ring - 2) as i:
                for j in range(ring):
                    step(ring * i + j, j, None, i)
            for e in range(n - 2 * ring, n):
                step(e, e % ring, e)
            for j in range(ring):
                act.wait_ge(stored[j], 16 * (n // ring))

        @block.vector
        def _(dve):
            def match_of(e, j):
                wait(dve, found, e - 1)
                at = bass.ds(e, 1)
                nc.vector.tensor_tensor(match[:, j % 2, :, :], slots[:].unsqueeze(1).to_broadcast([P, tok_tiles, P]),
                                        routing.slot[:, :, at].to_broadcast([P, tok_tiles, P]), ALU.is_equal)
                nc.vector.tensor_copy(pairs[:, j % 2, :, 0:1], tokens[:].unsqueeze(2))
                nc.vector.tensor_copy(pairs[:, j % 2, :, 1:2], routing.weight[:, :, at]).then_inc(matched, 1)

            def found_of(e, j):
                dve.wait_ge(found, e + 1)
                wait(dve, turned, e - ring + 1)
                nc.vector.tensor_copy(share[:, bass.ds(e, 1)], psum[:, FIND, 1:2])
                nc.vector.tensor_copy(who[:, j, :], psum[:, FIND, 0:1]).then_inc(found_out, 1)

            def gate_of(e, j):
                dve.wait_ge(silus, e + 1)
                wait(dve, gates_turned, e)
                nc.vector.tensor_tensor(gated[:], silu[:], psum[:, UP + j % 2, 256:BANK], ALU.mult).then_inc(gates, 1)

            def copy_gates(e, j):
                dve.wait_ge(gates_turned, e + 1)
                wait(dve, downs, e)
                nc.vector.tensor_copy(gated_t[:], psum[:, GATE_T, 0:2 * P].rearrange("p (m n) -> p m n", n=P)).then_inc(gates_out, 1)

            def weigh_high(e, j, rounds):
                dve.wait_ge(downs, e + 1)
                wait(dve, stored[j], rounds * 16)
                nc.vector.tensor_scalar(y[:, j, BANK:D], psum[:, DOWN + 1, :], share[:, bass.ds(e, 1)], None, ALU.mult).then_inc(y_high, 1)

            dve.wait_ge(small, 32)
            for e in range(ahead):
                match_of(e, e % ring)
                found_of(e, e % ring)
            match_of(ahead, ahead % ring)
            gate_of(0, 0)

            def step(e, j, known, i=None):
                rounds = known // ring if known is not None else i
                copy_gates(e, j)
                if known is None or known + ahead < n:
                    found_of(e + ahead, (j + ahead) % ring)
                if known is None or known + 1 < n:
                    gate_of(e + 1, (j + 1) % ring)
                if known is None or known + ahead + 1 < n:
                    match_of(e + (ahead + 1), (j + ahead + 1) % ring)
                weigh_high(e, j, rounds)

            for e in range(ring):
                step(e, e, e)
            with dve.Fori(1, n // ring - 2) as i:
                for j in range(ring):
                    step(ring * i + j, j, None, i)
            for e in range(n - 2 * ring, n):
                step(e, e % ring, e)


def spare_blocks_stage(nc, name, psum, ident, weights, first, h_dram, tables, routing, results):
    tok_tiles, spare = routing.tok_tiles, routing.spare
    with Stage(nc, name) as st:
        wbuf = st.sbuf("w", [P, 6 * D])
        slots, tokens = st.sbuf("slots", [P, P]), st.sbuf("tokens", [P, tok_tiles])
        match, pairs = st.sbuf("match", [P, tok_tiles, P]), st.sbuf("pairs", [P, tok_tiles, 2])
        who, share = st.sbuf("who", [P, 1], mybir.dt.uint32), st.sbuf("share", [P, 1])
        x_rows, x_cols = st.sbuf("x_rows", [P, D]), st.sbuf("x_cols", [P, KD, P])
        silu, gated, gated_t = st.sbuf("silu", [P, 256]), st.sbuf("gated", [P, 256]), st.sbuf("gated_t", [P, 2, P])
        y = st.sbuf("y", [P, D])
        mark, marked = st.sbuf("mark", [P, 2]), st.sem("marked")
        small, loaded, matched, found, found_out, gathered, turned, turned_out = (
            st.sem(k) for k in ("small", "loaded", "matched", "found", "found_out", "gathered", "turned", "turned_out"))
        ups, silus, gates, gates_turned, gates_out, downs, weighed, stored, moved = (
            st.sem(k) for k in ("ups", "silus", "gates", "gates_turned", "gates_out", "downs", "weighed", "stored", "moved"))
        block = st.block()
        gate_up = wbuf[:, 0:4 * D].rearrange("p (k n) -> p k n", k=KD)
        down = wbuf[:, 4 * D:6 * D].rearrange("p (m n) -> p m n", m=2)

        def blocks(eng, body):
            used = eng.value_load(routing.n_spare[0:1, 0:1], min_val=0, max_val=spare)
            with eng.Fori(0, spare) as x:
                with eng.If(x < used):
                    body(x)

        @block.sync
        def _(sp):
            sp.dma_start(slots[:], rows_of(tables["slots"])).then_inc(small, 16)
            sp.dma_start(tokens[:], tables["token_ids"][:, 0:tok_tiles]).then_inc(small, 16)

            def body(x):
                e = sp.value_load(routing.spare_expert[0:1, bass.ds(x, 1)], min_val=0, max_val=N_EXPERTS - 1)
                sp.wait_ge(moved, x + 1)
                sp.dma_start(wbuf[:], weights[e + first]).then_inc(loaded, 16)
                sp.wait_ge(weighed, x + 1)
                sp.dma_start(results[bass.ds(x * P + N_EXPERTS * P, P), :], y[:]).then_inc(stored, 16)
            blocks(sp, body)

        @block.gpsimd
        def _(pool):
            nc.gpsimd.memset(mark[:], 0.0).then_inc(marked, 1)

            def body(x):
                pool.wait_ge(found_out, x + 1)
                pool.wait_ge(marked, x + 1)
                nc.gpsimd.tensor_tensor(mark[0:1, 1:2], mark[0:1, 0:1], mark[0:1, 0:1], ALU.add).then_inc(marked, 1)
                nc.gpsimd.indirect_dma_start(out=x_rows[:], out_offset=None, in_=h_dram,
                                             in_offset=bass.IndirectOffsetOnAxis(ap=who[:], axis=0)).then_inc(gathered, 16)
            blocks(pool, body)

        @block.tensor
        def _(pe):
            pe.wait_ge(small, 32)

            def body(x):
                pe.wait_ge(matched, x + 1)
                for t in range(tok_tiles):
                    last = nc.tensor.matmul(psum[:, 0, 0:2], match[:, t, :], pairs[:, t, :], start=t == 0, stop=t == tok_tiles - 1)
                last.then_inc(found, 1)
                pe.wait_ge(gathered, 16 * x + 16)
                for k in range(KD):
                    last = nc.tensor.transpose(psum[:, 1 + k // 4, (k % 4) * P:(k % 4 + 1) * P], x_rows[:, k * P:(k + 1) * P], ident[:])
                last.then_inc(turned, 1)
                pe.wait_ge(loaded, 16 * x + 16)
                pe.wait_ge(turned_out, x + 1)
                for k in range(KD):
                    last = nc.tensor.matmul(psum[:, 4, :], x_cols[:, k, :], gate_up[:, k, :], start=k == 0, stop=k == KD - 1)
                last.then_inc(ups, 1)
                pe.wait_ge(gates, x + 1)
                for m in range(2):
                    last = nc.tensor.transpose(psum[:, 3, m * P:(m + 1) * P], gated[:, m * P:(m + 1) * P], ident[:])
                last.then_inc(gates_turned, 1)
                pe.wait_ge(gates_out, x + 1)
                for half in range(2):
                    for m in range(2):
                        last = nc.tensor.matmul(psum[:, 6 + half, :], gated_t[:, m, :], down[:, m, half * BANK:(half + 1) * BANK], start=m == 0, stop=m == 1)
                last.then_inc(downs, 1)
            blocks(pe, body)

        @block.scalar
        def _(act):
            def body(x):
                act.wait_ge(turned, x + 1)
                nc.scalar.activation(x_cols[:].rearrange("p k n -> p (k n)"), psum[:, 1:3, :].rearrange("p b n -> p (b n)"), ACT.Copy).then_inc(turned_out, 1)
                act.wait_ge(ups, x + 1)
                nc.scalar.activation(silu[:], psum[:, 4, 0:256], ACT.Silu).then_inc(silus, 1)
            blocks(act, body)

        @block.vector
        def _(dve):
            dve.wait_ge(small, 32)
            nc.vector.memset(share[:], 0.0).then_inc(moved, 1)

            def body(x):
                at = bass.ds(dve.value_load(routing.spare_expert[0:1, bass.ds(x, 1)], min_val=0, max_val=N_EXPERTS - 1), 1)
                dve.wait_ge(moved, x + 1)
                nc.vector.tensor_tensor(match[:], slots[:].unsqueeze(1).to_broadcast([P, tok_tiles, P]),
                                        routing.spare_slot[:, :, at].to_broadcast([P, tok_tiles, P]), ALU.is_equal)
                nc.vector.tensor_copy(pairs[:, :, 0:1], tokens[:].unsqueeze(2))
                nc.vector.tensor_copy(pairs[:, :, 1:2], routing.weight[:, :, at]).then_inc(matched, 1)
                dve.wait_ge(found, x + 1)
                nc.vector.tensor_copy(share[:], psum[:, 0, 1:2])
                nc.vector.tensor_copy(who[:], psum[:, 0, 0:1]).then_inc(found_out, 1)
                dve.wait_ge(silus, x + 1)
                nc.vector.tensor_tensor(gated[:], silu[:], psum[:, 4, 256:BANK], ALU.mult).then_inc(gates, 1)
                dve.wait_ge(gates_turned, x + 1)
                nc.vector.tensor_copy(gated_t[:].rearrange("p m n -> p (m n)"), psum[:, 3, 0:2 * P]).then_inc(gates_out, 1)
                dve.wait_ge(downs, x + 1)
                nc.vector.tensor_scalar(y[:], psum[:, 6:8, :].rearrange("p b n -> p (b n)"), share[:], None, ALU.mult).then_inc(weighed, 1)
                dve.wait_ge(weighed, x + 1)
                dve.wait_ge(stored, 16 * x + 16)
                nc.vector.tensor_scalar(routing.spare_slot[:], routing.spare_slot[:], -float(P), None, ALU.add).then_inc(moved, 1)
            blocks(dve, body)


def combine_stage(nc, name, acc, routing, results):
    depth = 8
    with Stage(nc, name) as st:
        rows = st.sbuf("rows", [P, depth, D])
        gathered = [st.sem(f"gathered{i}") for i in range(depth)]
        added = st.sem("added")
        total = routing.tok_tiles * TOP_K
        block = st.block()

        @block.gpsimd
        def _(pool):
            for g in range(total):
                if g >= depth:
                    pool.wait_ge(added, g - depth + 1)
                nc.gpsimd.indirect_dma_start(
                    out=rows[:, g % depth, :], out_offset=None, in_=results,
                    in_offset=bass.IndirectOffsetOnAxis(ap=routing.result_rows[:, g // TOP_K, g % TOP_K:g % TOP_K + 1], axis=0)).then_inc(gathered[g % depth], 16)

        @block.vector
        def _(dve):
            for g in range(total):
                dve.wait_ge(gathered[g % depth], 16 * (g // depth + 1))
                if g >= 1:
                    dve.wait_ge(added, g)
                t = g // TOP_K
                nc.vector.tensor_tensor(acc[:, t, :], acc[:, t, :], rows[:, g % depth, :], ALU.add).then_inc(added, 1)



def gated_units_stage(nc, name, psum, weights, first, n, cols, tokens, routes, acc):
    width = 256
    nd = tokens // P * 2
    with Stage(nc, name) as st:
        wbuf = st.sbuf("w", [P, 2, 6 * D])
        silu = st.sbuf("silu", [P, 2, tokens])
        gated = st.sbuf("gated", [P, 2, 2, tokens])
        loaded = [st.sem(f"loaded{i}") for i in range(2)]
        ups, silus, gates, downs, added = st.sem("ups"), st.sem("silus"), st.sem("gates"), st.sem("downs"), st.sem("added")
        block = st.block()
        gate_up = [wbuf[:, s, 0:4 * D].rearrange("p (k n) -> p k n", k=KD) for s in range(2)]
        down = [wbuf[:, s, 4 * D:6 * D].rearrange("p (m n) -> p m n", m=2) for s in range(2)]

        @block.sync
        def _(sp):
            for s in range(min(2, n)):
                sp.dma_start(wbuf[:, s, :], weights[first + s]).then_inc(loaded[s], 16)
            if n > 1:
                with sp.Fori(1, n // 2) as i:
                    for s in range(2):
                        sp.wait_ge(downs, i * (2 * nd) + (s - 1) * nd)
                        sp.dma_start(wbuf[:, s, :], weights[2 * i + (first + s)]).then_inc(loaded[s], 16)
                sp.wait_ge(downs, (n - 2) * nd)
                sp.dma_start(wbuf[:, 0, :], weights[first + n - 1]).then_inc(loaded[0], 16)

        @block.tensor
        def _(pe):
            def ups_of(slot, loads, earlier):
                pe.wait_ge(loaded[slot], loads)
                for m in range(2):
                    for kind in range(2):
                        if earlier is not None:
                            pe.wait_ge(gates if kind else silus, earlier + (m - 1))
                        for k in range(KD):
                            last = nc.tensor.matmul(psum[:, 2 * m + kind, 0:tokens], gate_up[slot][:, k, kind * width + m * P:kind * width + (m + 1) * P],
                                                    cols[:, k, 0:tokens], start=k == 0, stop=k == KD - 1)
                        last.then_inc(ups, 1)

            def down_of(slot, gates_wanted, adds_before):
                pe.wait_ge(gates, gates_wanted)
                for d in range(nd):
                    pe.wait_ge(added, adds_before + (d + 1))
                    for m in range(2):
                        last = nc.tensor.matmul(psum[:, 4 + d % 4, :], gated[:, slot, m, (d // 2) * P:(d // 2 + 1) * P],
                                                down[slot][:, m, (d % 2) * BANK:(d % 2 + 1) * BANK], start=m == 0, stop=m == 1)
                    last.then_inc(downs, 1)

            ups_of(0, 16, None)
            if n > 1:
                with pe.Fori(0, n // 2) as i:
                    ups_of(1, 16 * i + 16, 4 * i + 2)
                    down_of(0, 4 * i + 2, i * (2 * nd))
                    ups_of(0, 16 * i + 32, 4 * i + 4)
                    down_of(1, 4 * i + 4, i * (2 * nd) + nd)
            down_of(0, 2 * n, (n - 1) * nd)

        @block.scalar
        def _(act):
            def silus_of(ups_before, gates_before):
                for m in range(2):
                    act.wait_ge(ups, ups_before + (2 * m + 1))
                    if gates_before is not None:
                        act.wait_ge(gates, gates_before + (m - 1))
                    nc.scalar.activation(silu[:, m, :], psum[:, 2 * m, 0:tokens], ACT.Silu).then_inc(silus, 1)

            silus_of(0, None)
            if n > 1:
                with act.Fori(0, n // 2) as i:
                    silus_of(8 * i + 4, 4 * i + 2)
                    silus_of(8 * i + 8, 4 * i + 4)

        @block.vector
        def _(dve):
            def gates_of(slot, ups_before, silus_before):
                for m in range(2):
                    dve.wait_ge(ups, ups_before + (2 * m + 2))
                    dve.wait_ge(silus, silus_before + (m + 1))
                    nc.vector.tensor_tensor(gated[:, slot, m, :], silu[:, m, :], psum[:, 2 * m + 1, 0:tokens], ALU.mult).then_inc(gates, 1)

            def adds_of(expert, downs_before):
                for d in range(nd):
                    dve.wait_ge(downs, downs_before + (d + 1))
                    dve.wait_ge(added, downs_before + (d + 1))
                    part = acc[:, d // 2, (d % 2) * BANK:(d % 2 + 1) * BANK]
                    if routes is None:
                        ins = nc.vector.tensor_tensor(part, psum[:, 4 + d % 4, :], part, ALU.add)
                    else:
                        ins = nc.vector.scalar_tensor_tensor(part, psum[:, 4 + d % 4, :], routes[:, d // 2, bass.ds(expert, 1)], part, ALU.mult, ALU.add)
                    ins.then_inc(added, 1)

            for q in range(4):
                rows = acc[:, 0:tokens // P, :].rearrange("p t n -> p (t n)")
                quarter = tokens // P * D // 4
                nc.vector.memset(rows[:, q * quarter:(q + 1) * quarter], 0.0).then_inc(added, 1)
            gates_of(0, 0, 0)
            if n > 1:
                with dve.Fori(0, n // 2) as i:
                    gates_of(1, 8 * i + 4, 4 * i + 2)
                    adds_of(2 * i, i * (2 * nd))
                    gates_of(0, 8 * i + 8, 4 * i + 4)
                    adds_of(2 * i + 1, i * (2 * nd) + nd)
            adds_of(n - 1, (n - 1) * nd)




def split_cols(nc, name, psum, ident, rows, hi, lo, gain_cols):
    with Stage(nc, name) as st:
        transposed, his, los = st.sem("transposed"), st.sem("his"), st.sem("los")
        block = st.block()

        @block.tensor
        def _(pe):
            for j in range(KD):
                for t in range(2):
                    last = nc.tensor.transpose(psum[:, j, t * P:(t + 1) * P], rows[:, t, j * P:(j + 1) * P], ident[:])
                last.then_inc(transposed, 1)

        @block.scalar
        def _(act):
            for j in range(KD):
                act.wait_ge(transposed, j + 1)
                nc.scalar.activation(hi[:, j, :], psum[:, j, 0:LAT], ACT.Copy, scale=gain_cols[:, j:j + 1]).then_inc(his, 1)

        @block.vector
        def _(dve):
            for j in range(KD):
                dve.wait_ge(his, j + 1)
                nc.vector.scalar_tensor_tensor(lo[:, j, :], psum[:, j, 0:LAT], gain_cols[:, j:j + 1], hi[:, j, :].bitcast(F32),
                                               ALU.mult, ALU.subtract).then_inc(los, 1)


def ffn_stage(nc, name, psum, weights, first, x_hi, x_lo, acc):
    n = FFN_PARTS
    width = 256
    with Stage(nc, name) as st:
        raw_up, raw_down = st.sbuf("raw_up", [P, 2, 4 * D]), st.sbuf("raw_down", [P, 2, 2 * D])
        up_hi, up_lo = st.sbuf("up_hi", [P, 2, KD, BANK], F32R), st.sbuf("up_lo", [P, 2, KD, BANK], F32R)
        down_hi, down_lo = st.sbuf("down_hi", [P, 2, 2, D], F32R), st.sbuf("down_lo", [P, 2, 2, D], F32R)
        silu, gated = st.sbuf("silu", [P, 2, LAT]), st.sbuf("gated", [P, 2, LAT])
        gated_hi, gated_lo = st.sbuf("gated_hi", [P, 2, 2, LAT], F32R), st.sbuf("gated_lo", [P, 2, 2, LAT], F32R)
        up_loaded = [st.sem(f"up_loaded{i}") for i in range(2)]
        down_loaded = [st.sem(f"down_loaded{i}") for i in range(2)]
        up_his, up_los, down_his, down_los = (st.sem(k) for k in ("up_his", "up_los", "down_his", "down_los"))
        ups, silus, gates, gate_his, gate_los, downs, moved = (
            st.sem(k) for k in ("ups", "silus", "gates", "gate_his", "gate_los", "downs", "moved"))
        block = st.block()

        def steps(eng, step):
            step(0, 0, 0)
            with eng.Fori(0, (n - 3) // 2) as i:
                step(2 * i + 1, 1, None)
                step(2 * i + 2, 0, None)
            for e in (n - 2, n - 1):
                step(e, e % 2, e)

        @block.sync
        def _(sp):
            for e in range(2):
                sp.dma_start(raw_up[:, e, :], weights[first + e][:, 0:4 * D]).then_inc(up_loaded[e], 16)
                sp.dma_start(raw_down[:, e, :], weights[first + e][:, 4 * D:6 * D]).then_inc(down_loaded[e], 16)

            def load(e, j):
                sp.wait_ge(up_los, e - 1)
                sp.dma_start(raw_up[:, j, :], weights[e + first][:, 0:4 * D]).then_inc(up_loaded[j], 16)
                sp.wait_ge(down_los, e - 1)
                sp.dma_start(raw_down[:, j, :], weights[e + first][:, 4 * D:6 * D]).then_inc(down_loaded[j], 16)
            with sp.Fori(1, n // 2) as i:
                load(2 * i, 0)
                load(2 * i + 1, 1)
            load(n - 1, 0)

        @block.tensor
        def _(pe):
            def ups_of(e, j, at_first=False):
                pe.wait_ge(up_los, e + 1)
                for m in range(2):
                    for kind in range(2):
                        if not at_first:
                            pe.wait_ge(gates if kind else silus, 2 * e + (m - 1))
                        at = slice(kind * width + m * P, kind * width + (m + 1) * P)
                        for k in range(KD):
                            terms = ((up_hi, x_hi), (up_hi, x_lo), (up_lo, x_hi))
                            for which, (w, h) in enumerate(terms):
                                last = nc.tensor.matmul(psum[:, 2 * m + kind, 0:LAT], w[:, j, k, at], h[:, k, :],
                                                        start=k == 0 and which == 0, stop=k == KD - 1 and which == 2)
                        last.then_inc(ups, 1)

            def down_of(e, j, known):
                pe.wait_ge(down_los, e + 1)
                pe.wait_ge(gate_los, e + 1)
                for t in range(2):
                    for half in range(2):
                        for m in range(2):
                            terms = ((gated_hi, down_hi), (gated_lo, down_hi), (gated_hi, down_lo))
                            for which, (g, w) in enumerate(terms):
                                last = nc.tensor.matmul(psum[:, 4 + 2 * t + half, :], g[:, j, m, t * P:(t + 1) * P],
                                                        w[:, j, m, half * BANK:(half + 1) * BANK],
                                                        start=known == 0 and m == 0 and which == 0,
                                                        stop=known == n - 1 and m == 1 and which == 2)
                last.then_inc(downs, 1)

            def step(e, j, known):
                if known is None or known + 1 < n:
                    ups_of(e + 1, 1 - j)
                down_of(e, j, known)

            ups_of(0, 0, True)
            steps(pe, step)

        @block.scalar
        def _(act):
            def up_hi_of(e, j, loads, readers):
                act.wait_ge(up_loaded[j], loads)
                if readers:
                    act.wait_ge(ups, 4 * e - 4)
                nc.scalar.activation(up_hi[:, j, :, :].rearrange("p k n -> p (k n)"), raw_up[:, j, :], ACT.Copy).then_inc(up_his, 1)

            def down_hi_of(e, j, loads, readers):
                act.wait_ge(down_loaded[j], loads)
                if readers:
                    act.wait_ge(downs, e - 1)
                nc.scalar.activation(down_hi[:, j, :, :].rearrange("p m n -> p (m n)"), raw_down[:, j, :], ACT.Copy).then_inc(down_his, 1)

            def gate(e, j, at_first=False):
                for m in range(2):
                    act.wait_ge(ups, 4 * e + (2 * m + 1))
                    if not at_first:
                        act.wait_ge(gates, 2 * e + (m - 1))
                    nc.scalar.activation(silu[:, m, :], psum[:, 2 * m, 0:LAT], ACT.Silu).then_inc(silus, 1)
                act.wait_ge(gates, 2 * e + 2)
                nc.scalar.activation(gated_hi[:, j, :, :], gated[:], ACT.Copy).then_inc(gate_his, 1)

            def step(e, j, known):
                if known is None or known + 2 < n:
                    up_hi_of(e + 2, j, 8 * e + (32 - 8 * j), True)
                if known is None or known + 1 < n:
                    down_hi_of(e + 1, 1 - j, 8 * e + (16 + 8 * j), known != 0)
                    gate(e + 1, 1 - j)

            up_hi_of(0, 0, 16, False)
            up_hi_of(1, 1, 16, False)
            down_hi_of(0, 0, 16, False)
            gate(0, 0, True)
            steps(act, step)
            for b in (0, 2):
                act.wait_ge(downs, n)
                nc.scalar.activation(acc[:, b // 2, 0:BANK], psum[:, 4 + b, :], ACT.Copy).then_inc(moved, 1)

        @block.vector
        def _(dve):
            def up_lo_of(e, j):
                dve.wait_ge(up_his, e + 1)
                nc.vector.tensor_tensor(up_lo[:, j, :, :].rearrange("p k n -> p (k n)"), raw_up[:, j, :],
                                        up_hi[:, j, :, :].rearrange("p k n -> p (k n)").bitcast(F32), ALU.subtract).then_inc(up_los, 1)

            def down_lo_of(e, j):
                dve.wait_ge(down_his, e + 1)
                nc.vector.tensor_tensor(down_lo[:, j, :, :].rearrange("p m n -> p (m n)"), raw_down[:, j, :],
                                        down_hi[:, j, :, :].rearrange("p m n -> p (m n)").bitcast(F32), ALU.subtract).then_inc(down_los, 1)

            def gate(e, j, at_first=False):
                if not at_first:
                    dve.wait_ge(gate_los, e)
                for m in range(2):
                    dve.wait_ge(ups, 4 * e + (2 * m + 2))
                    dve.wait_ge(silus, 2 * e + (m + 1))
                    nc.vector.tensor_tensor(gated[:, m, :], silu[:, m, :], psum[:, 2 * m + 1, 0:LAT], ALU.mult).then_inc(gates, 1)
                dve.wait_ge(gate_his, e + 1)
                nc.vector.tensor_tensor(gated_lo[:, j, :, :], gated[:], gated_hi[:, j, :, :].bitcast(F32), ALU.subtract).then_inc(gate_los, 1)

            def step(e, j, known):
                if known is None or known + 2 < n:
                    up_lo_of(e + 2, j)
                if known is None or known + 1 < n:
                    down_lo_of(e + 1, 1 - j)
                    gate(e + 1, 1 - j)

            up_lo_of(0, 0)
            up_lo_of(1, 1)
            down_lo_of(0, 0)
            gate(0, 0, True)
            steps(dve, step)
            for b in (1, 3):
                dve.wait_ge(downs, n)
                nc.vector.tensor_copy(acc[:, b // 2, BANK:D], psum[:, 4 + b, :]).then_inc(moved, 1)



def neighbourhood_bias_stage(nc, table, rpb_turned, column_mask):
    with Stage(nc, "na_bias") as st:
        mask = st.sbuf("mask", [P, GRID_W])
        turned = st.sbuf("turned", [P, 2, NA_HEADS, LAT])
        loaded, masked = st.sem("loaded"), st.sem("masked")
        block = st.block()

        @block.sync
        def _(sp):
            sp.dma_start(mask[:], column_mask).then_inc(loaded, 16)
            for qt in range(2):
                for r in range(2):
                    dr0 = NA_KH - 1 - (2 * qt + r)
                    for h in range(NA_HEADS):
                        start = rpb_turned[h, dr0:dr0 + GRID_ROWS, 0:GRID_W]
                        diagonal = bass.AP(start.tensor, start.offset, [[1, GRID_W], [RPB_W, GRID_ROWS], [1, GRID_W]])
                        sp.dma_start(turned[r * GRID_W:(r + 1) * GRID_W, qt, h, :].rearrange("p (a b) -> p a b", b=GRID_W), diagonal).then_inc(loaded, 16)

        @block.vector
        def _(dve):
            dve.wait_ge(loaded, 16 * (1 + 4 * NA_HEADS))
            for qt in range(2):
                out = table[:, qt, :, :].rearrange("p h (a b) -> p (h a) b", b=GRID_W)
                of = turned[:, qt, :, :].rearrange("p h (a b) -> p (h a) b", b=GRID_W)
                steps = [list(x) for x in of.ap]
                right_to_left = bass.AP(of.tensor, of.offset + GRID_W - 1, [*steps[:2], [-1, GRID_W]])
                nc.vector.tensor_tensor(out, right_to_left, mask[:].unsqueeze(1).to_broadcast([P, NA_HEADS * GRID_ROWS, GRID_W]), ALU.add).then_inc(masked, 1)



def first_block(nc, i, psum, ident, x, cols, acc, mod_cols, mod_dram, h_dram, results):
    modulation_stage(nc, psum, ident, i["cvec"], i["w_mod"], i["b_mod"], mod_dram, mod_cols)

    def gate(layer, kind, row):
        return mod_dram[layer, row, kind * D:(kind + 1) * D]

    def to_rows(dst):
        return lambda engine, c, t, bank: copy_on(nc, engine, dst[:, t, c * BANK:(c + 1) * BANK], bank)

    def attention_outputs_to_cols(name, n_heads, tok_tiles, dst, k0):
        transpose_stage(nc, name, psum, ident, n_heads, tok_tiles, lambda j, t: acc[:, t, j * HEAD:(j + 1) * HEAD],
                        lambda engine, j, bank: copy_on(nc, engine, dst[:, k0 + j, 0:tok_tiles * P], bank[:, 0:tok_tiles * P]))

    for layer in range(DEPTH):
        tok_tiles = 4 if layer == 0 else 2
        modulated_cols(nc, f"h{layer}", psum, ident, x, cols, mod_cols, layer, 1, 4)
        if layer == 0:
            with Stage(nc, "ab") as st:
                proj = st.sbuf("proj", [P, 4, 3 * BANK])
                rows_product(nc, "ab_in", psum, cols, i["ab_w_in"], KD, 4, to_rows(proj))
                norm_rope_stage(nc, proj, i["qk_gains"], i["rope"])
                with Stage(nc, "ab_qk") as st2:
                    qk = st2.sbuf("qk", [P, 8, TOK])
                    transpose_stage(nc, "qk_t", psum, ident, 8, 4, lambda j, t: proj[:, t, LAT + j * HEAD:LAT + (j + 1) * HEAD],
                                    lambda engine, j, bank: copy_on(nc, engine, qk[:, j, :], bank))
                    units = [(h, t) for t in range(4) for h in range(6)]
                    first_key = lambda u: 0 if u[1] < 2 else LAT
                    attention_stage(
                        nc, "ab_att", psum, ident, units,
                        lambda u: [(0, qk[:, u[0], u[1] * P:(u[1] + 1) * P], qk[:, 6 + u[0] // 3, first_key(u):TOK])],
                        lambda u: TOK - first_key(u), lambda u: [], HEAD ** -0.5,
                        lambda u: [proj[:, t, 10 * HEAD + (u[0] // 3) * HEAD:10 * HEAD + (u[0] // 3 + 1) * HEAD] for t in range(first_key(u) // P, 4)],
                        lambda u: acc[:, u[1], u[0] * HEAD:(u[0] + 1) * HEAD], HEAD,
                        idle_fill=results[N_EXPERTS * P:, :])
                fourier_stages(nc, psum, proj, cols, i["ab_w_fnet"], i["dft_tokens"], i["dft_channels"])
                attention_outputs_to_cols("ab_o", 6, 4, cols, 2)
            rows_product(nc, "ab_out", psum, cols, i["ab_w_out"], KD, 4, to_rows(acc))
        else:
            with Stage(nc, "na") as st:
                q, k, v = st.sbuf("q", [P, 8, LAT]), st.sbuf("k", [P, 8, TOK]), st.sbuf("v", [P, 4, D])
                cols_product(nc, "na_qk", psum, cols, i["na_w_in"][0:4], lambda c: LAT if c < 2 else TOK,
                             lambda engine, c, t, bank: copy_on(nc, engine, (q if c < 2 else k)[:, (c % 2) * 4 + t, :], bank))
                rows_product(nc, "na_v", psum, cols, i["na_w_in"][4:6], KD, 4, to_rows(v))
                with Stage(nc, "na2") as st2:
                    table = st2.sbuf("table", [P, 2, NA_HEADS, LAT])
                    neighbourhood_bias_stage(nc, table, i["rpb_turned"], i["column_mask"])
                    units = [(h, t) for t in range(2) for h in range(NA_HEADS)]
                    attention_stage(
                        nc, "na_att", psum, ident, units,
                        lambda u: [(0, q[:, u[0], u[1] * P:(u[1] + 1) * P], k[:, u[0], :])],
                        lambda u: TOK,
                        lambda u: [(slice(0, LAT), table[:, u[1], u[0], :], None), (slice(LAT, TOK), None, None)], HEAD ** -0.5,
                        lambda u: [v[:, t, u[0] * HEAD:(u[0] + 1) * HEAD] for t in range(4)],
                        lambda u: acc[:, u[1], u[0] * HEAD:(u[0] + 1) * HEAD], HEAD)
                attention_outputs_to_cols("na_o", 8, 2, cols, 0)
            rows_product(nc, "na_out", psum, cols, i["na_w_out"], KD, 2, to_rows(acc))
        residual_norm_stage(nc, f"ln1_{layer}", x, acc, tok_tiles, gate(layer, 2, 0), gate(layer, 2, 1), i["ln1_g"][layer], i["ln1_b"][layer])
        rows_of_mod = [mod_dram[layer, row, kind * D:(kind + 1) * D] for row in range(tok_tiles // 2) for kind in (4, 3)]
        token_rows_stage(nc, f"h2_{layer}", x, acc, rows_of_mod, h_dram, tok_tiles)
        transpose_stage(nc, f"h2_cols{layer}", psum, ident, KD, tok_tiles, lambda j, t: acc[:, t, j * P:(j + 1) * P],
                        lambda engine, j, bank: copy_on(nc, engine, cols[:, j, 0:tok_tiles * P], bank[:, 0:tok_tiles * P]))
        with Stage(nc, f"moe{layer}") as st:
            routing = Routing(st, tok_tiles)
            router_stage(nc, f"router{layer}", psum, cols, i["w_router"][layer], i["moe_bias"][layer], i, routing)
            at = layer * (N_EXPERTS + 1)
            gated_units_stage(nc, f"shared{layer}", psum, i["experts"], at + N_EXPERTS, 1, cols, tok_tiles * P, None, acc)
            experts_stage(nc, f"experts{layer}", psum, ident, i["experts"], at, h_dram[0:tok_tiles * P, :], i, routing, results)
            spare_blocks_stage(nc, f"spare{layer}", psum, ident, i["experts"], at, h_dram[0:tok_tiles * P, :], i, routing, results)
            combine_stage(nc, f"combine{layer}", acc, routing, results)
        residual_norm_stage(nc, f"ln2_{layer}", x, acc, tok_tiles, gate(layer, 5, 0), gate(layer, 5, 1), i["ln2_g"][layer], i["ln2_b"][layer])



def rms_stage(nc, name, source, out, width, tok_tiles, gate=None):
    with Stage(nc, name) as st:
        square, ss = st.sbuf("square", [P, width]), st.sbuf("ss", [P, tok_tiles])
        std, rstd = st.sbuf("std", [P, tok_tiles]), st.sbuf("rstd", [P, tok_tiles])
        activated, gated, squared, varied, rooted, chain_sem = (
            st.sem("activated"), st.sem("gated"), st.sem("squared"), st.sem("varied"), st.sem("rooted"), st.sem("chain"))
        block = st.block()

        @block.scalar
        def _(act):
            if gate is not None:
                for t in range(tok_tiles):
                    nc.scalar.activation(gate[:, t, :], gate[:, t, :], ACT.Silu).then_inc(activated, 1)
            for t in range(tok_tiles):
                if gate is not None:
                    act.wait_ge(gated, t + 1)
                if t >= 1:
                    act.wait_ge(squared, t)
                nc.scalar.activation(square[:], source[:, t, 0:width], ACT.Square, accum_out=ss[:, t:t + 1]).then_inc(squared, 1)
            for t in range(tok_tiles):
                act.wait_ge(varied, t + 1)
                nc.scalar.activation(std[:, t:t + 1], ss[:, t:t + 1], ACT.Sqrt).then_inc(rooted, 1)

        @block.vector
        def _(dve):
            chain = Chain(dve, chain_sem)
            if gate is not None:
                for t in range(tok_tiles):
                    dve.wait_ge(activated, t + 1)
                    nc.vector.tensor_tensor(source[:, t, :], source[:, t, :], gate[:, t, :], ALU.mult).then_inc(gated, 1)
            for t in range(tok_tiles):
                dve.wait_ge(squared, t + 1)
                nc.vector.tensor_scalar(ss[:, t:t + 1], ss[:, t:t + 1], 1.0 / width, EPS, ALU.mult, ALU.add).then_inc(varied, 1)
            for t in range(tok_tiles):
                dve.wait_ge(rooted, t + 1)
                chain.then(nc.vector.reciprocal(rstd[:, t:t + 1], std[:, t:t + 1]))
                chain.then(nc.vector.tensor_scalar(out[:, t, 0:width], source[:, t, 0:width], rstd[:, t:t + 1], None, ALU.mult))


def scaled_cols(nc, name, psum, ident, rows, cols, k0, gain_cols):
    def drain(engine, j, bank):
        if engine == "v":
            return nc.vector.tensor_scalar(cols[:, k0 + j, 0:LAT], bank[:, 0:LAT], gain_cols[:, j:j + 1], None, ALU.mult)
        return nc.scalar.activation(cols[:, k0 + j, 0:LAT], bank[:, 0:LAT], ACT.Copy, scale=gain_cols[:, j:j + 1])
    transpose_stage(nc, name, psum, ident, KD, 2, lambda j, i: rows[:, i, j * P:(j + 1) * P], drain)


def add_scaled_stage(nc, name, x, y, gain, factor):
    with Stage(nc, name) as st:
        vec = st.sbuf("vec", [P, D])
        loaded, chain_sem = st.sem("loaded"), st.sem("chain")
        block = st.block()

        @block.sync
        def _(sp):
            sp.dma_start(vec[:], rows_of(gain)).then_inc(loaded, 16)

        @block.vector
        def _(dve):
            chain = Chain(dve, chain_sem)
            dve.wait_ge(loaded, 16)
            for t in range(2):
                chain.then(nc.vector.scalar_tensor_tensor(y[:, t, :], y[:, t, :], factor, vec[:], ALU.mult, ALU.mult))
                chain.then(nc.vector.tensor_tensor(x[:, t, :], x[:, t, :], y[:, t, :], ALU.add))



def causal_conv_stage(nc, name, padded, out, taps, bias, n_tiles, n_taps, activation=None):
    with Stage(nc, name) as st:
        w, b = st.sbuf("w", [P, n_tiles, n_taps]), st.sbuf("b", [P, n_tiles])
        loaded, tapped, activated = st.sem("loaded"), st.sem("tapped"), st.sem("activated")
        block = st.block()

        @block.sync
        def _(sp):
            sp.dma_start(w[:], taps).then_inc(loaded, 16)
            sp.dma_start(b[:], bias).then_inc(loaded, 16)

        @block.vector
        def _(dve):
            dve.wait_ge(loaded, 32)
            for j in range(n_taps):
                for m in range(n_tiles):
                    source = padded[:, m, j:j + LAT]
                    if j == 0:
                        ins = nc.vector.tensor_scalar(out[:, m, :], source, w[:, m, 0:1], b[:, m:m + 1], ALU.mult, ALU.add)
                    else:
                        dve.wait_ge(tapped, (j - 1) * n_tiles + m + 1)
                        ins = nc.vector.scalar_tensor_tensor(out[:, m, :], source, w[:, m, j:j + 1], out[:, m, :], ALU.mult, ALU.add)
                    ins.then_inc(tapped, 1)

        if activation is not None:
            @block.scalar
            def _(act):
                for m in range(n_tiles):
                    act.wait_ge(tapped, (n_taps - 1) * n_tiles + m + 1)
                    nc.scalar.activation(out[:, m, :], out[:, m, :], activation).then_inc(activated, 1)


def glu_stage(nc, val_gate, hidden, pad):
    with Stage(nc, "glu") as st:
        squashed, made = st.sem("squashed"), st.sem("made")
        block = st.block()

        @block.scalar
        def _(act):
            for half in range(2):
                at = val_gate[:, KD + 4 * half:KD + 4 * half + 4, :]
                nc.scalar.activation(at, at, ACT.Sigmoid).then_inc(squashed, 1)

        @block.gpsimd
        def _(pool):
            nc.gpsimd.memset(hidden[:, :, 0:pad], 0.0).then_inc(made, 1)

        @block.vector
        def _(dve):
            for half in range(2):
                dve.wait_ge(squashed, half + 1)
                ks = slice(4 * half, 4 * half + 4)
                nc.vector.tensor_tensor(hidden[:, ks, pad:pad + LAT], val_gate[:, ks, :],
                                        val_gate[:, KD + 4 * half:KD + 4 * half + 4, :], ALU.mult).then_inc(made, 1)


def conformer_norm_stage(nc, psum, hid, cat, averager, gain_cols, shift_cols):
    with Stage(nc, "conformer") as st:
        avg, gain, shift = st.sbuf("avg", [P, P]), st.sbuf("gain", [P, KD]), st.sbuf("shift", [P, KD])
        square, rstd = st.sbuf("square", [P, KD, LAT]), st.sbuf("rstd", [P, LAT])
        loaded, means, centred, squared, variances = st.sem("loaded"), st.sem("means"), st.sem("centred"), st.sem("squared"), st.sem("variances")
        shifted, rooted, scaled, activated, chain_sem = st.sem("shifted"), st.sem("rooted"), st.sem("scaled"), st.sem("activated"), st.sem("chain")
        block = st.block()

        @block.sync
        def _(sp):
            sp.dma_start(avg[:], averager).then_inc(loaded, 16)
            sp.dma_start(gain[:], gain_cols).then_inc(loaded, 16)
            sp.dma_start(shift[:], shift_cols).then_inc(loaded, 16)

        @block.tensor
        def _(pe):
            pe.wait_ge(loaded, 48)
            for m in range(KD):
                last = nc.tensor.matmul(psum[:, 0, 0:LAT], avg[:], hid[:, m, :], start=m == 0, stop=m == KD - 1)
            last.then_inc(means, 1)
            for m in range(KD):
                pe.wait_ge(squared, m + 1)
                last = nc.tensor.matmul(psum[:, 1, 0:LAT], avg[:], square[:, m, :], start=m == 0, stop=m == KD - 1)
            last.then_inc(variances, 1)

        @block.vector
        def _(dve):
            chain = Chain(dve, chain_sem)
            dve.wait_ge(means, 1)
            for m in range(KD):
                nc.vector.tensor_tensor(hid[:, m, :], hid[:, m, :], psum[:, 0, 0:LAT], ALU.subtract).then_inc(centred, 1)
            dve.wait_ge(variances, 1)
            nc.vector.tensor_scalar(rstd[:], psum[:, 1, 0:LAT], EPS, None, ALU.add).then_inc(shifted, 1)
            dve.wait_ge(rooted, 1)
            chain.then(nc.vector.reciprocal(rstd[:], rstd[:]))
            for m in range(KD):
                dve.wait_ge(squared, m + 1)
                nc.vector.tensor_tensor(hid[:, m, :], hid[:, m, :], rstd[:], ALU.mult).then_inc(scaled, 1)

        @block.scalar
        def _(act):
            act.wait_ge(loaded, 48)
            for m in range(KD):
                act.wait_ge(centred, m + 1)
                nc.scalar.activation(square[:, m, :], hid[:, m, :], ACT.Square).then_inc(squared, 1)
            act.wait_ge(shifted, 1)
            nc.scalar.activation(rstd[:], rstd[:], ACT.Sqrt).then_inc(rooted, 1)
            for m in range(KD):
                act.wait_ge(scaled, m + 1)
                nc.scalar.activation(cat[:, m, :], hid[:, m, :], ACT.Silu, scale=gain[:, m:m + 1], bias=shift[:, m:m + 1]).then_inc(activated, 1)



def time_step_stage(nc, dt_raw, dt_bias, a_log, dt, da):
    with Stage(nc, "time_step") as st:
        shape = [P, 2, SSM_HEADS]
        bias, rate = st.sbuf("bias", [P, SSM_HEADS]), st.sbuf("rate", [P, SSM_HEADS])
        size, tail = st.sbuf("size", shape), st.sbuf("tail", shape)
        loaded, biased, tailed, rated, chain_sem, act_chain = (
            st.sem("loaded"), st.sem("biased"), st.sem("tailed"), st.sem("rated"), st.sem("chain"), st.sem("act_chain"))
        block = st.block()

        @block.sync
        def _(sp):
            sp.dma_start(bias[:], rows_of(dt_bias)).then_inc(loaded, 16)
            sp.dma_start(rate[:], rows_of(a_log)).then_inc(loaded, 16)

        @block.scalar
        def _(act):
            chain = Chain(act, act_chain)
            act.wait_ge(loaded, 32)
            nc.scalar.activation(rate[:], rate[:], ACT.Exp).then_inc(rated, 1)
            act.wait_ge(biased, 1)
            chain.then(nc.scalar.activation(size[:], dt_raw[:], ACT.Abs))
            chain.then(nc.scalar.activation(size[:], size[:], ACT.Exp, scale=-1.0))
            nc.scalar.activation(tail[:], size[:], ACT.Ln, bias=1.0).then_inc(tailed, 1)

        @block.vector
        def _(dve):
            chain = Chain(dve, chain_sem)
            dve.wait_ge(loaded, 32)
            nc.vector.tensor_tensor(dt_raw[:], dt_raw[:], bias[:].unsqueeze(1).to_broadcast(shape), ALU.add).then_inc(biased, 1)
            dve.wait_ge(tailed, 1)
            dve.wait_ge(rated, 1)
            chain.then(nc.vector.scalar_tensor_tensor(dt[:], dt_raw[:], 0.0, tail[:], ALU.max, ALU.add))
            chain.then(nc.vector.scalar_tensor_tensor(da[:], dt[:], -1.0, rate[:].unsqueeze(1).to_broadcast(shape), ALU.mult, ALU.mult))


def state_space_stages(nc, psum, ident, xbc, dt, da, triangles, d_skip, y):
    heads, dim = SSM_HEADS, SSM_P
    per = heads // 2
    with Stage(nc, "ssd") as st:
        tri = st.sbuf("tri", [P, 2, P])
        skip = st.sbuf("skip", [P, heads])
        spread = st.sbuf("spread", [P, 2, heads, P])
        x_rows, x_dt = st.sbuf("x_rows", [P, 2, D]), st.sbuf("x_dt", [P, 2, D])
        x_state = st.sbuf("x_state", [P, D])
        b_rows = st.sbuf("b_rows", [P, 2, P])
        cum, tail_decay, cum_exp = st.sbuf("cum", [P, 2, heads]), st.sbuf("tail_decay", [P, heads]), st.sbuf("cum_exp", [P, heads])
        pair = st.sbuf("pair", [P, 2, 2, P])
        decay = st.sbuf("decay", [P, 2, heads, P])
        state = st.sbuf("state", [P, 2, BANK])
        loaded, chain_sem = st.sem("loaded"), st.sem("chain")
        rows_turned, rows_out = st.sem("rows_turned"), st.sem("rows_out")
        sums_ready, sums_out, spread_made = st.sem("sums_ready"), st.sem("sums_out"), st.sem("spread_made")
        pairs_ready, pairs_out = st.sem("pairs_ready"), st.sem("pairs_out")
        with nc.Block() as block:
            @block.sync
            def _(sp):
                sp.dma_start(tri[:], triangles).then_inc(loaded, 16)
                sp.dma_start(skip[:], rows_of(d_skip)).then_inc(loaded, 16)

            @block.tensor
            def _(pe):
                for c in range(2):
                    for k in range(KD):
                        last = nc.tensor.transpose(psum[:, 2 * c + k // 4, (k % 4) * P:(k % 4 + 1) * P], xbc[:, k, c * P:(c + 1) * P], ident[:])
                    last.then_inc(rows_turned, 1)
                for g in range(2):
                    last = nc.tensor.transpose(psum[:, 4, g * P:(g + 1) * P], xbc[:, KD + g, 0:P], ident[:])
                last.then_inc(rows_turned, 1)
                pe.wait_ge(loaded, 32)
                for c in range(2):
                    nc.tensor.matmul(psum[:, 5, c * heads:(c + 1) * heads], tri[:, 0, :], da[:, c, :], start=True, stop=True)
                nc.tensor.matmul(psum[:, 5, 2 * heads:3 * heads], tri[:, 1, :], da[:, 0, :], start=True, stop=True).then_inc(sums_ready, 1)
                for c in range(2):
                    for g in range(2):
                        last = nc.tensor.matmul(psum[:, 6, (2 * c + g) * P:(2 * c + g + 1) * P], xbc[:, KD + g, c * P:(c + 1) * P],
                                                xbc[:, KD + 2 + g, c * P:(c + 1) * P], start=True, stop=True)
                last.then_inc(pairs_ready, 1)

            @block.scalar
            def _(act):
                act.wait_ge(rows_turned, 1)
                nc.scalar.activation(x_rows[:, 0, :], psum[:, 0:2, :].rearrange("p b n -> p (b n)"), ACT.Copy).then_inc(rows_out, 1)
                act.wait_ge(rows_turned, 2)
                nc.scalar.activation(x_rows[:, 1, :], psum[:, 2:4, :].rearrange("p b n -> p (b n)"), ACT.Copy).then_inc(rows_out, 1)
                act.wait_ge(rows_turned, 3)
                nc.scalar.activation(b_rows[:], psum[:, 4, 0:2 * P].rearrange("p (g n) -> p g n", g=2), ACT.Copy).then_inc(rows_out, 1)
                act.wait_ge(sums_out, 1)
                nc.scalar.activation(tail_decay[:], psum[:, 5, 2 * heads:3 * heads], ACT.Exp).then_inc(sums_out, 1)
                nc.scalar.activation(cum_exp[:], psum[:, 5, heads:2 * heads], ACT.Exp).then_inc(sums_out, 1)

            @block.gpsimd
            def _(pool):
                for c in range(2):
                    nc.gpsimd.tensor_copy(spread[:, c, :, :], da[:, c, :].unsqueeze(2).to_broadcast([P, heads, P])).then_inc(spread_made, 1)

            @block.vector
            def _(dve):
                chain = Chain(dve, chain_sem)
                dve.wait_ge(sums_ready, 1)
                nc.vector.tensor_copy(cum[:], psum[:, 5, 0:2 * heads].rearrange("p (c h) -> p c h", c=2)).then_inc(sums_out, 1)
                dve.wait_ge(pairs_ready, 1)
                dve.wait_ge(loaded, 32)
                nc.vector.tensor_tensor(pair[:].rearrange("p c g l -> p (c g) l"), psum[:, 6, :].rearrange("p (a l) -> p a l", l=P),
                                        tri[:, 0, :].unsqueeze(1).to_broadcast([P, 4, P]), ALU.mult).then_inc(pairs_out, 1)
                for c in range(2):
                    dve.wait_ge(rows_out, c + 1)
                    chain.then(nc.vector.tensor_tensor(x_dt[:, c, :].rearrange("p (h d) -> p h d", d=dim), x_rows[:, c, :].rearrange("p (h d) -> p h d", d=dim),
                                                       dt[:, c, :].unsqueeze(2).to_broadcast([P, heads, dim]), ALU.mult))
                dve.wait_ge(sums_out, 3)
                chain.then(nc.vector.tensor_tensor(x_state[:].rearrange("p (h d) -> p h d", d=dim), x_dt[:, 0, :].rearrange("p (h d) -> p h d", d=dim),
                                                   tail_decay[:].unsqueeze(2).to_broadcast([P, heads, dim]), ALU.mult))

        decays, narrowed, exped, weighed = st.sem("decays"), st.sem("narrowed"), st.sem("exped"), st.sem("weighed")
        with nc.Block() as block:
            @block.tensor
            def _(pe):
                for b in range(8):
                    for j in range(4):
                        h = 4 * (b % 4) + j
                        last = nc.tensor.matmul(psum[:, b, j * P:(j + 1) * P], spread[:, b // 4, h, :], tri[:, 0, :], start=True, stop=True)
                    last.then_inc(decays, 1)

            @block.vector
            def _(dve):
                for step in range(9):
                    if step < 8:
                        b = step
                        dve.wait_ge(decays, b + 1)
                        for j in range(4):
                            h = 4 * (b % 4) + j
                            last = nc.vector.tensor_scalar(decay[:, b // 4, h, :], psum[:, b, j * P:(j + 1) * P], cum[:, b // 4, h:h + 1], 0.0, ALU.subtract, ALU.min)
                        last.then_inc(narrowed, 1)
                    if step >= 1:
                        b = step - 1
                        dve.wait_ge(exped, b + 1)
                        at = decay[:, b // 4, 4 * (b % 4):4 * (b % 4) + 4, :]
                        nc.vector.tensor_tensor(at, at, pair[:, b // 4, (b % 4) // 2, :].unsqueeze(1).to_broadcast([P, 4, P]), ALU.mult).then_inc(weighed, 1)

            @block.scalar
            def _(act):
                for b in range(8):
                    act.wait_ge(narrowed, b + 1)
                    at = decay[:, b // 4, 4 * (b % 4):4 * (b % 4) + 4, :]
                    nc.scalar.activation(at, at, ACT.Exp).then_inc(exped, 1)

        states, states_out, inner, outer, chain2 = st.sem("states"), st.sem("states_out"), st.sem("inner"), st.sem("outer"), st.sem("chain2")
        with nc.Block() as block:
            @block.tensor
            def _(pe):
                for g in range(2):
                    last = nc.tensor.matmul(psum[:, 4 + g, :], b_rows[:, g, :], x_state[:, g * BANK:(g + 1) * BANK], start=True, stop=True)
                last.then_inc(states, 1)
                for c in range(2):
                    for h in range(heads):
                        last = nc.tensor.matmul(psum[:, 2 * c + h // per, (h % per) * dim:(h % per + 1) * dim], decay[:, c, h, :],
                                                x_dt[:, c, h * dim:(h + 1) * dim], start=True, stop=True)
                    last.then_inc(inner, 1)
                pe.wait_ge(states_out, 1)
                for g in range(2):
                    last = nc.tensor.matmul(psum[:, 6 + g, :], xbc[:, KD + 2 + g, P:2 * P], state[:, g, :], start=True, stop=True)
                last.then_inc(outer, 1)

            @block.scalar
            def _(act):
                act.wait_ge(states, 1)
                nc.scalar.activation(state[:], psum[:, 4:6, :], ACT.Copy).then_inc(states_out, 1)

            @block.vector
            def _(dve):
                chain = Chain(dve, chain2)
                for c in range(2):
                    chain.then(nc.vector.tensor_tensor(y[:, c, :].rearrange("p (h d) -> p h d", d=dim), x_rows[:, c, :].rearrange("p (h d) -> p h d", d=dim),
                                                       skip[:].unsqueeze(2).to_broadcast([P, heads, dim]), ALU.mult))
                    dve.wait_ge(inner, c + 1)
                    chain.then(nc.vector.tensor_tensor(y[:, c, :], y[:, c, :], psum[:, 2 * c:2 * c + 2, :].rearrange("p b n -> p (b n)"), ALU.add))
                dve.wait_ge(outer, 1)
                chain.then(nc.vector.tensor_tensor(x_state[:].rearrange("p (h d) -> p h d", d=dim), psum[:, 6:8, :].rearrange("p b (h d) -> p (b h) d", d=dim),
                                                   cum_exp[:].unsqueeze(2).to_broadcast([P, heads, dim]), ALU.mult))
                chain.then(nc.vector.tensor_tensor(y[:, 1, :], y[:, 1, :], x_state[:], ALU.add))



def second_block(nc, i, psum, ident, x, acc):
    def ffn(layer, which):
        g = 4 * which
        name = f"ffn{layer}{which}"
        rms_stage(nc, name + "_pre", x, acc, D, 2)
        with Stage(nc, name + "_h") as st:
            x_hi, x_lo = st.sbuf("x_hi", [P, KD, LAT], F32R), st.sbuf("x_lo", [P, KD, LAT], F32R)
            split_cols(nc, name + "_cols", psum, ident, acc, x_hi, x_lo, gains[:, layer, g, :])
            ffn_stage(nc, name, psum, i["ffn"], (2 * layer + which) * FFN_PARTS, x_hi, x_lo, acc)
        rms_stage(nc, name + "_post", acc, acc, D, 2)
        add_scaled_stage(nc, name + "_add", x, acc, i["norm_g"][layer, g + 1], 0.5)

    def to_cols(dst, k0, per_chunk=4):
        return lambda engine, c, t, bank: copy_on(nc, engine, dst[:, k0 + c * per_chunk + t, :], bank)

    def to_rows(dst):
        return lambda engine, c, t, bank: copy_on(nc, engine, dst[:, t, c * BANK:(c + 1) * BANK], bank)

    with Stage(nc, "second") as top:
        gains, ssm_gain = top.sbuf("gains", [P, DEPTH, 6, KD]), top.sbuf("ssm_gain", [P, KD])
        loaded = top.sem("loaded")
        with nc.Block() as block:
            @block.sync
            def _(sp):
                sp.dma_start(gains[:], i["norm_g_cols"]).then_inc(loaded, 16)
                sp.dma_start(ssm_gain[:], i["ssm_norm_g_cols"]).then_inc(loaded, 16)
                sp.wait_ge(loaded, 32)
        for layer in range(DEPTH):
            ffn(layer, 0)
            rms_stage(nc, f"mix{layer}_pre", x, acc, D, 2)
            with Stage(nc, f"mixer{layer}") as mst:
                cols = mst.sbuf("cols", [P, KD, LAT])
                scaled_cols(nc, f"mix{layer}_cols", psum, ident, acc, cols, 0, gains[:, layer, 2, :])
                if layer == 0:
                    with Stage(nc, "hyb") as st:
                        cat, z = st.sbuf("cat", [P, 2 * KD, LAT]), st.sbuf("z", [P, 2, D])
                        hid = st.sbuf("hid", [P, KD, CONV_TAPS - 1 + LAT])
                        xbc = st.sbuf("xbc", [P, 12, SSM_TAPS - 1 + LAT])
                        dt_raw, dt, da = (st.sbuf(n, [P, 2, SSM_HEADS]) for n in ("dt_raw", "dt", "da"))
                        with Stage(nc, "hyb_glu") as st2:
                            val_gate = st2.sbuf("val_gate", [P, 2 * KD, LAT])
                            cols_product(nc, "hyb_vg", psum, cols, i["hyb_w_in"][0:4], lambda c: LAT, to_cols(val_gate, 0))
                            glu_stage(nc, val_gate, hid, CONV_TAPS - 1)
                        rows_product(nc, "hyb_z", psum, cols, i["hyb_w_in"][4:6], KD, 2, to_rows(z))
                        cleared = st.sem("cleared")
                        with nc.Block() as block:
                            @block.gpsimd
                            def _(pool):
                                nc.gpsimd.memset(xbc[:, :, 0:SSM_TAPS - 1], 0.0).then_inc(cleared, 1)
                        cols_product(nc, "hyb_xbc", psum, cols, i["hyb_w_in"][6:9], lambda c: LAT,
                                     lambda engine, c, t, bank: copy_on(nc, engine, xbc[:, 4 * c + t, SSM_TAPS - 1:], bank))
                        rows_product(nc, "hyb_dt", psum, cols, i["hyb_w_dt"], KD, 2,
                                     lambda engine, c, t, bank: copy_on(nc, engine, dt_raw[:, t, :], bank))
                        with Stage(nc, "hyb_conv") as st2:
                            conv = st2.sbuf("conv", [P, KD, LAT])
                            causal_conv_stage(nc, "conv31", hid, conv, i["conv_taps"], i["conv_b_cols"], KD, CONV_TAPS)
                            conformer_norm_stage(nc, psum, conv, cat, i["averager"], i["conv_ln_g_cols"], i["conv_ln_b_cols"])
                        with Stage(nc, "hyb_ssm") as st2:
                            mixed = st2.sbuf("mixed", [P, 12, LAT])
                            causal_conv_stage(nc, "conv4", xbc, mixed, i["ssm_taps"], i["ssm_b_cols"], 12, SSM_TAPS, ACT.Silu)
                            time_step_stage(nc, dt_raw, i["ssm_dt_bias"], i["ssm_a_log"], dt, da)
                            state_space_stages(nc, psum, ident, mixed, dt, da, i["triangles"], i["ssm_d"], acc)
                            rms_stage(nc, "ssm_norm", acc, acc, D, 2, gate=z)
                            scaled_cols(nc, "ssm_cols", psum, ident, acc, cat, KD, ssm_gain)
                        rows_product(nc, "hyb_out", psum, cat, i["hyb_w_out"], 2 * KD, 2, to_rows(acc))
                else:
                    with Stage(nc, "dil") as st:
                        q, k = st.sbuf("q", [P, 12, LAT]), st.sbuf("k", [P, 12, LAT])
                        v = st.sbuf("v", [P, 2, 3 * BANK])
                        cols_product(nc, "dil_q", psum, cols, i["attn_w_qkv"][0:3], lambda c: LAT, to_cols(q, 0))
                        cols_product(nc, "dil_k", psum, cols, i["attn_w_qkv"][3:6], lambda c: LAT, to_cols(k, 0))
                        rows_product(nc, "dil_v", psum, cols, i["attn_w_qkv"][6:9], KD, 2, to_rows(v))
                        with Stage(nc, "dil2") as st2:
                            table = st2.sbuf("table", [P, 2, DIL_GROUPS, LAT])
                            there = st2.sem("there")
                            with nc.Block() as block:
                                @block.sync
                                def _(sp):
                                    sp.dma_start(table[:], i["distances"]).then_inc(there, 16)
                                    sp.wait_ge(there, 16)
                            scale = DIL_DH ** -0.5
                            units = [(h, t) for t in range(2) for h in range(DIL_HEADS)]
                            n_keys = lambda t: P * (t + 1)

                            def head_of(tensor, h, g):
                                return tensor[(h % 2) * DIL_DH:(h % 2 + 1) * DIL_DH, 4 * g + h // 2, :]

                            attention_stage(
                                nc, "dil_att", psum, ident, units,
                                lambda u: [(g * n_keys(u[1]), head_of(q, u[0], g)[:, u[1] * P:(u[1] + 1) * P], head_of(k, u[0], g)[:, 0:n_keys(u[1])]) for g in range(DIL_GROUPS)],
                                lambda u: DIL_GROUPS * n_keys(u[1]),
                                lambda u: [(slice(g * n_keys(u[1]), (g + 1) * n_keys(u[1])), table[:, u[1], g, 0:n_keys(u[1])],
                                            -(2.0 ** -(u[0] + 1)) / scale) for g in range(DIL_GROUPS)],
                                scale,
                                lambda u: [v[:, t, g * BANK + u[0] * DIL_DH:g * BANK + (u[0] + 1) * DIL_DH] for g in range(DIL_GROUPS) for t in range(u[1] + 1)],
                                lambda u: acc[:, u[1], u[0] * DIL_DH:(u[0] + 1) * DIL_DH], DIL_DH)
                        transpose_stage(nc, "dil_o", psum, ident, 4, 2, lambda j, t: acc[:, t, j * P:(j + 1) * P],
                                        lambda engine, j, bank: copy_on(nc, engine, cols[:, j, 0:LAT], bank[:, 0:LAT]))
                    rows_product(nc, "dil_out", psum, cols, i["attn_w_o"], 4, 2, to_rows(acc))
            rms_stage(nc, f"mix{layer}_post", acc, acc, D, 2)
            add_scaled_stage(nc, f"mix{layer}_add", x, acc, i["norm_g"][layer, 3], 1.0)
            ffn(layer, 1)



def program(nc, i, out):
    with Stage(nc, "all") as st:
        psum = st.stack.enter_context(nc.psum_tensor("psum", [P, NBANKS, BANK], F32))
        mod_dram = nc.dram_tensor("mod_dram", [DEPTH, 2, 6 * D], F32, kind="Internal").ap()
        h_dram = nc.dram_tensor("h_dram", [TOK, D], F32, kind="Internal").ap()
        most_blocks = N_EXPERTS + TOK * TOP_K // P - 1
        results = nc.dram_tensor("results", [most_blocks * P, D], F32, kind="Internal").ap()
        x, ident = st.sbuf("x", [P, 4, D]), st.sbuf("ident", [P, P])
        loaded, stored = st.sem("loaded"), st.sem("stored")
        with nc.Block() as block:
            @block.sync
            def _(sp):
                sp.dma_start(x[:, 0:2, :], i["x"].rearrange("(t p) d -> p t d", p=P)).then_inc(loaded, 16)
                sp.dma_start(x[:, 2:4, :], i["ctx"].rearrange("(t p) d -> p t d", p=P)).then_inc(loaded, 16)
                sp.dma_start(ident[:], i["ident"]).then_inc(loaded, 16)
                sp.wait_ge(loaded, 48)
        with Stage(nc, "block1") as st1:
            cols, acc = st1.sbuf("cols", [P, KD, TOK]), st1.sbuf("acc", [P, 4, D])
            mod_cols = st1.sbuf("mod_cols", [P, DEPTH, 6 * KD, 2])
            first_block(nc, i, psum, ident, x, cols, acc, mod_cols, mod_dram, h_dram, results)
        with Stage(nc, "block2") as st2:
            acc = st2.sbuf("acc", [P, 2, D])
            second_block(nc, i, psum, ident, x, acc)
        with nc.Block() as block:
            @block.sync
            def _(sp):
                sp.dma_start(out.rearrange("(t p) d -> p t d", p=P), x[:, 0:2, :]).then_inc(stored, 16)
                sp.wait_ge(stored, 16)



def chunks(w, width=BANK, k_tiles=None):
    k, n = w.shape
    return np.ascontiguousarray(w.reshape(k // P, P, n // width, width).transpose(2, 1, 0, 3)).reshape(n // width, P, -1)


def gated_parts(gate, up, down):
    lead = gate.shape[:-2]
    n = gate.shape[-1] // 256
    g = gate.reshape(*lead, KD, P, n, 256)
    u = up.reshape(*lead, KD, P, n, 256)
    d = down.reshape(*lead, n, 2, P, D)
    g, u, d = np.moveaxis(g, -2, -4), np.moveaxis(u, -2, -4), np.swapaxes(d, -3, -2)
    g, u = np.swapaxes(g, -3, -2), np.swapaxes(u, -3, -2)
    out = np.empty((*lead, n, P, 6 * D), np.float32)
    gu = out[..., 0:4 * D].reshape(*lead, n, P, KD, 2, 256)
    out[..., 0:4 * D].reshape(*lead, n, P, KD, 2, 256)
    for kind, w in enumerate((g, u)):
        for k in range(KD):
            out[..., k * 512 + kind * 256:k * 512 + kind * 256 + 256] = w[..., k, :]
    for m in range(2):
        out[..., 4 * D + m * D:4 * D + (m + 1) * D] = d[..., m, :]
    return out.reshape(-1, P, 6 * D)


def shape_tables():
    t = {"ident": np.eye(P)}
    half, nf = HEAD // 2, HEAD // 4
    inv = (10000.0 ** (-(2.0 / half) * np.arange(nf, dtype=np.float32))).astype(np.float32)
    tok = np.arange(LAT)
    rope = np.zeros((LAT, 2, HEAD))
    for h, pos in enumerate((tok // GRID_W, tok % GRID_W)):
        ang = (pos.astype(np.float32)[:, None] * inv).astype(np.float64)
        rope[:, 0, h * half:(h + 1) * half] = np.concatenate([np.cos(ang)] * 2, -1)
        rope[:, 1, h * half:(h + 1) * half] = np.concatenate([-np.sin(ang), np.sin(ang)], -1)
    t["rope"] = rope.reshape(2, P, 2, HEAD).transpose(1, 0, 2, 3)
    n, c = np.arange(LAT), np.arange(64)
    tok_angle = 2 * np.pi * (np.outer(n, n) % LAT) / LAT
    chan_angle = 2 * np.pi * (np.outer(c, c) % 64) / 64
    t["dft_tokens"] = np.stack([np.cos(tok_angle), np.sin(tok_angle)], 1).reshape(2, P, 2, LAT).transpose(1, 0, 2, 3) / 16
    chan = np.zeros((P, 2, P))
    for g in range(2):
        chan[g * 64:(g + 1) * 64, 0, g * 64:(g + 1) * 64] = np.cos(chan_angle) / 8
        chan[g * 64:(g + 1) * 64, 1, g * 64:(g + 1) * 64] = -np.sin(chan_angle) / 8
    t["dft_channels"] = chan
    k = np.arange(P)
    t["before"], t["every"] = k[:, None] < k[None, :], np.ones((P, P))
    t["first_row"], t["count_to"], t["slots"] = P * np.arange(N_EXPERTS), np.arange(32), k
    t["token_ids"] = np.arange(TOK).reshape(TOK // P, P).T
    col = np.arange(GRID_W)
    start = np.clip(col - NA_KW // 2, 0, GRID_W - NA_KW)
    inside = (col[None, :] >= start[:, None]) & (col[None, :] < start[:, None] + NA_KW)
    t["column_mask"] = np.tile(np.where(inside, 0.0, NEG), (2, 1))
    return {name: np.ascontiguousarray(a, dtype=np.float32) for name, a in t.items()}


def first_block_arrays(v):
    a = {}
    a["x"], a["ctx"] = v["x"][0], v["ctx"][0]
    a["cvec"] = np.stack([v["c"][0], v["c_ctx"]], -1).reshape(KD, P, 2).transpose(1, 0, 2)
    a["w_mod"] = np.concatenate([chunks(v["w_mod"][l]) for l in range(DEPTH)])
    for n in ("b_mod", "ln1_g", "ln1_b", "ln2_g", "ln2_b", "moe_bias"):
        a[n] = v[n]
    a["w_router"] = v["moe_w_router"]
    a["ab_w_in"], a["ab_w_out"] = chunks(v["ab_w_in"][0]), chunks(v["ab_w_out"][0])
    a["na_w_in"], a["na_w_out"] = chunks(v["na_w_in"][0]), chunks(v["na_w_out"][0])
    a["ab_w_fnet"] = v["ab_w_fnet"][0]
    a["qk_gains"] = np.concatenate([np.tile(v["ab_q_norm"][0], 6), np.tile(v["ab_k_norm"][0], 2)])
    a["rpb_turned"] = np.pad(v["na_rpb"][0], ((0, 0), (0, 0), (RPB_PAD, RPB_PAD)))[:, :, ::-1]
    parts = []
    for l in range(DEPTH):
        parts.append(gated_parts(v["moe_w_gate"][l], v["moe_w_up"][l], v["moe_w_down"][l]))
        parts.append(gated_parts(v["sh_w_gate"][l], v["sh_w_up"][l], v["sh_w_down"][l]))
    a["experts"] = np.concatenate(parts)
    return a


def second_tables():
    t = {"averager": np.full((P, P), 1.0 / D)}
    k = np.arange(P)
    t["triangles"] = np.stack([k[:, None] <= k[None, :], k[:, None] > k[None, :]], 1)
    q, key = np.arange(LAT)[:, None], np.arange(LAT)[None, :]
    tables = []
    for window, dilation in ((128, 1), (512, 4), (2048, 16)):
        near = (q >= key) & (q - key <= window) & ((q - key) % dilation == 0)
        tables.append(np.where(near, q - key, -NEG))
    t["distances"] = np.stack(tables, 1).reshape(2, P, DIL_GROUPS, LAT).transpose(1, 0, 2, 3)
    return {name: np.ascontiguousarray(a, dtype=np.float32) for name, a in t.items()}


def columns(v):
    return np.moveaxis(v.reshape(*v.shape[:-1], -1, P), -1, 0)


def second_block_arrays(v):
    a = {}
    a["norm_g"], a["norm_g_cols"] = v["norm_g_2"], columns(v["norm_g_2"])
    parts = []
    for l in range(DEPTH):
        for f in range(2):
            w1 = v["ffn_w1_2"][l, f]
            half = w1.shape[-1] // 2
            parts.append(gated_parts(w1[:, :half], w1[:, half:], v["ffn_w2_2"][l, f]))
    a["ffn"] = np.concatenate(parts)
    w = v["hyb_w_in_2"][0]
    n = w.shape[-1] - SSM_HEADS
    a["hyb_w_in"], a["hyb_w_dt"] = chunks(w[:, :n]), chunks(w[:, n:], SSM_HEADS)
    a["hyb_w_out"] = chunks(v["hyb_w_out_2"][0])
    a["attn_w_qkv"], a["attn_w_o"] = chunks(v["attn_w_qkv_2"][0]), chunks(v["attn_w_o_2"][0])
    a["conv_taps"] = columns(v["conv_dw_w_2"][0]).transpose(0, 2, 1)
    a["conv_b_cols"] = columns(v["conv_dw_b_2"][0])
    a["conv_ln_g_cols"], a["conv_ln_b_cols"] = columns(v["conv_ln_g_2"][0]), columns(v["conv_ln_b_2"][0])
    a["ssm_taps"] = columns(v["ssm_conv_w_2"][0]).transpose(0, 2, 1)
    a["ssm_b_cols"] = columns(v["ssm_conv_b_2"][0])
    a["ssm_norm_g_cols"] = columns(v["ssm_norm_g_2"][0])
    a["ssm_dt_bias"], a["ssm_a_log"], a["ssm_d"] = v["ssm_dt_bias_2"][0], v["ssm_a_log_2"][0], v["ssm_d_2"][0]
    return a


def kernel(**inputs):
    import concourse.bacc as bacc
    from concourse.bass_utils import run_bass_kernel_spmd

    values = {name: np.asarray(a) for name, a in inputs.items()}
    arrays = {**shape_tables(), **second_tables(), **first_block_arrays(values), **second_block_arrays(values)}
    nc = bacc.Bacc("TRN2", target_bir_lowering=False, num_devices=1)
    aps = {}
    feeds = {}
    for name, a in arrays.items():
        feeds[f"in_{name}"] = np.ascontiguousarray(a)
        aps[name] = nc.dram_tensor(f"in_{name}", a.shape, mybir.dt.from_np(a.dtype), kind="ExternalInput").ap()
    out = nc.dram_tensor("out_rows", [LAT, D], F32, kind="ExternalOutput").ap()
    program(nc, aps, out)
    result = run_bass_kernel_spmd(nc, [feeds], core_ids=[0])
    return result.results[0]["out_rows"].reshape(1, LAT, D)
```
